# Optimizing a Trainium2 kernel written in Bass

```python
import jax, jax.numpy as jnp
from jax import lax
import numpy as np
import math

D_MODEL = 1024
BATCH = 1
SEQ = 512
DEPTH = 1

HEAD_DIM = 64
A_HEADS = D_MODEL // 128
B_HEADS = D_MODEL // 256
C_HEADS = D_MODEL // 256
A_DIM = A_HEADS * HEAD_DIM
B_DIM = B_HEADS * HEAD_DIM
C_DIM = C_HEADS * HEAD_DIM
D_MIX = A_DIM + B_DIM + C_DIM
IN_SPLITS = (A_DIM, A_DIM, A_DIM, A_HEADS, 2 * B_DIM, B_DIM, B_HEADS, B_HEADS, B_DIM, C_DIM, C_DIM, C_DIM, C_DIM)
IN_WIDTH = 3 * A_DIM + A_HEADS + 4 * B_DIM + 2 * B_HEADS + 4 * C_DIM
Q_BLOCK = 128
MLSTM_CHUNK = 64
HGRN_CHUNK = 16
MLSTM_CONV = 4
FFN_CONV = 3
D_FF = ((8 * D_MODEL // 3 + 255) // 256) * 256
EPS = 1e-6


def _rms(x, g):
    xf = x.astype(jnp.float32)
    y = xf * lax.rsqrt(jnp.mean(xf * xf, axis=-1, keepdims=True) + EPS)
    return (y * g.astype(jnp.float32)).astype(x.dtype)

def _heads(z, h):
    b, t, _ = z.shape
    return z.reshape(b, t, h, -1).transpose(0, 2, 1, 3).astype(jnp.float32)

def _merge(o):
    return o.transpose(0, 2, 1, 3)

def _split_cols(z):
    idx = np.cumsum(IN_SPLITS)[:-1].tolist()
    return jnp.split(z, idx, axis=-1)

def _causal_dwconv(x, w):
    k, c = w.shape
    return lax.conv_general_dilated(x, w[:, None, :], window_strides=(1,), padding=[(k - 1, 0)],
                                    dimension_numbers=('NWC', 'WIO', 'NWC'), feature_group_count=c)

def _fox_attention(q, k, v, c):
    bsz, h, t, d = q.shape
    nb = t // Q_BLOCK
    qb = q.reshape(bsz, h, nb, Q_BLOCK, d).transpose(2, 0, 1, 3, 4)
    cb = c.reshape(bsz, h, nb, Q_BLOCK).transpose(2, 0, 1, 3)
    kpos = jnp.arange(t)
    scale = d ** -0.5

    def one_block(args):
        qi, ci, bi = args
        s = jnp.einsum('bhqd,bhkd->bhqk', qi, k) * scale
        s = s + ci[..., None] - c[:, :, None, :]
        qpos = bi * Q_BLOCK + jnp.arange(Q_BLOCK)
        s = jnp.where(kpos[None, :] <= qpos[:, None], s, -jnp.inf)
        p = jax.nn.softmax(s, axis=-1)
        return jnp.einsum('bhqk,bhkd->bhqd', p, v)

    ob = lax.map(one_block, (qb, cb, jnp.arange(nb)))
    return ob.transpose(1, 2, 0, 3, 4).reshape(bsz, h, t, d)

def _mlstm_chunkwise(q, k, v, i_pre, f_pre):
    bsz, h, t, d = q.shape
    L = MLSTM_CHUNK
    nc = t // L
    k = k * d ** -0.5
    qc = q.reshape(bsz, h, nc, L, d)
    kc = k.reshape(bsz, h, nc, L, d)
    vc = v.reshape(bsz, h, nc, L, d)
    ic = i_pre.reshape(bsz, h, nc, L)
    bc = jnp.cumsum(jax.nn.log_sigmoid(f_pre).reshape(bsz, h, nc, L), axis=-1)
    gc = bc[..., -1]
    ac = gc[..., None] - bc + ic

    def step(carry, inp):
        cs, ns, m = carry
        kj, vj, aj, gj = inp
        m_new = jnp.maximum(gj + m, jnp.max(aj, axis=-1))
        decay = jnp.exp(gj + m - m_new)
        w = jnp.exp(aj - m_new[..., None])
        cs_new = decay[..., None, None] * cs + jnp.einsum('bhl,bhld,bhle->bhde', w, kj, vj)
        ns_new = decay[..., None] * ns + jnp.einsum('bhl,bhld->bhd', w, kj)
        return (cs_new, ns_new, m_new), (cs, ns, m)

    mv = lambda a: jnp.moveaxis(a, 2, 0)
    init = (jnp.zeros((bsz, h, d, d), jnp.float32), jnp.zeros((bsz, h, d), jnp.float32),
            jnp.full((bsz, h), -jnp.inf, jnp.float32))
    _, (c_prev, n_prev, m_prev) = lax.scan(step, init, (mv(kc), mv(vc), mv(ac), gc.transpose(2, 0, 1)))
    c_prev = jnp.moveaxis(c_prev, 0, 2)
    n_prev = jnp.moveaxis(n_prev, 0, 2)
    m_prev = jnp.moveaxis(m_prev, 0, 2)

    tri = jnp.tril(jnp.ones((L, L), bool))
    log_d = jnp.where(tri, bc[..., :, None] - bc[..., None, :] + ic[..., None, :], -jnp.inf)
    m_inter = bc + m_prev[..., None]
    m_out = jnp.maximum(m_inter, jnp.max(log_d, axis=-1))
    sqk = jnp.einsum('bhcld,bhcsd->bhcls', qc, kc) * jnp.exp(log_d - m_out[..., None])
    inter_w = jnp.exp(m_inter - m_out)
    num = jnp.einsum('bhcls,bhcse->bhcle', sqk, vc) + inter_w[..., None] * jnp.einsum('bhcld,bhcde->bhcle', qc, c_prev)
    den = jnp.sum(sqk, axis=-1) + inter_w * jnp.einsum('bhcld,bhcd->bhcl', qc, n_prev)
    out = num / jnp.maximum(jnp.abs(den), jnp.exp(-m_out))[..., None]
    return out.reshape(bsz, h, t, d)

def _hgrn2_chunkwise(q, logf, i):
    bsz, h, t, dk = q.shape
    dv = i.shape[-1]
    L = HGRN_CHUNK
    nc = t // L
    k = -jnp.expm1(logf)
    qc = q.reshape(bsz, h, nc, L, dk)
    kc = k.reshape(bsz, h, nc, L, dk)
    vc = i.reshape(bsz, h, nc, L, dv)
    bc = jnp.cumsum(logf.reshape(bsz, h, nc, L, dk), axis=3)
    blast = bc[:, :, :, -1]
    tri = jnp.tril(jnp.ones((L, L), bool))
    rel = jnp.where(tri[:, :, None], bc[:, :, :, :, None, :] - bc[:, :, :, None, :, :], -jnp.inf)
    att = jnp.einsum('bhctd,bhcsd,bhctsd->bhcts', qc, kc, jnp.exp(rel))
    intra = jnp.einsum('bhcts,bhcse->bhcte', att, vc)

    def step(s, inp):
        kj, vj, bj, blj = inp
        kd = kj * jnp.exp(blj[:, :, None, :] - bj)
        return jnp.exp(blj)[..., None] * s + jnp.einsum('bhld,bhle->bhde', kd, vj), s

    mv = lambda a: jnp.moveaxis(a, 2, 0)
    _, s_prev = lax.scan(step, jnp.zeros((bsz, h, dk, dv), jnp.float32), (mv(kc), mv(vc), mv(bc), mv(blast)))
    s_prev = jnp.moveaxis(s_prev, 0, 2)
    inter = jnp.einsum('bhctd,bhcde->bhcte', qc * jnp.exp(bc), s_prev)
    return (intra + inter).reshape(bsz, h, t, dv)

def _mixer(h, lb, w_in, b_in, a_q_g, a_k_g, b_conv_w, out_g, w_out):
    bsz, t, _ = h.shape
    f32 = jnp.float32
    z = h @ w_in + b_in
    (a_q, a_k, a_v, a_f, b_qk, b_v, b_i, b_f, b_o, c_q, c_f, c_i, c_g) = _split_cols(z)
    qa = _rms(_heads(a_q, A_HEADS), a_q_g)
    ka = _rms(_heads(a_k, A_HEADS), a_k_g)
    ca = jnp.cumsum(jax.nn.log_sigmoid(a_f.astype(f32)), axis=1).transpose(0, 2, 1)
    oa = _fox_attention(qa, ka, _heads(a_v, A_HEADS), ca)
    qk = jax.nn.silu(_causal_dwconv(b_qk, b_conv_w))
    qb, kb = jnp.split(qk, 2, axis=-1)
    ob = _mlstm_chunkwise(_heads(qb, B_HEADS), _heads(kb, B_HEADS), _heads(b_v, B_HEADS),
                          b_i.astype(f32).transpose(0, 2, 1), b_f.astype(f32).transpose(0, 2, 1))
    lbh = lb.reshape(C_HEADS, 1, HEAD_DIM)
    logf = jnp.logaddexp(jnp.log(lbh), jnp.log1p(-lbh) + jax.nn.log_sigmoid(_heads(c_f, C_HEADS)))
    oc = _hgrn2_chunkwise(jax.nn.silu(_heads(c_q, C_HEADS)), logf, _heads(c_i, C_HEADS))
    g_a, g_b, g_c = jnp.split(out_g.astype(f32), [A_DIM, A_DIM + B_DIM])
    ya = _rms(_merge(oa), g_a.reshape(A_HEADS, HEAD_DIM)).reshape(bsz, t, A_DIM)
    yb = jax.nn.sigmoid(b_o.astype(f32)) * _rms(_merge(ob), g_b.reshape(B_HEADS, HEAD_DIM)).reshape(bsz, t, B_DIM)
    yc = jax.nn.silu(c_g.astype(f32)) * _rms(_merge(oc), g_c.reshape(C_HEADS, HEAD_DIM)).reshape(bsz, t, C_DIM)
    y = jnp.concatenate([ya, yb, yc], axis=-1).astype(h.dtype)
    return y @ w_out

def _conv_glu(h, w_up, conv_w, conv_b, w_down):
    u = _causal_dwconv(h @ w_up, conv_w) + conv_b
    gate, up = jnp.split(u, 2, axis=-1)
    return (jax.nn.silu(gate) * up) @ w_down

def first_inputs(seed: int = 0) -> dict:
    key = jax.random.key(seed)
    ks = jax.random.split(key, 16)
    f32 = jnp.float32
    nrm = lambda k, shape, s: jax.random.normal(k, shape, f32) * s
    gate_offsets = jnp.concatenate([
        jnp.zeros((3 * A_DIM,), f32), jnp.linspace(1.0, 4.0, A_HEADS, dtype=f32),
        jnp.zeros((3 * B_DIM + B_HEADS,), f32), jnp.linspace(3.0, 6.0, B_HEADS, dtype=f32),
        jnp.zeros((B_DIM + 4 * C_DIM,), f32)])
    return {
        "x": nrm(ks[0], (BATCH, SEQ, D_MODEL), 1.0),
        "lb_logits": nrm(ks[1], (DEPTH, C_DIM), 0.5),
        "norm_mix_g": 1.0 + nrm(ks[2], (DEPTH, D_MODEL), 0.02),
        "w_in": nrm(ks[3], (DEPTH, D_MODEL, IN_WIDTH), D_MODEL ** -0.5),
        "b_in": nrm(ks[4], (DEPTH, IN_WIDTH), 0.02) + gate_offsets,
        "a_q_g": 1.0 + nrm(ks[5], (DEPTH, HEAD_DIM), 0.02),
        "a_k_g": 1.0 + nrm(ks[6], (DEPTH, HEAD_DIM), 0.02),
        "b_conv_w": nrm(ks[7], (DEPTH, MLSTM_CONV, 2 * B_DIM), MLSTM_CONV ** -0.5),
        "out_g": 1.0 + nrm(ks[8], (DEPTH, D_MIX), 0.02),
        "w_out": nrm(ks[9], (DEPTH, D_MIX, D_MODEL), D_MIX ** -0.5),
        "norm_ffn_g": 1.0 + nrm(ks[10], (DEPTH, D_MODEL), 0.02),
        "w_up": nrm(ks[11], (DEPTH, D_MODEL, 2 * D_FF), D_MODEL ** -0.5),
        "ffn_conv_w": nrm(ks[12], (DEPTH, FFN_CONV, 2 * D_FF), FFN_CONV ** -0.5),
        "ffn_conv_b": nrm(ks[13], (DEPTH, 2 * D_FF), 0.02),
        "w_down": nrm(ks[14], (DEPTH, D_FF, D_MODEL), D_FF ** -0.5),
    }

def first_block(x, lb_logits, norm_mix_g, w_in, b_in, a_q_g, a_k_g, b_conv_w, out_g, w_out,
              norm_ffn_g, w_up, ffn_conv_w, ffn_conv_b, w_down):
    p = jax.nn.softmax(lb_logits.astype(jnp.float32), axis=0)
    lb_all = jnp.maximum(jnp.cumsum(p, axis=0) - p[0], 0.0)
    for l in range(DEPTH):
        h = _rms(x, norm_mix_g[l])
        x = x + _mixer(h, lb_all[l], w_in[l], b_in[l], a_q_g[l], a_k_g[l], b_conv_w[l], out_g[l], w_out[l])
        h = _rms(x, norm_ffn_g[l])
        x = x + _conv_glu(h, w_up[l], ffn_conv_w[l], ffn_conv_b[l], w_down[l])
    return x


ROPE_THETA = 10000.0
NORM_EPS = 1e-6

DIFF_HEADS = 4
DIFF_HEAD_DIM = 64
DIFF_V_DIM = 2 * DIFF_HEAD_DIM
DIFF_WIDTH = DIFF_HEADS * DIFF_V_DIM
DIFF_QK_COLS = DIFF_HEADS * 2 * DIFF_HEAD_DIM

MLA_HEADS = 4
MLA_NOPE = 128
MLA_ROPE = 64
MLA_V = 128
MLA_Q_RANK = 384
MLA_KV_RANK = 256
MLA_WIDTH = MLA_HEADS * MLA_V

SPLIT_SIZES = (DIFF_QK_COLS, DIFF_QK_COLS, DIFF_WIDTH, DIFF_WIDTH,
               MLA_Q_RANK, MLA_KV_RANK, MLA_ROPE, MLA_WIDTH,
               D_MODEL, D_MODEL)
IN_COLS = sum(SPLIT_SIZES)


def rms_norm(x, gain):
    xf = x.astype(jnp.float32)
    y = xf * lax.rsqrt(jnp.mean(xf * xf, axis=-1, keepdims=True) + NORM_EPS)
    return (y * gain.astype(jnp.float32)).astype(x.dtype)

def rope_tables(positions, dim):
    inv_freq = ROPE_THETA ** (-jnp.arange(0, dim, 2, dtype=jnp.float32) / dim)
    ang = positions.astype(jnp.float32)[..., None] * inv_freq
    return jnp.cos(ang), jnp.sin(ang)

def apply_rope(x, cos, sin):
    b, s, half = cos.shape
    shape = (b,) + (1,) * (x.ndim - 3) + (s, half)
    c = cos.reshape(shape).astype(x.dtype)
    sn = sin.reshape(shape).astype(x.dtype)
    x1, x2 = x[..., :half], x[..., half:]
    return jnp.concatenate([x1 * c - x2 * sn, x2 * c + x1 * sn], axis=-1)

def causal_multimap_attention(q, k, v, map_weights, scale):
    b, h, m, s, dk = q.shape
    dv = v.shape[-1]
    nb = s // Q_BLOCK
    qb = jnp.moveaxis(q.reshape(b, h, m, nb, Q_BLOCK, dk), 3, 0)
    kpos = jnp.arange(s)
    w = map_weights.astype(jnp.float32)

    def one_block(args):
        q_blk, i = args
        qpos = i * Q_BLOCK + jnp.arange(Q_BLOCK)
        sc = jnp.einsum('bhmqd,bhmkd->bhmqk', q_blk, k).astype(jnp.float32) * scale
        sc = jnp.where(kpos[None, :] <= qpos[:, None], sc, -jnp.inf)
        p = jax.nn.softmax(sc, axis=-1)
        p = jnp.einsum('m,bhmqk->bhqk', w, p)
        return jnp.einsum('bhqk,bhkd->bhqd', p.astype(v.dtype), v)

    out = lax.map(one_block, (qb, jnp.arange(nb)))
    return jnp.moveaxis(out, 0, 2).reshape(b, h, s, dv)

def second_inputs(seed: int = 0) -> dict:
    key = jax.random.key(seed)
    ks = jax.random.split(key, 20)
    L = DEPTH
    nrm = lambda k, shape, fan: jax.random.normal(k, shape, jnp.float32) * fan ** -0.5
    gain = lambda k, n: 1.0 + 0.05 * jax.random.normal(k, (L, n), jnp.float32)
    x = jax.random.normal(ks[0], (BATCH, SEQ, D_MODEL), jnp.float32)
    positions = jnp.broadcast_to(jnp.arange(SEQ, dtype=jnp.int32), (BATCH, SEQ))
    return {
        "x": x,
        "positions": positions,
        "norm_in": gain(ks[1], D_MODEL),
        "w_in": nrm(ks[2], (L, D_MODEL, IN_COLS), D_MODEL),
        "diff_lambda_q1": 0.1 * jax.random.normal(ks[3], (L, DIFF_HEAD_DIM), jnp.float32),
        "diff_lambda_k1": 0.1 * jax.random.normal(ks[4], (L, DIFF_HEAD_DIM), jnp.float32),
        "diff_lambda_q2": 0.1 * jax.random.normal(ks[5], (L, DIFF_HEAD_DIM), jnp.float32),
        "diff_lambda_k2": 0.1 * jax.random.normal(ks[6], (L, DIFF_HEAD_DIM), jnp.float32),
        "diff_subln": gain(ks[7], DIFF_V_DIM),
        "mla_q_norm": gain(ks[8], MLA_Q_RANK),
        "w_uq": nrm(ks[9], (L, MLA_Q_RANK, MLA_HEADS * (MLA_NOPE + MLA_ROPE)), MLA_Q_RANK),
        "mla_kv_norm": gain(ks[10], MLA_KV_RANK),
        "w_ukv": nrm(ks[11], (L, MLA_KV_RANK, MLA_HEADS * (MLA_NOPE + MLA_V)), MLA_KV_RANK),
        "w_proj_diff": nrm(ks[12], (L, DIFF_WIDTH, D_MODEL), DIFF_WIDTH),
        "w_proj_mla": nrm(ks[13], (L, MLA_WIDTH, D_MODEL), MLA_WIDTH),
        "w_out": nrm(ks[14], (L, D_MODEL, D_MODEL), D_MODEL),
        "norm_final": 1.0 + 0.05 * jax.random.normal(ks[15], (D_MODEL,), jnp.float32),
    }

def second_block(x, positions, norm_in, w_in, diff_lambda_q1, diff_lambda_k1,
              diff_lambda_q2, diff_lambda_k2, diff_subln, mla_q_norm, w_uq,
              mla_kv_norm, w_ukv, w_proj_diff, w_proj_mla, w_out, norm_final):
    b, s, _ = x.shape
    cos_d, sin_d = rope_tables(positions, DIFF_HEAD_DIM)
    cos_m, sin_m = rope_tables(positions, MLA_ROPE)
    split_idx = list(np.cumsum(SPLIT_SIZES)[:-1])

    for layer in range(DEPTH):
        lambda_init = 0.8 - 0.6 * math.exp(-0.3 * layer)
        h = rms_norm(x, norm_in[layer])
        proj = h @ w_in[layer]
        (dq, dk, dv, dgate, cq, ckv, kr, mgate, g_diff, g_mla) = jnp.split(proj, split_idx, axis=-1)

        dq = dq.reshape(b, s, DIFF_HEADS, 2, DIFF_HEAD_DIM).transpose(0, 2, 3, 1, 4)
        dk = dk.reshape(b, s, DIFF_HEADS, 2, DIFF_HEAD_DIM).transpose(0, 2, 3, 1, 4)
        dv = dv.reshape(b, s, DIFF_HEADS, DIFF_V_DIM).transpose(0, 2, 1, 3)
        dq = apply_rope(dq, cos_d, sin_d)
        dk = apply_rope(dk, cos_d, sin_d)
        lam = (jnp.exp(jnp.sum(diff_lambda_q1[layer] * diff_lambda_k1[layer]))
               - jnp.exp(jnp.sum(diff_lambda_q2[layer] * diff_lambda_k2[layer]))
               + lambda_init)
        weights = jnp.stack([jnp.ones_like(lam), -lam])
        o_diff = causal_multimap_attention(dq, dk, dv, weights, DIFF_HEAD_DIM ** -0.5)
        o_diff = rms_norm(o_diff, diff_subln[layer]) * (1.0 - lambda_init)
        o_diff = o_diff.transpose(0, 2, 1, 3).reshape(b, s, DIFF_WIDTH)
        o_diff = o_diff * jax.nn.silu(dgate)

        cq = rms_norm(cq, mla_q_norm[layer])
        q = (cq @ w_uq[layer]).reshape(b, s, MLA_HEADS, MLA_NOPE + MLA_ROPE).transpose(0, 2, 1, 3)
        q_nope, q_rope = q[..., :MLA_NOPE], apply_rope(q[..., MLA_NOPE:], cos_m, sin_m)
        ckv = rms_norm(ckv, mla_kv_norm[layer])
        kv = (ckv @ w_ukv[layer]).reshape(b, s, MLA_HEADS, MLA_NOPE + MLA_V).transpose(0, 2, 1, 3)
        k_nope, mv = kv[..., :MLA_NOPE], kv[..., MLA_NOPE:]
        k_rope = apply_rope(kr[:, None], cos_m, sin_m)
        mq = jnp.concatenate([q_nope, q_rope], axis=-1)[:, :, None]
        mk = jnp.concatenate([k_nope, jnp.broadcast_to(k_rope, k_nope.shape[:-1] + (MLA_ROPE,))], axis=-1)[:, :, None]
        o_mla = causal_multimap_attention(mq, mk, mv, jnp.ones((1,), jnp.float32),
                                          (MLA_NOPE + MLA_ROPE) ** -0.5)
        o_mla = o_mla.transpose(0, 2, 1, 3).reshape(b, s, MLA_WIDTH)
        o_mla = o_mla * jax.nn.silu(mgate)

        merged = (jax.nn.sigmoid(g_diff) * (o_diff @ w_proj_diff[layer])
                  + jax.nn.sigmoid(g_mla) * (o_mla @ w_proj_mla[layer]))
        x = x + merged @ w_out[layer]

    return rms_norm(x, norm_final)


def setup_inputs(seed=0):
    out = dict(first_inputs(seed))
    for name, value in second_inputs(seed + 1).items():
        if name != "x":
            out[name + "_2"] = value
    return out


def reference(
    x, lb_logits, norm_mix_g, w_in, b_in, a_q_g, a_k_g, b_conv_w, out_g, w_out, norm_ffn_g,
    w_up, ffn_conv_w, ffn_conv_b, w_down, positions_2, norm_in_2, w_in_2, diff_lambda_q1_2,
    diff_lambda_k1_2, diff_lambda_q2_2, diff_lambda_k2_2, diff_subln_2, mla_q_norm_2, w_uq_2,
    mla_kv_norm_2, w_ukv_2, w_proj_diff_2, w_proj_mla_2, w_out_2, norm_final_2,
):
    x = first_block(
        x, lb_logits, norm_mix_g, w_in, b_in, a_q_g, a_k_g, b_conv_w, out_g, w_out, norm_ffn_g,
        w_up, ffn_conv_w, ffn_conv_b, w_down,
    )
    return second_block(
        x, positions_2, norm_in_2, w_in_2, diff_lambda_q1_2, diff_lambda_k1_2, diff_lambda_q2_2,
        diff_lambda_k2_2, diff_subln_2, mla_q_norm_2, w_uq_2, mla_kv_norm_2, w_ukv_2,
        w_proj_diff_2, w_proj_mla_2, w_out_2, norm_final_2,
    )


_drawn_inputs = setup_inputs


def setup_inputs(seed=0):
    import zlib

    import numpy as np

    out = dict(_drawn_inputs(seed))
    spreads = {}
    factors = {'a_q_g': 5.184,
     'a_k_g': 5.099,
     'out_g': 4.174,
     'norm_ffn_g': 4.647,
     'ffn_conv_b': 4.396,
     'norm_in_2': 3.403,
     'diff_lambda_q1_2': 43.584,
     'diff_lambda_q2_2': 8.0,
     'diff_lambda_k2_2': 8.0,
     'diff_subln_2': 22.538,
     'mla_q_norm_2': 8.0,
     'mla_kv_norm_2': 8.0,
     'diff_lambda_k1_2': 8.0}
    for name, (base, spread) in spreads.items():
        noise = np.random.default_rng([zlib.crc32(name.encode()), seed]).standard_normal(out[name].shape)
        drawn = base * np.exp(spread * noise) if base else spread * noise
        out[name] = __import__('jax').numpy.asarray(drawn.astype(out[name].dtype))
    for name, factor in factors.items():
        out[name] = (out[name] * factor).astype(out[name].dtype)
    return out
```

```python
from contextlib import ExitStack

import numpy as np

import concourse.bass as bass
from concourse import mybir

F32 = mybir.dt.float32
F32R = mybir.dt.float32r
BF16 = mybir.dt.bfloat16
I32 = mybir.dt.int32
ACT = mybir.ActivationFunctionType
ALU = mybir.AluOpType
AX = mybir.AxisListType

P = 128
T = 512
NB = T // P
D = 1024
KD = D // P
HD = 64
AH, BH, CH = 8, 4, 4
LC = 16
NC = T // LC
DFF = 2816
FT = DFF // P
FHALF = (12, FT - 12)
HSLOT = 14
EPS = 1e-6
NEG = -1e30
LAMBDA_INIT = 0.2
MLA_SCALE = 192.0 ** -0.5
SLOT = 2048
KIB = 1024

OFF_AQ, OFF_AK, OFF_AV, OFF_AF, OFF_BQK, OFF_BV, OFF_BI, OFF_BF, OFF_BO, OFF_CQ, OFF_CF, OFF_CI, OFF_CG, _ = (
    int(v) for v in np.cumsum([0, 512, 512, 512, 8, 512, 256, 4, 4, 256, 256, 256, 256, 256]))
OFF_DQ, OFF_DK, OFF_DV, OFF_DG, OFF_CQ2, OFF_CKV, OFF_KR, OFF_MG, OFF_GD, OFF_GM, _ = (
    int(v) for v in np.cumsum([0, 512, 512, 512, 512, 384, 256, 64, 512, 1024, 1024]))

PCOL = {}
for _name, _n in [("g_mix", 8), ("g_ffn", 8), ("g_in2", 8), ("g_out", 8), ("b_aq", 4), ("b_ak", 4), ("b_bqk", 4),
                  ("b_bo", 2), ("b_cq", 2), ("b_cf", 2), ("b_cg", 2), ("g_cq2", 3), ("g_ckv", 2), ("lb", 2),
                  ("w_bconv", 16), ("g_sub", 1), ("g_aq", 1), ("g_ak", 1), ("b_gate", 1), ("w_fconv", 132),
                  ("b_fconv", 44)]:
    PCOL[_name] = (sum(n for _, n in PCOL.values()), _n)
NPC = sum(n for _, n in PCOL.values())

CCOL = {}
for _name, _n in [("ident", 128), ("ones", 128), ("blk", 128), ("neg", 128), ("tri", 128), ("chunk", 128),
                  ("rep", 128), ("win", 96), ("inchunk", 8), ("eps", 1), ("freq", 1), ("sign", 1), ("halfpi", 1)]:
    CCOL[_name] = (sum(n for _, n in CCOL.values()), _n)
NCC = sum(n for _, n in CCOL.values())


def constant_table():
    t = np.zeros((P, NCC), np.float32)
    r, c = np.arange(P)[:, None], np.arange(P)[None, :]

    def put(name, value):
        at, n = CCOL[name]
        t[:value.shape[0], at:at + n] = value

    put("ident", np.float32(r == c))
    put("ones", np.ones((P, P), np.float32))
    put("blk", np.float32(r // HD == c // HD))
    put("neg", np.where(c > r, np.float32(NEG), np.float32(0)))
    put("tri", np.float32(r <= c))
    put("chunk", np.float32((r // LC == c // LC) & (r <= c)))
    put("rep", np.float32(np.arange(64)[:, None] % 32 == c % LC))
    put("win", np.float32(np.arange(96)[None, :] == LC - 1 + 32 * (r // HD)))
    put("inchunk", np.float32(r // LC == np.arange(8)[None, :]))
    put("eps", np.full((P, 1), EPS, np.float32))
    half = np.arange(0, 64, 2, dtype=np.float32)
    freq = np.float32(10000.0) ** (-half / np.float32(64))
    put("freq", np.tile(freq, 4)[:, None].astype(np.float32))
    put("sign", np.where(r % 64 < 32, np.float32(-1), np.float32(1)))
    put("halfpi", np.full((P, 1), np.pi / 2, np.float32))
    return t


def two_blocks(nc, x_d, w_in_d, b_in_d, w_gate_d, w_out_d, w_up_d, w_down_d, pos_d, w_in2_d, lam_d, w_uq_d, w_ukv_d,
               w_pd_d, w_pm_d, w_out2_d, g_fin_d, par_d, con_d, out_d):
    ctx = ExitStack()
    with ctx:
        base = 1152

        def sb(name, shape, dt, kib):
            return nc.alloc_sbuf_tensor_at(name, shape, dt, offset=base + int(round(kib * KIB)))

        def sem(name):
            return ctx.enter_context(nc.semaphore(name))

        x_in, const_in, wg_in, bias_in, lam_in, pos_in, xres_in, gfin_in = (
            sem(n) for n in ("x_in", "const_in", "wg_in", "bias_in", "lam_in", "pos_in", "xres_in", "gfin_in"))
        hi_done, split_done = (sem(n) for n in ("hi_done", "split_done"))
        act_step, dve_step = (sem(n) for n in ("act_step", "dve_step"))
        x_ss, x_var, x_rs, x_h, h_hi = (sem(n) for n in ("x_ss", "x_var", "x_rs", "x_h", "h_hi"))
        lb_d, lb_e, nbcf_ready, mask_ready = (sem(n) for n in ("lb_d", "lb_e", "nbcf_ready", "mask_ready"))
        gate_ln, gate_m, gate_rows, gate_cols, gate_cols_out, negC_ready = (
            sem(n) for n in ("gate_ln", "gate_m", "gate_rows", "gate_cols", "gate_cols_out", "negC_ready"))
        hg_a, hg_a_used, hg_q, hg_att_s, hg_kdT_mm, hg_kdT_s = (
            sem(n) for n in ("hg_a", "hg_a_used", "hg_q", "hg_att_s", "hg_kdT_mm", "hg_kdT_s"))
        hg_vx, hg_u_mm, hg_u_s, hg_scan, hg_rep_mm, hg_dm, hg_o_mm, hg_n, hg_done = (
            sem(n) for n in ("hg_vx", "hg_u_mm", "hg_u_s", "hg_scan", "hg_rep_mm", "hg_dm", "hg_o_mm", "hg_n", "hg_done"))
        nrm_sq, nrm_mm, nrm_rs, nrm_done, qk_done = (sem(n) for n in ("nrm_sq", "nrm_mm", "nrm_rs", "nrm_done", "qk_done"))
        conv_b, qkB_ready, ml_m_mm, ml_w, ml_e, ml_s_mm, ml_p, ml_o_mm, ml_o_s = (
            sem(n) for n in ("conv_b", "qkB_ready", "ml_m_mm", "ml_w", "ml_e", "ml_s_mm", "ml_p", "ml_o_mm", "ml_o_s"))
        yb_var, yb_rs, yb_n = (sem(n) for n in ("yb_var", "yb_rs", "yb_n"))
        fox_s_mm, fox_m, fox_e, fox_t_mm, fox_pt, fox_v_mm, fox_o_free = (
            sem(n) for n in ("fox_s_mm", "fox_m", "fox_e", "fox_t_mm", "fox_pt", "fox_v_mm", "fox_o_free"))
        ya_var, ya_rs, ya_n, ya_hi, ys_hi, y_lo = (sem(n) for n in ("ya_var", "ya_rs", "ya_n", "ya_hi", "ys_hi", "y_lo"))
        n_sq, n_mm, n_rs, normed, n_hi, n_lo = (sem(n) for n in ("n_sq", "n_mm", "n_rs", "normed", "n_hi", "n_lo"))
        zp_zero, conv_g, conv_u, silu_ready, hidden, hid_hi, hid_lo = (
            sem(n) for n in ("zp_zero", "conv_g", "conv_u", "silu_ready", "hidden", "hid_hi", "hid_lo"))
        rot_ready, sin_ready, cos_ready, lam_s, lam_e, lam_done, rope_z, rope_done = (
            sem(n) for n in ("rot_ready", "sin_ready", "cos_ready", "lam_s", "lam_e", "lam_done", "rope_z", "rope_done"))
        dif_s_mm, dif_m, dif_e, dif_c, dif_t_mm, dif_pt, dif_v_mm, dif_o_free = (
            sem(n) for n in ("dif_s_mm", "dif_m", "dif_e", "dif_c", "dif_t_mm", "dif_pt", "dif_v_mm", "dif_o_free"))
        yd_var, yd_rs, yd_n = (sem(n) for n in ("yd_var", "yd_rs", "yd_n"))
        lat_sq, lat_mm, lat_rs, lat_t, lat_hi, lat_lo = (sem(n) for n in ("lat_sq", "lat_mm", "lat_rs", "lat_t", "lat_hi", "lat_lo"))
        mla_s_mm, mla_m, mla_e, mla_t_mm, mla_pt, mla_v_mm, mla_o_free, ym_n = (
            sem(n) for n in ("mla_s_mm", "mla_m", "mla_e", "mla_t_mm", "mla_pt", "mla_v_mm", "mla_o_free", "ym_n"))
        o_hi, o_lo = (sem(n) for n in ("o_hi", "o_lo"))
        gated_d, gated_m, merged, m_hi, m_lo = (sem(n) for n in ("gated_d", "gated_m", "merged", "m_hi", "m_lo"))
        ssf_ready, f_var, f_rs, out_ready, out_done = (sem(n) for n in ("ssf_ready", "f_var", "f_rs", "out_ready", "out_done"))
        raw_in = [sem(f"raw_in{i}") for i in range(2)]
        tile_done = sem("tile_done")
        ring_free = [sem(f"ring_free{i}") for i in range(2)]

        raw = [sb(f"w_raw{i}", [P, SLOT], F32, 8 * i) for i in range(2)]
        whi = [sb(f"w_hi{i}", [P, SLOT], F32R, 16 + 8 * i) for i in range(3)]
        wlo = [sb(f"w_lo{i}", [P, SLOT], F32R, 40 + 8 * i) for i in range(3)]
        hH = sb("act_hi", [P, KD, T], F32R, 64)
        hL = sb("act_lo", [P, KD, T], F32R, 80)
        con = sb("con", [P, NCC], F32, 96)
        par = sb("par", [P, NPC], F32, 100)
        small = sb("small", [P, 320], F32, 101.25)
        identb = sb("identb", [P, P], BF16, 102.5)
        maskb = sb("maskb", [P, P], BF16, 102.75)
        M = 104
        xtok = sb("xtok", [P, NB, D], F32, M + 28)
        htok = sb("htok", [P, NB, D], F32, M + 44)
        U = sb("U", [P, HD, NC], F32, M)
        Gx = sb("Gx", [P, HD // 2, NC], F32, M + 8)
        Ab = [sb(f"Ab{i}", [P, 2, T], F32, M + 12 + 4 * i) for i in range(2)]
        Vx = [sb(f"Vx{i}", [P, 8, HD], F32, M + 12 + 2 * i) for i in range(4)]
        kd = sb("kd", [P, 2, NC, LC], F32, M + 20)
        kdT = sb("kdT", [P, 2, NB, P], F32, M + 24)
        qT = sb("qT", [P, 4, T], F32, M + 28)
        kT = sb("kT", [P, 4, T], F32, M + 36)
        av = sb("av", [P, NB, T], F32, M + 44)
        bqk = sb("bqk", [P, 4, T + 3], F32, M + 52)
        qkB = sb("qkB", [P, 4, T], F32, M + 60.25)
        bv = sb("bv", [P, NB, BH, HD + 1], F32, M + 68.25)
        bo = sb("bo", [P, 2, T], F32, M + 72.5)
        cq = sb("cq", [P, 2, NC, LC + 1], F32, M + 76.5)
        cf = sb("cf", [P, 2, NC, LC], F32, M + 80.75)
        ck = sb("ck", [P, 2, NC, LC], F32, M + 84.75)
        ci = sb("ci", [P, NB, 256], F32, M + 88.75)
        cg = sb("cg", [P, 2, T], F32, M + 92.75)
        bias_t = sb("bias_t", [P, 1024], F32, M + 96.75)
        gz = sb("gz", [96, T], F32, M + 100.75)
        g1 = sb("g1", [96, T], F32, M + 102.75)
        g2 = sb("g2", [96, T], F32, M + 104.75)
        g3 = sb("g3", [96, T], F32, M + 106.75)
        negC = sb("negC", [P, T], F32, M + 108.75)
        wg = sb("wg", [P, KD, 96], F32, M + 110.75)
        scr = [sb(f"scr{i}", [P, T], F32, M + 113.75 + 2 * i) for i in range(2)]
        Dm = [sb(f"Dm{i}", [P, NB, P], F32, M + 80.75 + 2 * i) for i in range(2)]
        attS = sb("attS", [64, 2, T], F32, M + 84.75)
        PM = [sb(f"PM{i}", [P, 1280], F32, M + 5 * i) for i in range(2)]
        Oh = sb("Oh", [P, NB, HD + 1], F32, M + 12)
        onB = sb("onB", [P, NB, BH, HD], F32, M + 14)
        sqB = sb("sqB", [P, NB, BH, HD], F32, M + 18)
        Pf = [sb(f"Pf{i}", [P, T], F32, M + 2 * i) for i in range(2)]
        PTs = [sb(f"PTs{i}", [P, T], F32, M + 4 + 2 * i) for i in range(2)]
        on = sb("on", [P, AH, HD], F32, M + 8)
        sqA = sb("sqA", [P, AH, HD], F32, M + 10)
        yt = sb("yt", [P, 4, P], F32, M + 12)
        xT = sb("xT", [P, KD, T], F32, M)
        xres = sb("xres", [P, NB, D], F32, M + 76.5)
        sqn = [sb(f"sqn{i}", [P, T], F32, M + 16 + 2 * i) for i in range(2)]
        rsn = sb("rsn", [P, T], F32, M + 20)
        hb = [sb(f"hb{i}", [P, T], F32, M + 22 + 2 * i) for i in range(2)]
        hidH = sb("hidH", [P, HSLOT, T], F32R, M + 26)
        hidL = sb("hidL", [P, HSLOT, T], F32R, M + 54)
        zp = [sb(f"zp{i}", [P, T + 2], F32, M + 82 + 2.25 * i) for i in range(4)]
        cvg = [sb(f"cvg{i}", [P, T], F32, M + 91 + 2 * i) for i in range(2)]
        cvu = [sb(f"cvu{i}", [P, T], F32, M + 95 + 2 * i) for i in range(2)]
        hid = [sb(f"hid{i}", [P, T], F32, M + 99 + 2 * i) for i in range(2)]
        cosT = sb("cosT", [P, T], F32, M + 104)
        sinT = sb("sinT", [P, T], F32, M + 106)
        posI = sb("posI", [P, T], I32, M + 108)
        angT = sb("angT", [P, T], F32, M + 110)
        rotT = sb("rotT", [P, T], F32, M + 112)
        dq = sb("dq", [P, 4, T], F32, M + 26)
        dk = sb("dk", [P, 4, T], F32, M + 34)
        dv = sb("dv", [P, NB, T], F32, M + 42)
        sdg = sb("sdg", [P, 4, T], F32, M + 50)
        oH = sb("oH", [P, KD, T], F32R, M + 58)
        oL = sb("oL", [P, KD, T], F32R, M + 74)
        smg = sb("smg", [P, 4, T], F32, M + 90)
        zs = [sb(f"zs{i}", [P, T], F32, M + 98 + 2 * i) for i in range(2)]
        P2 = [sb(f"P2{i}", [P, T], F32, M + 108 + 2 * i) for i in range(4)]
        PT2 = [sb(f"PT2{i}", [P, T], F32, M + 98 + 2 * i) for i in range(2)]
        on2 = sb("on2", [P, 4, P], F32, M + 16)
        sq2 = sb("sq2", [P, 4, P], F32, M + 18)
        yt2 = sb("yt2", [P, 4, P], F32, M + 20)
        qn = sb("qn", [P, 4, T], F32, M + 26)
        kn = sb("kn", [P, 4, T], F32, M + 34)
        mv = sb("mv", [P, NB, T], F32, M + 42)
        qr = sb("qr", [P, 2, T], F32, M + 50)
        kr = sb("kr", [P, T], F32, M + 54)
        lat = sb("lat", [P, 5, T], F32, M + 108)
        latHq = [sb(f"latHq{i}", [P, T], F32R, M + (66, 68, 70, 72, 56)[i]) for i in range(5)]
        latLq = [sb(f"latLq{i}", [P, T], F32R, M + (82, 84, 86, 88, 102)[i]) for i in range(5)]
        mH = sb("mH", [P, KD, T], F32R, M + 26)
        mL = sb("mL", [P, KD, T], F32R, M + 42)
        sgd = [sb(f"sgd{i}", [P, T], F32, M + 90 + 2 * i) for i in range(2)]
        sgm = [sb(f"sgm{i}", [P, T], F32, M + 94 + 2 * i) for i in range(2)]
        mt = [sb(f"mt{i}", [P, T], F32, M + 98 + 2 * i) for i in range(2)]
        mt2 = [sb(f"mt2{i}", [P, T], F32, M + 102 + 2 * i) for i in range(2)]
        xo = sb("xo", [P, NB, D], F32, M + 58)
        gfin = sb("gfin", [P, D], F32, M + 74)
        lamv = sb("lamv", [P, 4, HD], F32, M + 117.75)
        assert M + 118.75 <= (nc.sbuf_usable_end - base) / KIB

        ring = [ctx.enter_context(nc.psum_tensor(f"ring{i}", [P, T], F32)) for i in range(2)]
        bank = [ctx.enter_context(nc.psum_tensor(f"bank{i}", [P, T], F32)) for i in range(6)]

        def cc(name, r=slice(0, P)):
            at, n = CCOL[name]
            return con[r, at:at + n]

        def pc(name, i=0, n=1, r=slice(0, P)):
            return par[r, PCOL[name][0] + i:PCOL[name][0] + i + n]

        ident = cc("ident")
        sm_at = [0]

        def sm(n):
            at = sm_at[0]
            sm_at[0] += n
            assert sm_at[0] <= 320
            return small[:, at:at + n]

        ss_x, var_x, rs_x = sm(4), sm(4), sm(4)
        lbd, lbe, lbr, lbp, lb, lb1 = (sm(2) for _ in range(6))
        nbcf = sm(2)
        gq8 = sm(1)
        colB = sm(32)
        denB, recB = sm(4), sm(4)
        msB, rsB = sm(16), sm(16)
        nmx = sm(4)
        rsum = sm(16)
        recA, msA, rsA = sm(8), sm(8), sm(8)
        rsum2, rec2, wgt2 = sm(16), sm(4), sm(2)
        ms2, rs2 = sm(4), sm(4)
        lams = sm(2)
        lame = sm(2)
        nlam = sm(1)
        gsub = sm(1)
        ssf = sm(16)
        sst, rsf = sm(4), sm(4)
        lamm = sb("lamm", [P, 2, HD], F32, M + 108)

        chunks = []
        chunk_of = {}

        def chunk(name, *areas):
            parts, at = [], 0
            for sources in areas:
                if not isinstance(sources, list):
                    sources = [sources]
                nk, n = sources[0].shape[1], sum(src.shape[2] for src in sources)
                parts.append((at, nk, n, sources))
                at += nk * n
            assert at <= SLOT
            chunk_of[name] = len(chunks)
            chunks.append((name, parts, at))

        tiles = []
        tile_at = {}
        last_use = {}

        def tile(name, of=None):
            tile_at[name] = len(tiles)
            tiles.append(name)
            if of is not None:
                last_use[chunk_of[of]] = len(tiles) - 1

        k_in = w_in_d.rearrange("(k p) n -> p k n", p=P)
        k_out = w_out_d.rearrange("(k p) n -> p k n", p=P)
        k_up = w_up_d.rearrange("(k p) n -> p k n", p=P)
        k_down = w_down_d.rearrange("(k p) n -> p k n", p=P)
        k_in2 = w_in2_d.rearrange("(k p) n -> p k n", p=P)
        k_uq = w_uq_d.rearrange("(k p) (h n) -> p k h n", p=P, h=4)
        k_ukv = w_ukv_d.rearrange("(k p) n -> p k n", p=P)
        k_pd = w_pd_d.rearrange("(k p) n -> p k n", p=P)
        k_pm = w_pm_d.rearrange("(k p) n -> p k n", p=P)
        k_out2 = w_out2_d.rearrange("(k p) n -> p k n", p=P)

        order = []

        def stage(*s):
            order.append(s)

        stage("params")
        stage("x_norm")
        for j in range(KD):
            tile(("x", j))
            stage("x_t", j)

        def in_chunk(name, at):
            chunk(name, k_in[:, :, at:at + 256])

        in_chunk("c_f", OFF_CF)
        in_chunk("c_q", OFF_CQ)
        in_chunk("c_i", OFF_CI)
        in_chunk("c_g", OFF_CG)
        in_chunk("b_o", OFF_BO)
        for i in range(2):
            in_chunk(f"b_qk{i}", OFF_BQK + 256 * i)
        in_chunk("b_v", OFF_BV)
        for kind, at in (("a_q", OFF_AQ), ("a_k", OFF_AK), ("a_v", OFF_AV)):
            for i in range(2):
                in_chunk(f"{kind}{i}", at + 256 * i)

        def in_tile(kind, i, of):
            tile((kind, i), of)
            stage(kind, i)

        for kind in ("c_f", "c_q", "c_i"):
            for i in range(2):
                in_tile(kind, i, kind)
        later = [("c_g", i, "c_g") for i in range(2)] + [("b_o", i, "b_o") for i in range(2)] + [("gates", 0, None)]
        later += [("b_qk", i, f"b_qk{i // 2}") for i in range(4)] + [("b_v", i, "b_v") for i in range(2)]
        for kind in ("a_q", "a_k", "a_v"):
            later += [(kind, i, f"{kind}{i // 2}") for i in range(4)]
        stage("hg_begin")
        beside = [("hg_att", j) for j in range(LC - 1, -1, -1)]
        beside += [("hg_att_out",), ("hg_kdT", 0), ("hg_kdT", 1)]
        for p in range(2):
            beside += [("hg_rep", p, hh) for hh in range(2)]
            beside += [("hg_u", p, b) for b in range(NB)] + [("hg_scan", p), ("hg_o", p), ("hg_y", p)]
        late = beside[:]
        for n, (kind, i, of) in enumerate(later):
            in_tile(kind, i, of)
            for _ in range(2 if n >= 2 else 1):
                if late:
                    stage(*late.pop(0))
            if kind == "gates":
                stage("gate_math")
        for s in late:
            stage(*s)
        for t in range(4):
            stage("conv", t)
        for h in range(BH):
            stage("ml", h)
            if h >= 1:
                stage("ml_o", h - 1)
        stage("ml_o", BH - 1)
        for i in range(8):
            stage("qk_norm", i)
        stage("yb_norm")
        for p in range(2):
            tile(("yb", p))
            stage("yb", p)
        fox = [(qb, h) for qb in range(NB) for h in range(AH)]
        for u in range(len(fox)):
            if u == 0:
                stage("fox_s", 0)
            if u + 1 < len(fox):
                stage("fox_s", u + 1)
            stage("fox_t", u)
            if u >= 1:
                stage("fox_v", u - 1)
            if u % AH == 2 and u > AH:
                tile(("ya", u // AH - 1))
                stage("ya", u // AH - 1)
            if u == 3:
                for i in range(4):
                    stage("y_split", i)
        stage("fox_v", len(fox) - 1)
        tile(("ya", NB - 1))
        stage("ya", NB - 1)
        for c in range(4):
            chunk(f"w_out{c}", k_out[:, :, 256 * c:256 * c + 256])
        for j in range(KD):
            tile(("w_out", j), f"w_out{j // 2}")
            stage("w_out", j)
        stage("norm", 0)

        def up_pair(c):
            for kind, at in (("gate", 0), ("up", DFF)):
                chunk(f"{kind}{c}", k_up[:, :, at + 256 * c:at + 256 * c + 256])
                for i in (2 * c, 2 * c + 1):
                    tile((kind, i), f"{kind}{c}")
                    stage(kind, i)

        def down_half(half):
            k0, nk = half * FHALF[0], FHALF[half]
            for j in range(KD):
                chunk(f"down{half}{j}", k_down[:, k0:k0 + nk, P * j:P * j + P])
                tile(("down", half, j), f"down{half}{j}")
                stage("down", half, j)

        for c in range(FT // 2):
            up_pair(c)
            if 2 * c == FHALF[0]:
                down_half(0)
        stage("hid_flush")
        stage("rope_tables")
        down_half(1)
        stage("norm", 1)
        for kind, at in (("dq", OFF_DQ), ("dk", OFF_DK), ("dv", OFF_DV), ("dg", OFF_DG)):
            for c in range(2):
                chunk(f"{kind}{c}", k_in2[:, :, at + 256 * c:at + 256 * c + 256])
            for i in range(4):
                in_tile(kind, i, f"{kind}{i // 2}")
        dif = [(qb, h) for qb in range(NB) for h in range(4)]

        def attention(name, units, per, tag):
            for u in range(len(units)):
                if u == 0:
                    stage(name + "_s", 0)
                if u + 1 < len(units):
                    stage(name + "_s", u + 1)
                stage(name + "_t", u)
                if u >= 1:
                    stage(name + "_v", u - 1)
                if u % per == 2 and u > per:
                    tile((tag, u // per - 1))
                    stage(tag, u // per - 1)
            stage(name + "_v", len(units) - 1)
            tile((tag, NB - 1))
            stage(tag, NB - 1)

        attention("dif", dif, 4, "yd")
        chunk("cq0", k_in2[:, :, OFF_CQ2:OFF_CQ2 + 256])
        chunk("cq1", k_in2[:, :, OFF_CQ2 + 256:OFF_CQ2 + 384], [k_in2[:, :, OFF_KR:OFF_KR + 64]] * 2)
        chunk("ckv", k_in2[:, :, OFF_CKV:OFF_CKV + 256])
        for c in range(2):
            chunk(f"mg{c}", k_in2[:, :, OFF_MG + 256 * c:OFF_MG + 256 * c + 256])
        for i in range(3):
            in_tile("lat", i, "cq0" if i < 2 else "cq1")
        in_tile("kr", 0, "cq1")
        for i in range(3, 5):
            in_tile("lat", i, "ckv")
        stage("lat_norm", 0)
        stage("lat_norm", 1)
        for i in range(4):
            in_tile("mg", i, f"mg{i // 2}")
        chunk("uqn", *[k_uq[:, :, h, 0:128] for h in range(4)])
        chunk("uqr", [k_uq[:, :, h, 128:192] for h in range(4)])
        chunk("ukv", k_ukv)
        for i in range(4):
            in_tile("qn", i, "uqn")
        for i in range(2):
            in_tile("qr", i, "uqr")
        for i in range(4):
            in_tile("kn", i, "ukv")
        for i in range(4):
            in_tile("mv", i, "ukv")
        mla = [(qb, h) for qb in range(NB) for h in range(4)]
        attention("mla", mla, 4, "ym")
        for c in range(4):
            chunk(f"gd{c}", k_in2[:, :, OFF_GD + 256 * c:OFF_GD + 256 * c + 256])
            chunk(f"gm{c}", k_in2[:, :, OFF_GM + 256 * c:OFF_GM + 256 * c + 256])
            chunk(f"pj{c}", k_pd[:, :, 256 * c:256 * c + 256], k_pm[:, :, 256 * c:256 * c + 256])
            for kind, of in (("gd", f"gd{c}"), ("gm", f"gm{c}"), ("pd", f"pj{c}"), ("pm", f"pj{c}")):
                for i in (2 * c, 2 * c + 1):
                    tile((kind, i), of)
                    stage(kind, i)
        stage("m_flush")
        for c in range(4):
            chunk(f"w_out2{c}", k_out2[:, :, 256 * c:256 * c + 256])
            for i in range(2):
                tile(("out", c, i), f"w_out2{c}")
                stage("out", c, i)
        stage("final")

        def upto(name):
            return tile_at[name] + 1

        def bank_free(name):
            return ring_free[tile_at[name] % 2]

        def drains(name):
            return tile_at[name] // 2 + 1

        def at_ring(name):
            return ring[tile_at[name] % 2]

        def v3(ap, b):
            return ap.rearrange("p (a b) -> p a b", b=b)

        N_CONST = 5
        HG = {("u", p, b): p * NB + b for p in range(2) for b in range(NB)}

        block = ctx.enter_context(nc.Block())

        @block.sync
        def _(sp):
            sp.dma_start(xtok[:], x_d.rearrange("(b p) d -> p b d", p=P)).then_inc(x_in, 16)
            sp.dma_start(con[:], con_d).then_inc(const_in, 16)
            sp.dma_start(par[:], par_d).then_inc(const_in, 16)
            for c, (name, parts, n) in enumerate(chunks):
                if name == "w_out0":
                    sp.wait_ge(hg_done, 2)
                    sp.dma_start(xres[:], x_d.rearrange("(b p) d -> p b d", p=P)).then_inc(xres_in, 16)
                if c >= 2:
                    sp.wait_ge(split_done, c - 1)
                for at, nk, w, sources in parts:
                    dst = raw[c % 2][:, at:at + nk * w].rearrange("p (k n) -> p k n", k=nk)
                    col = 0
                    for src in sources:
                        sp.dma_start(dst[:, :, col:col + src.shape[2]], src).then_inc(raw_in[c % 2], 16)
                        col += src.shape[2]
                if c == 0:
                    sp.dma_start(wg[:], w_gate_d).then_inc(wg_in, 16)
                    for i, (at, w) in enumerate(((OFF_AV, 512), (OFF_BV, 256), (OFF_CI, 256))):
                        to = (0, 512, 768)[i]
                        sp.dma_start(bias_t[:, to:to + w], b_in_d[at:at + w].partition_broadcast(P)).then_inc(bias_in, 16)
                    sp.dma_start(lamv[:].rearrange("p a b -> p (a b)"), lam_d.partition_broadcast(P)).then_inc(lam_in, 16)
                if name == f"down0{KD - 1}":
                    sp.dma_start(posI[:], pos_d.partition_broadcast(P)).then_inc(pos_in, 16)
            sp.wait_ge(tile_done, upto(("pm", KD - 1)))
            sp.dma_start(gfin[:], g_fin_d.partition_broadcast(P)).then_inc(gfin_in, 16)
            for b in range(NB):
                sp.wait_ge(out_ready, b + 1)
                sp.dma_start(out_d.rearrange("(b p) d -> p b d", p=P)[:, b, :], xo[:, b, :]).then_inc(out_done, 16)
            sp.wait_ge(out_done, 16 * NB)

        @block.gpsimd
        def _(pool):
            landed = [0, 0]
            for c, (name, parts, n) in enumerate(chunks):
                landed[c % 2] += 16 * sum(len(sources) for _, _, _, sources in parts)
                pool.wait_ge(raw_in[c % 2], landed[c % 2])
                if c >= 3:
                    pool.wait_ge(tile_done, last_use[c - 3] + 1)
                pool.tensor_scalar(whi[c % 3][:, 0:n], raw[c % 2][:, 0:n], 1.0, 0.0, ALU.mult, ALU.add).then_inc(hi_done, 1)
                pool.wait_ge(hi_done, c + 1)
                pool.tensor_tensor(wlo[c % 3][:, 0:n], raw[c % 2][:, 0:n], whi[c % 3][:, 0:n].bitcast(F32),
                                   ALU.subtract).then_inc(split_done, 1)

        @block.tensor
        def _(pe):
            def weights(of, part=0):
                c = chunk_of[of]
                at, nk, n, _ = chunks[c][1][part]
                pe.wait_ge(split_done, c + 1)
                return [w[c % 3][:, at:at + nk * n].rearrange("p (k n) -> p k n", k=nk) for w in (whi, wlo)]

            def product(out, pairs, last=True, before=None):
                for n, ((ah, al), (bh, bl)) in enumerate(pairs):
                    if before is not None:
                        before(n)
                    pe.matmul(out, ah, bh, start=(n == 0), stop=False)
                    pe.matmul(out, ah, bl, start=False, stop=False)
                    mm = pe.matmul(out, al, bh, start=False, stop=(last and n == len(pairs) - 1))
                return mm

            def open_bank(name):
                n = tile_at[name]
                if n >= 2:
                    pe.wait_ge(ring_free[n % 2], n // 2)
                return ring[n % 2]

            def channels(name, of, col, acts, nk=KD, part=0, before=None, m=P):
                out = open_bank(name)
                wh, wl = weights(of, part)
                ah, al = acts
                pairs = [((wh[:, k, col:col + m], wl[:, k, col:col + m]), (ah[:, k, :], al[:, k, :])) for k in range(nk)]
                product(out[:], pairs, before=before).then_inc(tile_done, 1)

            def tokens(name, of, i, acts):
                out = open_bank(name)
                wh, wl = weights(of)
                ah, al = acts
                for s in range(2):
                    b = 2 * i + s
                    pairs = [((ah[:, k, b * P:b * P + P], al[:, k, b * P:b * P + P]), (wh[:, k, :], wl[:, k, :])) for k in range(KD)]
                    mm = product(out[:, 256 * s:256 * s + 256], pairs)
                mm.then_inc(tile_done, 1)

            act = (hH, hL)
            for s in order:
                kind = s[0]
                if kind == "x_t":
                    j = s[1]
                    if j == 0:
                        pe.wait_ge(const_in, 32)
                        pe.wait_ge(x_h, NB)
                    out = open_bank(("x", j))
                    for b in range(NB):
                        mm = pe.transpose(out[:, b * P:b * P + P], htok[:, b, j * P:j * P + P], ident)
                    mm.then_inc(tile_done, 1)
                elif kind in ("c_f", "c_q", "c_g", "b_o"):
                    def first(k):
                        pe.wait_ge(bank_free(("x", k)), drains(("x", k)))
                    channels((kind, s[1]), kind, P * s[1], act, before=first if s == ("c_f", 0) else None)
                elif kind in ("b_qk", "a_q", "a_k"):
                    channels((kind, s[1]), f"{kind}{s[1] // 2}", P * (s[1] % 2), act)
                elif kind in ("c_i", "b_v"):
                    tokens((kind, s[1]), kind, s[1], act)
                elif kind == "a_v":
                    tokens((kind, s[1]), f"a_v{s[1] // 2}", s[1] % 2, act)
                elif kind == "gates":
                    pe.wait_ge(wg_in, 16)
                    out = open_bank(("gates", 0))
                    pairs = KD
                    for k in range(KD):
                        pe.matmul(out[0:96, :], wg[:, k, :], hH[:, k, :].bitcast(F32), start=(k == 0), stop=False)
                        mm = pe.matmul(out[0:96, :], wg[:, k, :], hL[:, k, :].bitcast(F32), start=False, stop=(k == KD - 1))
                    mm.then_inc(tile_done, 1)
                elif kind == "gate_math":
                    pe.wait_ge(gate_rows, 2)
                    for n, src in enumerate((g1, g3)):
                        for b in range(NB):
                            mm = pe.transpose(bank[2][:, 16 * n + 4 * b:16 * n + 4 * b + 4], src[32:36, b * P:b * P + P],
                                              con[32:36, 32:36])
                    mm.then_inc(gate_cols, 1)
                elif kind == "hg_att":
                    j = s[1]
                    n = LC - 1 - j
                    pe.wait_ge(hg_a, n + 1)
                    for p in range(2):
                        mm = pe.matmul(bank[p][0:64, :], con[:, CCOL["win"][0] + LC - 1 - j:CCOL["win"][0] + LC - 1 - j + 64],
                                       Ab[n % 2][:, p, :], start=(n == 0), stop=(n == LC - 1))
                    mm.then_inc(hg_a_used, 1)
                elif kind == "hg_kdT":
                    p = s[1]
                    pe.wait_ge(hg_q, 1)
                    for b in range(NB):
                        mm = pe.transpose(bank[4 + p][:, b * P:b * P + P], kd[:, p, 8 * b:8 * b + 8, :], ident)
                    mm.then_inc(hg_kdT_mm, 1)
                elif kind == "hg_rep":
                    p, hh = s[1:]
                    n = 2 * p + hh
                    pe.wait_ge(hg_att_s, 2)
                    if n == 0:
                        pe.wait_ge(gate_cols_out, 1)
                    if n >= 2:
                        pe.wait_ge(hg_dm, n - 1)
                    pe.matmul(bank[2 + hh][:], cc("rep", slice(32 * hh, 32 * hh + LC)), attS[32 * hh:32 * hh + LC, p, :],
                              start=True, stop=True).then_inc(hg_rep_mm, 1)
                elif kind == "hg_u":
                    p, b = s[1:]
                    n = HG["u", p, b]
                    pe.wait_ge(hg_kdT_s, 2)
                    pe.wait_ge(hg_vx, n + 1)
                    if n >= 2:
                        pe.wait_ge(hg_u_s, n - 1)
                    for hh in range(2):
                        mm = pe.matmul(bank[4 + n % 2][64 * hh:64 * hh + 64, :], kdT[:, p, b, 64 * hh:64 * hh + 64],
                                       Vx[2 * (n % 2) + hh][:], start=True, stop=True)
                    mm.then_inc(hg_u_mm, 1)
                elif kind == "hg_o":
                    p = s[1]
                    pe.wait_ge(hg_scan, p + 1)
                    pe.wait_ge(hg_dm, 2 * p + 2)
                    for hh in range(2):
                        r = slice(64 * hh, 64 * hh + 64)
                        for b in range(NB):
                            pe.matmul(bank[p][r, b * P:b * P + P], ci[:, b, (2 * p + hh) * HD:(2 * p + hh + 1) * HD],
                                      Dm[hh][:, b, :], start=True, stop=False)
                            for c in range(max(8 * b, 1), 8 * b + 8):
                                mm = pe.matmul(bank[p][r, c * LC:c * LC + LC], U[r, :, c - 1], cq[r, p, c, 0:LC],
                                               start=False, stop=(c == 8 * b + 7))
                    mm.then_inc(hg_o_mm, 1)
                elif kind in ("hg_y", "qk_norm"):
                    n = s[1] + (2 if kind == "qk_norm" else 0)
                    pe.wait_ge(nrm_sq, n + 1)
                    if n == 0:
                        pe.wait_ge(hg_u_s, NB)
                    if n == 1:
                        pe.wait_ge(hg_u_s, 2 * NB)
                    if n >= 2:
                        pe.wait_ge(nrm_rs, n - 1)
                    pe.matmul(bank[4 + n % 2][:], cc("blk"), scr[n % 2][:], start=True, stop=True).then_inc(nrm_mm, 1)
                elif kind == "ml":
                    h = s[1]
                    r = slice(64 * (h % 2), 64 * (h % 2) + 64)
                    if h == 0:
                        pe.wait_ge(hg_done, 2)
                        pe.wait_ge(hg_dm, 4)
                        pe.wait_ge(qkB_ready, 4)
                        pe.wait_ge(gate_rows, 2)
                    if h >= 1:
                        pe.wait_ge(ml_w, 4 * h)
                    pe.matmul(bank[0][:], con[32:36, 32 + h:33 + h].broadcast_to([4, P]), g2[32:36, :],
                              start=True, stop=True).then_inc(ml_m_mm, 1)
                    for b in range(NB):
                        n = 4 * h + b
                        if n >= 2:
                            pe.wait_ge(ml_p, n - 1)
                        pe.matmul(bank[1 + n % 2][:, 0:T - P * b], qkB[r, 2 + h // 2, b * P:b * P + P],
                                  qkB[r, h // 2, b * P:T], start=True, stop=True).then_inc(ml_s_mm, 1)
                elif kind == "ml_o":
                    h = s[1]
                    pe.wait_ge(ml_p, 4 * h + 4)
                    if h >= 1:
                        pe.wait_ge(ml_o_s, h)
                    for tb in range(NB):
                        for b in range(tb + 1):
                            at = (0, 512, 896, 1152)[b] + (tb - b) * P
                            mm = pe.matmul(bank[3][:, 65 * tb:65 * tb + 65], PM[h % 2][:, at:at + P], bv[:, b, h, :],
                                           start=(b == 0), stop=(b == tb))
                    mm.then_inc(ml_o_mm, 1)
                elif kind == "yb":
                    p = s[1]
                    out = open_bank(("yb", p))
                    pe.wait_ge(yb_n, 1)
                    for b in range(NB):
                        mm = pe.transpose(out[:, b * P:b * P + P], onB[:, b, 2 * p:2 * p + 2, :], ident)
                    mm.then_inc(tile_done, 1)
                elif kind == "fox_s":
                    u = s[1]
                    qb, h = fox[u]
                    n = (qb + 1) * P
                    r = slice(64 * (h % 2), 64 * (h % 2) + 64)
                    if u == 0:
                        pe.wait_ge(qk_done, 8)
                        pe.wait_ge(negC_ready, 1)
                        pe.wait_ge(mask_ready, 2)
                        pe.wait_ge(ml_p, 16)
                        pe.wait_ge(ml_o_s, 4)
                    if u >= 2:
                        pe.wait_ge(fox_e, u - 1)
                    out = bank[u % 2]
                    pe.matmul(out[:, 0:n], qT[r, h // 2, qb * P:qb * P + P], kT[r, h // 2, 0:n], start=True, stop=False)
                    pe.matmul(out[:, 0:n], con[r, 64 * (h % 2) + h:64 * (h % 2) + h + 1].broadcast_to([64, P]), negC[r, 0:n],
                              start=False, stop=False)
                    pe.matmul(out[:, qb * P:n], identb[:], maskb[:], start=False, stop=True).then_inc(fox_s_mm, 1)
                elif kind == "fox_t":
                    u = s[1]
                    qb, h = fox[u]
                    pe.wait_ge(fox_e, u + 1)
                    if u >= 2:
                        pe.wait_ge(fox_pt, u - 1)
                    for b in range(qb + 1):
                        mm = pe.transpose(bank[2 + u % 2][:, b * P:b * P + P], Pf[u % 2][:, b * P:b * P + P], ident)
                    mm.then_inc(fox_t_mm, 1)
                elif kind == "fox_v":
                    u = s[1]
                    qb, h = fox[u]
                    pe.wait_ge(fox_pt, u + 1)
                    if u == 0:
                        pe.wait_ge(nrm_rs, 10)
                    if h == 0:
                        if qb >= 2:
                            pe.wait_ge(fox_o_free, qb - 1)
                    for b in range(qb + 1):
                        mm = pe.matmul(bank[4 + qb % 2][:, HD * h:HD * h + HD], PTs[u % 2][:, b * P:b * P + P],
                                       av[:, b, HD * h:HD * h + HD], start=(b == 0), stop=(b == qb))
                    mm.then_inc(fox_v_mm, 1)
                elif kind == "ya":
                    qb = s[1]
                    out = open_bank(("ya", qb))
                    pe.wait_ge(ya_n, qb + 1)
                    for j in range(4):
                        mm = pe.transpose(out[:, j * P:j * P + P], on[:, 2 * j:2 * j + 2, :], ident)
                    mm.then_inc(tile_done, 1)
                elif kind == "w_out":
                    j = s[1]
                    if j == 0:
                        pe.wait_ge(y_lo, 4 + NB)
                        pe.wait_ge(xres_in, 16)
                    out = open_bank(("w_out", j))
                    wh, wl = weights(f"w_out{j // 2}")
                    col = P * (j % 2)
                    product(out[:], [((wh[:, k, col:col + P], wl[:, k, col:col + P]), (hH[:, k, :], hL[:, k, :])) for k in range(KD)],
                            last=False)
                    for b in range(NB):
                        mm = pe.matmul(out[:, b * P:b * P + P], xres[:, b, j * P:j * P + P], ident, start=False, stop=(b == NB - 1))
                    mm.then_inc(tile_done, 1)
                elif kind == "norm":
                    i = s[1]
                    if i == 0:
                        pe.wait_ge(fox_e, len(fox))
                    for j in range(KD):
                        pe.wait_ge(n_sq, KD * i + j + 1)
                        mm = pe.matmul(bank[0][:], cc("ones"), sqn[j % 2][:], start=(j == 0), stop=(j == KD - 1))
                        mm.then_inc(n_mm, 1)
                elif kind in ("gate", "up"):
                    def first(k):
                        pe.wait_ge(n_lo, k + 1)
                    channels(s, f"{kind}{s[1] // 2}", P * (s[1] % 2), act, before=first if s == ("gate", 0) else None)
                elif kind == "down":
                    half, j = s[1:]
                    k0, nk = half * FHALF[0], FHALF[half]
                    pe.wait_ge(hid_lo, k0 + nk)
                    out = open_bank(s)
                    wh, wl = weights(f"down{half}{j}")
                    product(out[:], [((wh[:, k, :], wl[:, k, :]), (hidH[:, (k0 + k) % HSLOT, :], hidL[:, (k0 + k) % HSLOT, :]))
                                     for k in range(nk)]).then_inc(tile_done, 1)
                elif kind in ("dq", "dk", "dg", "mg", "gd", "gm"):
                    def first(k):
                        pe.wait_ge(n_lo, KD + k + 1)
                    channels(s, f"{kind}{s[1] // 2}", P * (s[1] % 2), act, before=first if s == ("dq", 0) else None)
                elif kind == "dv":
                    tokens(s, f"dv{s[1] // 2}", s[1] % 2, act)
                elif kind == "lat":
                    i = s[1]
                    channels(s, ("cq0", "cq0", "cq1", "ckv", "ckv")[i], (0, P, 0, 0, P)[i], act)
                elif kind == "kr":
                    channels(s, "cq1", 0, act, part=1)
                elif kind == "lat_norm":
                    i = s[1]
                    for n in ((0, 1, 2), (3, 4))[i]:
                        pe.wait_ge(lat_sq, n + 1)
                        if n == 0:
                            pe.wait_ge(dif_e, 2 * len(dif))
                        pe.matmul(bank[i][:], cc("ones"), zs[n % 2][:], start=n in (0, 3), stop=n in (2, 4)).then_inc(lat_mm, 1)
                elif kind in ("qn", "qr", "kn"):
                    i = s[1]
                    if kind == "qn" and i == 0:
                        pe.wait_ge(lat_lo, 5)
                    out = open_bank(s)
                    if kind == "qn":
                        wh, wl = weights("uqn", i)
                        st = [(wh[:, k, :], wl[:, k, :]) for k in range(3)]
                    elif kind == "qr":
                        wh, wl = weights("uqr")
                        st = [(wh[:, k, P * i:P * i + P], wl[:, k, P * i:P * i + P]) for k in range(3)]
                    else:
                        wh, wl = weights("ukv")
                        st = [(wh[:, k, 256 * i:256 * i + P], wl[:, k, 256 * i:256 * i + P]) for k in range(2)]
                    first = 3 if kind == "kn" else 0
                    product(out[:], [(w, (latHq[first + k][:], latLq[first + k][:])) for k, w in enumerate(st)]).then_inc(tile_done, 1)
                elif kind == "mv":
                    b = s[1]
                    out = open_bank(s)
                    wh, wl = weights("ukv")
                    of = [w.rearrange("p k (h n) -> p k h n", h=4) for w in (wh, wl)]
                    t = slice(b * P, b * P + P)
                    product(v3(out[:], P), [((latHq[3 + k][:, t], latLq[3 + k][:, t]), (of[0][:, k, :, P:256], of[1][:, k, :, P:256]))
                                     for k in range(2)]).then_inc(tile_done, 1)
                elif kind == "dif_s":
                    u = s[1]
                    qb, h = dif[u]
                    n = (qb + 1) * P
                    if u == 0:
                        pe.wait_ge(rope_done, 8)
                        pe.wait_ge(n_rs, 2)
                    for m in range(2):
                        r = slice(64 * m, 64 * m + 64)
                        if 2 * u + m - 1 > 0:
                            pe.wait_ge(dif_e, 2 * u + m - 1)
                        pe.matmul(bank[m][:, 0:n], dq[r, h, qb * P:qb * P + P], dk[r, h, 0:n], start=True, stop=False)
                        pe.matmul(bank[m][:, qb * P:n], identb[:], maskb[:], start=False, stop=True).then_inc(dif_s_mm, 1)
                elif kind == "dif_t":
                    u = s[1]
                    qb, h = dif[u]
                    pe.wait_ge(dif_c, u + 1)
                    if u >= 2:
                        pe.wait_ge(dif_pt, u - 1)
                    for b in range(qb + 1):
                        mm = pe.transpose(bank[2 + u % 2][:, b * P:b * P + P], P2[2 * (u % 2)][:, b * P:b * P + P], ident)
                    mm.then_inc(dif_t_mm, 1)
                elif kind in ("dif_v", "mla_v"):
                    u = s[1]
                    qb, h = dif[u]
                    name = kind[:3]
                    vals = dv if name == "dif" else mv
                    pt, o_free, v_mm = (dif_pt, dif_o_free, dif_v_mm) if name == "dif" else (mla_pt, mla_o_free, mla_v_mm)
                    pe.wait_ge(pt, u + 1)
                    if h == 0:
                        if qb >= 2:
                            pe.wait_ge(o_free, qb - 1)
                    if u == 0 and name == "dif":
                        pe.wait_ge(bank_free(("dv", 3)), drains(("dv", 3)))
                    for b in range(qb + 1):
                        mm = pe.matmul(bank[4 + qb % 2][:, P * h:P * h + P], PT2[u % 2][:, b * P:b * P + P],
                                       vals[:, b, P * h:P * h + P], start=(b == 0), stop=(b == qb))
                    mm.then_inc(v_mm, 1)
                elif kind in ("yd", "ym"):
                    qb = s[1]
                    out = open_bank(s)
                    pe.wait_ge((yd_n if kind == "yd" else ym_n), qb + 1)
                    for h in range(4):
                        mm = pe.transpose(out[:, h * P:h * P + P], on2[:, h, :], ident)
                    mm.then_inc(tile_done, 1)
                elif kind == "mla_s":
                    u = s[1]
                    qb, h = mla[u]
                    n = (qb + 1) * P
                    r = slice(64 * (h % 2), 64 * (h % 2) + 64)
                    if u == 0:
                        for b in range(2, 4):
                            pe.wait_ge(bank_free(("mv", b)), drains(("mv", b)))
                        pe.wait_ge(rope_done, 11)
                        pe.wait_ge(lat_rs, 2)
                    if u >= 2:
                        pe.wait_ge(mla_e, u - 1)
                    out = bank[u % 2]
                    pe.matmul(out[:, 0:n], qn[:, h, qb * P:qb * P + P], kn[:, h, 0:n], start=True, stop=False)
                    pe.matmul(out[:, 0:n], qr[r, h // 2, qb * P:qb * P + P], kr[r, 0:n], start=False, stop=False)
                    pe.matmul(out[:, qb * P:n], identb[:], maskb[:], start=False, stop=True).then_inc(mla_s_mm, 1)
                elif kind == "mla_t":
                    u = s[1]
                    qb, h = mla[u]
                    pe.wait_ge(mla_e, u + 1)
                    if u >= 2:
                        pe.wait_ge(mla_pt, u - 1)
                    for b in range(qb + 1):
                        mm = pe.transpose(bank[2 + u % 2][:, b * P:b * P + P], P2[u % 2][:, b * P:b * P + P], ident)
                    mm.then_inc(mla_t_mm, 1)
                elif kind in ("pd", "pm"):
                    i = s[1]
                    if s == ("pd", 0):
                        pe.wait_ge(o_lo, 2 * NB)
                    at = 0 if kind == "pd" else 4
                    channels(s, f"pj{i // 2}", P * (i % 2), (oH[:, at:at + 4, :], oL[:, at:at + 4, :]), nk=4, part=0 if kind == "pd" else 1)
                elif kind == "out":
                    c, i = s[1:]
                    out = open_bank(s)
                    wh, wl = weights(f"w_out2{c}")
                    if c == 0 and i == 0:
                        pe.wait_ge(m_lo, KD)
                    for e in range(2):
                        b = 2 * i + e
                        t = slice(b * P, b * P + P)
                        to = out[:, 256 * e:256 * e + 256]
                        product(to, [((mH[:, k, t], mL[:, k, t]), (wh[:, k, :], wl[:, k, :])) for k in range(KD)], last=False)
                        for j in range(2):
                            mm = pe.matmul(out[:, 256 * e + P * j:256 * e + P * j + P], xT[:, 2 * c + j, t], ident, start=False, stop=(j == 1))
                    mm.then_inc(tile_done, 1)

        @block.scalar
        def _(act):
            steps = [0]

            def step():
                steps[0] += 1
                return steps[0]

            A = act.activation
            for s in order:
                kind = s[0]
                if kind == "params":
                    act.wait_ge(const_in, 32)
                    act.wait_ge(lb_d, 1)
                    A(lbe, lbd, ACT.Exp).then_inc(lb_e, 1)
                elif kind == "x_norm":
                    act.wait_ge(x_in, 16)
                    for b in range(NB):
                        A(htok[:, b, :], xtok[:, b, :], ACT.Square, accum_out=ss_x[:, b:b + 1]).then_inc(x_ss, 1)
                    act.wait_ge(x_var, 1)
                    A(var_x, var_x, ACT.Ln).then_inc(act_step, 1)
                    act.wait_ge(act_step, step())
                    A(rs_x, var_x, ACT.Exp, scale=-0.5).then_inc(x_rs, 1)
                elif kind == "x_t":
                    j = s[1]
                    act.wait_ge(tile_done, upto(("x", j)))
                    A(hH[:, j, :], at_ring(("x", j))[:], ACT.Identity, scale=pc("g_mix", j)).then_inc(h_hi, 1)
                elif kind == "c_f":
                    p = s[1]
                    act.wait_ge(nbcf_ready, 1)
                    act.wait_ge(tile_done, upto(s))
                    A(cf[:, p].rearrange("p c t -> p (c t)"), at_ring(s)[:], ACT.Sigmoid, bias=pc("b_cf", p))
                    A(ck[:, p].rearrange("p c t -> p (c t)"), at_ring(s)[:], ACT.Sigmoid, bias=nbcf[:, p:p + 1], scale=-1.0).then_inc(bank_free(s), 1)
                elif kind == "c_q":
                    p = s[1]
                    act.wait_ge(tile_done, upto(s))
                    A(cq[:, p, :, 0:LC], v3(at_ring(s)[:], LC), ACT.Silu, bias=pc("b_cq", p)).then_inc(bank_free(s), 1)
                elif kind == "c_g":
                    act.wait_ge(tile_done, upto(s))
                    A(cg[:, s[1], :], at_ring(s)[:], ACT.Silu, bias=pc("b_cg", s[1])).then_inc(bank_free(s), 1)
                elif kind == "b_o":
                    act.wait_ge(tile_done, upto(s))
                    A(bo[:, s[1], :], at_ring(s)[:], ACT.Sigmoid, bias=pc("b_bo", s[1])).then_inc(bank_free(s), 1)
                elif kind == "gates":
                    act.wait_ge(tile_done, upto(s))
                    A(gz[:], at_ring(s)[0:96, :], ACT.Identity, bias=pc("b_gate", r=slice(0, 96))).then_inc(bank_free(s), 1)
                elif kind == "gate_math":
                    act.wait_ge(bank_free(("gates", 0)), drains(("gates", 0)))
                    A(g1[:], gz[:], ACT.Abs).then_inc(act_step, 1)
                    act.wait_ge(act_step, step())
                    A(g1[:], g1[:], ACT.Exp, scale=-1.0).then_inc(act_step, 1)
                    act.wait_ge(act_step, step())
                    A(g1[:], g1[:], ACT.Ln, bias=1.0).then_inc(gate_ln, 1)
                    act.wait_ge(gate_m, 1)
                    A(g3[32:36, :], g3[32:36, :], ACT.Exp, scale=-1.0).then_inc(gate_rows, 1)
                elif kind in ("b_qk", "a_q", "a_k"):
                    i = s[1]
                    dst, b = {"b_qk": (bqk[:, i, 3:T + 3], "b_bqk"), "a_q": (qT[:, i, :], "b_aq"), "a_k": (kT[:, i, :], "b_ak")}[kind]
                    act.wait_ge(tile_done, upto(s))
                    A(dst, at_ring(s)[:], ACT.Identity, bias=pc(b, i)).then_inc(bank_free(s), 1)
                elif kind == "hg_att_out":
                    act.wait_ge(hg_a_used, LC)
                    act.wait_ge(hg_q, 1)
                    for p in range(2):
                        A(attS[:, p, :], bank[p][0:64, :], ACT.Identity).then_inc(hg_att_s, 1)
                elif kind == "hg_kdT":
                    p = s[1]
                    act.wait_ge(hg_kdT_mm, p + 1)
                    A(kdT[:, p].rearrange("p b d -> p (b d)"), bank[4 + p][:], ACT.Identity).then_inc(hg_kdT_s, 1)
                elif kind == "hg_u":
                    p, b = s[1:]
                    n = HG["u", p, b]
                    act.wait_ge(hg_u_mm, n + 1)
                    if p == 1:
                        act.wait_ge(hg_o_mm, 1)
                    A(U[:, :, 8 * b:8 * b + 8], bank[4 + n % 2][:].rearrange("p (c e) -> p e c", e=HD), ACT.Identity).then_inc(hg_u_s, 1)
                elif kind in ("hg_y", "qk_norm"):
                    i = s[1]
                    n = i + (2 if kind == "qk_norm" else 0)
                    if n >= 2:
                        act.wait_ge(nrm_done, n - 1)
                    if kind == "hg_y":
                        act.wait_ge(hg_o_mm, i + 1)
                        src = bank[i][:]
                    else:
                        src = (qT if i < 4 else kT)[:, i % 4, :]
                        act.wait_ge(bank_free(("a_q" if i < 4 else "a_k", i % 4)), drains(("a_q" if i < 4 else "a_k", i % 4)))
                    A(scr[n % 2][:], src, ACT.Square).then_inc(nrm_sq, 1)
                    act.wait_ge(nrm_mm, n + 1)
                    A(scr[n % 2][:], bank[4 + n % 2][:], ACT.Ln, bias=cc("eps"), scale=1.0 / HD).then_inc(act_step, 1)
                    act.wait_ge(act_step, step())
                    A(scr[n % 2][:], scr[n % 2][:], ACT.Exp, scale=-0.5).then_inc(nrm_rs, 1)
                elif kind == "conv":
                    t = s[1]
                    act.wait_ge(conv_b, t + 1)
                    A(qkB[:, t, :], qkB[:, t, :], ACT.Silu).then_inc(qkB_ready, 1)
                elif kind == "ml":
                    h = s[1]
                    act.wait_ge(ml_w, 4 * h + 4)
                    A(PM[h % 2][:], PM[h % 2][:], ACT.Exp).then_inc(ml_e, 1)
                elif kind == "yb_norm":
                    act.wait_ge(yb_var, 1)
                    A(msB, msB, ACT.Ln).then_inc(act_step, 1)
                    act.wait_ge(act_step, step())
                    A(rsB, msB, ACT.Exp, scale=-0.5).then_inc(yb_rs, 1)
                elif kind == "fox_s":
                    u = s[1]
                    qb, h = fox[u]
                    n = (qb + 1) * P
                    act.wait_ge(fox_m, u + 1)
                    if u >= 2:
                        act.wait_ge(fox_t_mm, u - 1)
                    A(Pf[u % 2][:, 0:n], bank[u % 2][:, 0:n], ACT.Exp, bias=nmx[:, u % 4:u % 4 + 1],
                      accum_out=rsum[:, 8 * (qb % 2) + h:8 * (qb % 2) + h + 1]).then_inc(fox_e, 1)
                elif kind == "ya":
                    qb = s[1]
                    act.wait_ge(ya_var, qb + 1)
                    A(msA, msA, ACT.Ln).then_inc(act_step, 1)
                    act.wait_ge(act_step, step())
                    A(rsA, msA, ACT.Exp, scale=-0.5).then_inc(ya_rs, 1)
                    act.wait_ge(bank_free(s), drains(s))
                    A(hH[:, 0:4, qb * P:qb * P + P], yt[:], ACT.Identity).then_inc(ya_hi, 1)
                elif kind == "y_split":
                    i = s[1]
                    src = (bo if i < 2 else cg)[:, i % 2, :]
                    if i == 0:
                        act.wait_ge(bank_free(("yb", 0)), drains(("yb", 0)))
                        act.wait_ge(bank_free(("yb", 1)), drains(("yb", 1)))
                        act.wait_ge(hg_done, 2)
                        act.wait_ge(tile_done, upto(("a_v", 3)))
                    A(hH[:, 4 + i, :], src, ACT.Identity).then_inc(ys_hi, 1)
                elif kind == "w_out":
                    j = s[1]
                    act.wait_ge(tile_done, upto(s))
                    A(xT[:, j, :], at_ring(s)[:], ACT.Identity).then_inc(bank_free(s), 1)
                elif kind == "norm":
                    i = s[1]
                    for j in range(KD):
                        act.wait_ge(bank_free(("w_out", j) if i == 0 else ("down", 1, j)), drains(("w_out", j) if i == 0 else ("down", 1, j)))
                        if KD * i + j - 1 > 0:
                            act.wait_ge(n_mm, KD * i + j - 1)
                        A(sqn[j % 2][:], xT[:, j, :], ACT.Square).then_inc(n_sq, 1)
                    act.wait_ge(n_mm, KD * i + KD)
                    A(rsn[:], bank[0][:], ACT.Ln, bias=cc("eps"), scale=1.0 / D).then_inc(act_step, 1)
                    act.wait_ge(act_step, step())
                    A(rsn[:], rsn[:], ACT.Exp, scale=-0.5).then_inc(n_rs, 1)
                    for j in range(KD):
                        act.wait_ge(normed, KD * i + j + 1)
                        A(hH[:, j, :], hb[j % 2][:], ACT.Identity).then_inc(n_hi, 1)
                elif kind in ("gate", "up"):
                    i = s[1]
                    act.wait_ge(tile_done, upto(s))
                    if i >= 2:
                        act.wait_ge((conv_g if kind == "gate" else conv_u), i - 1)
                    if i == 0 and kind == "gate":
                        act.wait_ge(zp_zero, 1)
                    A(zp[(0 if kind == "gate" else 2) + i % 2][:, 2:T + 2], at_ring(s)[:], ACT.Identity).then_inc(bank_free(s), 1)
                    if kind == "up":
                        act.wait_ge(conv_g, i + 1)
                        A(cvg[i % 2][:], cvg[i % 2][:], ACT.Silu).then_inc(silu_ready, 1)
                        if i >= 1:
                            if i >= 1:
                                act.wait_ge(hidden, i)
                            A(hidH[:, (i - 1) % HSLOT, :], hid[(i - 1) % 2][:], ACT.Identity).then_inc(hid_hi, 1)
                elif kind == "hid_flush":
                    act.wait_ge(hidden, FT)
                    A(hidH[:, (FT - 1) % HSLOT, :], hid[(FT - 1) % 2][:], ACT.Identity).then_inc(hid_hi, 1)
                elif kind == "rope_tables":
                    act.wait_ge(rot_ready, 1)
                    A(sinT[:], rotT[:], ACT.Sin).then_inc(sin_ready, 1)
                    act.wait_ge(rot_ready, 2)
                    A(cosT[:], angT[:], ACT.Sin).then_inc(cos_ready, 1)
                    act.wait_ge(lam_s, 2)
                    A(lame, lams, ACT.Exp).then_inc(lam_e, 1)
                elif kind in ("dq", "dk", "qr", "kr"):
                    n = {"dq": 0, "dk": 4, "kr": 8, "qr": 9}[kind] + s[1]
                    act.wait_ge(tile_done, upto(s))
                    if n >= 2:
                        act.wait_ge(rope_done, n - 1)
                    z, o = zs[n % 2], at_ring(s)
                    if n == 8:
                        act.wait_ge(dif_v_mm, len(dif))
                    for g in range(4):
                        f = g ^ 1
                        ins = A(z[32 * g:32 * g + 32, :], o[32 * f:32 * f + 32, :], ACT.Identity)
                    ins.then_inc(rope_z, 1)
                elif kind in ("dg", "mg"):
                    act.wait_ge(tile_done, upto(s))
                    A((sdg if kind == "dg" else smg)[:, s[1], :], at_ring(s)[:], ACT.Silu).then_inc(bank_free(s), 1)
                elif kind == "dif_s":
                    u = s[1]
                    qb, h = dif[u]
                    n = (qb + 1) * P
                    if u == 0:
                        act.wait_ge(lam_done, 1)
                        act.wait_ge(cos_ready, 1)
                    for m in range(2):
                        act.wait_ge(dif_m, 2 * u + m + 1)
                        if m == 0:
                            if u >= 2:
                                act.wait_ge(dif_t_mm, u - 1)
                            if u >= 2:
                                act.wait_ge(dif_c, u - 1)
                        A(P2[2 * (u % 2) + m][:, 0:n], bank[m][:, 0:n], ACT.Exp, bias=nmx[:, 2 * (u % 2) + m:2 * (u % 2) + m + 1],
                          accum_out=rsum2[:, 8 * (qb % 2) + 4 * m + h:8 * (qb % 2) + 4 * m + h + 1]).then_inc(dif_e, 1)
                elif kind == "yd":
                    qb = s[1]
                    act.wait_ge(yd_var, qb + 1)
                    A(ms2, ms2, ACT.Ln).then_inc(act_step, 1)
                    act.wait_ge(act_step, step())
                    A(rs2, ms2, ACT.Exp, scale=-0.5).then_inc(yd_rs, 1)
                    act.wait_ge(bank_free(s), drains(s))
                    A(oH[:, 0:4, qb * P:qb * P + P], yt2[:], ACT.Identity).then_inc(o_hi, 1)
                elif kind == "ym":
                    qb = s[1]
                    act.wait_ge(bank_free(s), drains(s))
                    if qb == 0:
                        act.wait_ge(tile_done, upto(("mv", 3)))
                    A(oH[:, 4:8, qb * P:qb * P + P], yt2[:], ACT.Identity).then_inc(o_hi, 1)
                elif kind == "lat":
                    i = s[1]
                    act.wait_ge(tile_done, upto(s))
                    if i == 0:
                        act.wait_ge(dif_t_mm, len(dif))
                    A(lat[:, i, :], at_ring(s)[:], ACT.Identity).then_inc(bank_free(s), 1)
                elif kind == "lat_norm":
                    i = s[1]
                    for n in ((0, 1, 2), (3, 4))[i]:
                        if n >= 2:
                            act.wait_ge(lat_mm, n - 1)
                        if n == 0:
                            act.wait_ge(bank_free(("lat", 4)), drains(("lat", 4)))
                            act.wait_ge(bank_free(("lat", 3)), drains(("lat", 3)))
                            act.wait_ge(rope_done, 9)
                        A(zs[n % 2][:], lat[:, n, :], ACT.Square).then_inc(lat_sq, 1)
                    act.wait_ge(lat_mm, (3, 5)[i])
                    if i == 1:
                        act.wait_ge(lat_t, 3)
                    A(rsn[:], bank[i][:], ACT.Ln, bias=cc("eps"), scale=1.0 / (384, 256)[i]).then_inc(act_step, 1)
                    act.wait_ge(act_step, step())
                    A(rsn[:], rsn[:], ACT.Exp, scale=-0.5).then_inc(lat_rs, 1)
                    for n in ((0, 1, 2), (3, 4))[i]:
                        act.wait_ge(lat_t, n + 1)
                        A(latHq[n][:], lat[:, n, :], ACT.Identity).then_inc(lat_hi, 1)
                elif kind in ("qn", "kn"):
                    act.wait_ge(tile_done, upto(s))
                    A((qn if kind == "qn" else kn)[:, s[1], :], at_ring(s)[:], ACT.Identity, scale=MLA_SCALE if kind == "qn" else 1.0).then_inc(bank_free(s), 1)
                elif kind == "mv":
                    act.wait_ge(tile_done, upto(s))
                    A(mv[:, s[1], :], at_ring(s)[:], ACT.Identity).then_inc(bank_free(s), 1)
                elif kind == "mla_s":
                    u = s[1]
                    qb, h = mla[u]
                    n = (qb + 1) * P
                    act.wait_ge(mla_m, u + 1)
                    if u >= 2:
                        act.wait_ge(mla_t_mm, u - 1)
                    A(P2[u % 2][:, 0:n], bank[u % 2][:, 0:n], ACT.Exp, bias=nmx[:, u % 4:u % 4 + 1],
                      accum_out=rsum2[:, 4 * (qb % 2) + h:4 * (qb % 2) + h + 1]).then_inc(mla_e, 1)
                elif kind in ("gd", "gm"):
                    i = s[1]
                    act.wait_ge(tile_done, upto(s))
                    if i >= 2:
                        act.wait_ge((gated_d if kind == "gd" else gated_m), i - 1)
                    if i == 0:
                        act.wait_ge(o_lo, 2 * NB)
                    A((sgd if kind == "gd" else sgm)[i % 2][:], at_ring(s)[:], ACT.Sigmoid).then_inc(bank_free(s), 1)
                elif kind == "pm":
                    i = s[1]
                    if i >= 1:
                        if i >= 1:
                            act.wait_ge(merged, i)
                        A(mH[:, i - 1, :], mt2[(i - 1) % 2][:], ACT.Identity).then_inc(m_hi, 1)
                elif kind == "m_flush":
                    act.wait_ge(merged, KD)
                    A(mH[:, KD - 1, :], mt2[(KD - 1) % 2][:], ACT.Identity).then_inc(m_hi, 1)
                elif kind == "out":
                    c, i = s[1:]
                    act.wait_ge(tile_done, upto(s))
                    A(xo[:, 2 * i:2 * i + 2, 256 * c:256 * c + 256], v3(at_ring(s)[:], 256), ACT.Identity).then_inc(bank_free(s), 1)
                    act.wait_ge(bank_free(s), drains(s))
                    for e in range(2):
                        b = 2 * i + e
                        A(sqn[e][:, 0:256], xo[:, b, 256 * c:256 * c + 256], ACT.Square,
                          accum_out=ssf[:, 4 * b + c:4 * b + c + 1]).then_inc(ssf_ready, 1)
                    act.wait_ge(ssf_ready, 4 * c + 2 * i + 2)
                elif kind == "final":
                    act.wait_ge(f_var, 1)
                    A(sst, sst, ACT.Ln).then_inc(act_step, 1)
                    act.wait_ge(act_step, step())
                    A(rsf, sst, ACT.Exp, scale=-0.5).then_inc(f_rs, 1)

        @block.vector
        def _(dve):
            steps = [0]

            def step():
                steps[0] += 1
                return steps[0]

            TT, TS, STT, CP = dve.tensor_tensor, dve.tensor_scalar, dve.scalar_tensor_tensor, dve.tensor_copy

            def wide(ap, n):
                return ap.unsqueeze(2).broadcast_to([ap.shape[0], ap.shape[1], n])

            def low(hi, full, dst):
                return TT(dst, full, hi.bitcast(F32), ALU.subtract)

            for s in order:
                kind = s[0]
                if kind == "params":
                    dve.wait_ge(const_in, 32)
                    TT(lbd, pc("lb", 0, 2), pc("lb", 0, 2), ALU.subtract).then_inc(lb_d, 1)
                    TS(nbcf, pc("b_cf", 0, 2), -1.0, None, ALU.mult).then_inc(nbcf_ready, 1)
                    TS(gq8, pc("g_aq"), HD ** -0.5, None, ALU.mult).then_inc(dve_step, 1)
                    dve.wait_ge(dve_step, step())
                    TS(gsub, pc("g_sub"), 1.0 - LAMBDA_INIT, None, ALU.mult).then_inc(dve_step, 1)
                    dve.wait_ge(dve_step, step())
                    CP(identb[:], cc("ident")).then_inc(mask_ready, 1)
                    CP(maskb[:], cc("neg")).then_inc(mask_ready, 1)
                    dve.wait_ge(lb_e, 1)
                    dve.reciprocal(lbr, lbe).then_inc(dve_step, 1)
                    dve.wait_ge(dve_step, step())
                    TT(lbp, lbe, lbr, ALU.mult).then_inc(dve_step, 1)
                    dve.wait_ge(dve_step, step())
                    TT(lb, lbp, lbp, ALU.subtract).then_inc(dve_step, 1)
                    dve.wait_ge(dve_step, step())
                    TS(lb, lb, 0.0, None, ALU.max).then_inc(dve_step, 1)
                    dve.wait_ge(dve_step, step())
                    TS(lb1, lb, -1.0, 1.0, ALU.mult, ALU.add).then_inc(dve_step, 1)
                    dve.wait_ge(dve_step, step())
                elif kind == "x_norm":
                    dve.wait_ge(x_ss, NB)
                    TS(var_x, ss_x, 1.0 / D, EPS, ALU.mult, ALU.add).then_inc(x_var, 1)
                    dve.wait_ge(x_rs, 1)
                    for b in range(NB):
                        TS(htok[:, b, :], xtok[:, b, :], rs_x[:, b:b + 1], None, ALU.mult).then_inc(x_h, 1)
                elif kind == "x_t":
                    j = s[1]
                    dve.wait_ge(h_hi, j + 1)
                    STT(hL[:, j, :], at_ring(("x", j))[:], pc("g_mix", j), hH[:, j, :].bitcast(F32),
                             ALU.mult, ALU.subtract).then_inc(bank_free(("x", j)), 1)
                elif kind == "hg_begin":
                    for p in range(2):
                        dve.wait_ge(bank_free(("c_f", p)), drains(("c_f", p)))
                        dve.wait_ge(bank_free(("c_q", p)), drains(("c_q", p)))
                        TS(cf[:, p], cf[:, p], lb1[:, p:p + 1], lb[:, p:p + 1], ALU.mult, ALU.add).then_inc(dve_step, 1)
                        dve.wait_ge(dve_step, step())
                        TS(ck[:, p], ck[:, p], lb1[:, p:p + 1], None, ALU.mult).then_inc(dve_step, 1)
                        dve.wait_ge(dve_step, step())
                    dve.memset(cq[:, :, :, LC:LC + 1], 1.0).then_inc(dve_step, 1)
                    dve.wait_ge(dve_step, step())
                    for i in range(2):
                        dve.wait_ge(bank_free(("c_i", i)), drains(("c_i", i)))
                elif kind == "c_i":
                    i = s[1]
                    if i == 0:
                        dve.wait_ge(bias_in, 48)
                    dve.wait_ge(tile_done, upto(s))
                    TT(ci[:, 2 * i:2 * i + 2, :], v3(at_ring(s)[:], 256),
                            bias_t[:, 768:1024].unsqueeze(1).broadcast_to([P, 2, 256]), ALU.add).then_inc(bank_free(s), 1)
                elif kind == "b_v":
                    i = s[1]
                    if i == 0:
                        dve.wait_ge(tile_done, upto(("x", KD - 1)))
                        dve.memset(bv[:, :, :, HD:HD + 1], 1.0).then_inc(dve_step, 1)
                        dve.wait_ge(dve_step, step())
                    dve.wait_ge(tile_done, upto(s))
                    for e in range(2):
                        ins = TT(bv[:, 2 * i + e, :, 0:HD], v3(at_ring(s)[:, 256 * e:256 * e + 256], HD), v3(bias_t[:, 512:768], HD), ALU.add)
                    ins.then_inc(bank_free(s), 1)
                elif kind == "a_v":
                    i = s[1]
                    half, e = i // 2, i % 2
                    dve.wait_ge(tile_done, upto(s))
                    TT(av[:, 2 * e:2 * e + 2, 256 * half:256 * half + 256], v3(at_ring(s)[:], 256),
                            bias_t[:, 256 * half:256 * half + 256].unsqueeze(1).broadcast_to([P, 2, 256]), ALU.add).then_inc(bank_free(s), 1)
                elif kind == "gate_math":
                    dve.wait_ge(gate_ln, 1)
                    STT(g2[:], gz[:], 0.0, g1[:], ALU.min, ALU.subtract).then_inc(dve_step, 1)
                    dve.wait_ge(dve_step, step())
                    dve.memset(g1[:], 1.0).then_inc(dve_step, 1)
                    dve.wait_ge(dve_step, step())
                    dve.tensor_tensor_scan(g3[:], g1[:], g2[:], 0.0, ALU.mult, ALU.add).then_inc(dve_step, 1)
                    dve.wait_ge(dve_step, step())
                    dve.memset(negC[:], 0.0).then_inc(dve_step, 1)
                    dve.wait_ge(dve_step, step())
                    TS(negC[0:8, :], g3[0:8, :], -1.0, None, ALU.mult).then_inc(dve_step, 1)
                    dve.wait_ge(dve_step, step())
                    TS(negC[64:72, :], g3[0:8, :], -1.0, None, ALU.mult).then_inc(negC_ready, 1)
                    CP(g3[32:36, :], g3[64:68, :]).then_inc(dve_step, 1)
                    dve.wait_ge(dve_step, step())
                    TT(gz[32:36, :], gz[32:36, :], g3[32:36, :], ALU.subtract).then_inc(dve_step, 1)
                    dve.wait_ge(dve_step, step())
                    dve.tensor_tensor_scan(g2[32:36, :], g1[32:36, :], gz[32:36, :], -3e38, ALU.mult, ALU.max).then_inc(dve_step, 1)
                    dve.wait_ge(dve_step, step())
                    CP(g1[32:36, :], gz[32:36, :]).then_inc(dve_step, 1)
                    dve.wait_ge(dve_step, step())
                    TT(g3[32:36, :], g3[32:36, :], g2[32:36, :], ALU.add).then_inc(gate_m, 1)
                    dve.wait_ge(gate_m, 1)
                    TS(g2[32:36, :], g2[32:36, :], -1.0, None, ALU.mult).then_inc(gate_rows, 1)
                    dve.wait_ge(gate_cols, 1)
                    CP(colB, bank[2][:, 0:32]).then_inc(gate_cols_out, 1)
                elif kind == "hg_att":
                    j = s[1]
                    n = LC - 1 - j
                    if n >= 2:
                        dve.wait_ge(hg_a_used, n - 1)
                    q64 = cq[:].rearrange("p h c t -> p (h c) t")
                    f64 = cf[:].rearrange("p h c t -> p (h c) t")
                    k64 = ck[:].rearrange("p h c t -> p (h c) t")
                    d64 = kd[:].rearrange("p h c t -> p (h c) t")
                    TT(Ab[n % 2][:].rearrange("p h (c t) -> p (h c) t", t=LC), q64[:, :, 0:LC], k64[:, :, j:j + 1].broadcast_to([P, 64, LC]),
                       ALU.mult).then_inc(hg_a, 1)
                    TT(d64[:, :, j:j + 1], q64[:, :, LC:LC + 1], k64[:, :, j:j + 1], ALU.mult).then_inc(dve_step, 1)
                    dve.wait_ge(dve_step, step())
                    dve.wait_ge(hg_a, n + 1)
                    m = LC + 1 - j
                    ins = TT(q64[:, :, j:LC + 1], q64[:, :, j:LC + 1], f64[:, :, j:j + 1].broadcast_to([P, 64, m]), ALU.mult)
                    if j == 0:
                        ins.then_inc(hg_q, 1)
                        dve.wait_ge(hg_q, 1)
                        for p in range(2):
                            dve.memset(cq[:, p, 0, LC:LC + 1], 0.0).then_inc(dve_step, 1)
                            dve.wait_ge(dve_step, step())
                    else:
                        ins.then_inc(dve_step, 1)
                        dve.wait_ge(dve_step, step())
                elif kind == "hg_rep":
                    p, hh = s[1:]
                    n = 2 * p + hh
                    dve.wait_ge(hg_rep_mm, n + 1)
                    if p >= 1:
                        dve.wait_ge(hg_o_mm, p)
                    TT(Dm[hh][:], v3(bank[2 + hh][:], P), cc("chunk").unsqueeze(1).broadcast_to([P, NB, P]), ALU.mult).then_inc(hg_dm, 1)
                elif kind == "hg_u":
                    p, b = s[1:]
                    n = HG["u", p, b]
                    if n >= 2:
                        dve.wait_ge(hg_u_mm, n - 1)
                    if n == 0:
                        dve.wait_ge(hg_a_used, LC)
                    for hh in range(2):
                        c = (2 * p + hh) * HD
                        ins = TT(Vx[2 * (n % 2) + hh][:], ci[:, b, c:c + HD].unsqueeze(1).broadcast_to([P, 8, HD]),
                                 wide(cc("inchunk"), HD), ALU.mult)
                    ins.then_inc(hg_vx, 1)
                elif kind == "hg_scan":
                    p = s[1]
                    CP(Gx[:], cq[:, p, :, LC:LC + 1].rearrange("p c o -> p o c").broadcast_to([P, HD // 2, NC])).then_inc(dve_step, 1)
                    dve.wait_ge(dve_step, step())
                    dve.wait_ge(hg_u_s, NB * (p + 1))
                    g = Gx[:].rearrange("p e c -> p (e c)")
                    for e in range(2):
                        u = U[:, 32 * e:32 * e + 32, :].rearrange("p e c -> p (e c)")
                        ins = dve.tensor_tensor_scan(u, g, u, 0.0, ALU.mult, ALU.add)
                        if e == 0:
                            ins.then_inc(dve_step, 1)
                            dve.wait_ge(dve_step, step())
                    ins.then_inc(hg_scan, 1)
                    dve.wait_ge(hg_scan, p + 1)
                elif kind == "hg_y":
                    p = s[1]
                    dve.wait_ge(nrm_rs, p + 1)
                    TT(scr[p][:], bank[p][:], scr[p][:], ALU.mult).then_inc(hg_n, 1)
                    dve.wait_ge(hg_n, p + 1)
                    STT(cg[:, p, :], scr[p][:], pc("g_out", 6 + p), cg[:, p, :], ALU.mult, ALU.mult).then_inc(nrm_done, 1)
                    dve.wait_ge(nrm_done, p + 1)
                    dve.engine_nop().then_inc(hg_done, 1)
                elif kind == "conv":
                    t = s[1]
                    if t == 0:
                        dve.memset(bqk[:, :, 0:3], 0.0).then_inc(dve_step, 1)
                        dve.wait_ge(dve_step, step())
                    dve.wait_ge(bank_free(("b_qk", t)), drains(("b_qk", t)))
                    TS(qkB[:, t, :], bqk[:, t, 0:T], pc("w_bconv", t), None, ALU.mult).then_inc(dve_step, 1)
                    dve.wait_ge(dve_step, step())
                    for k in range(1, 4):
                        ins = STT(qkB[:, t, :], bqk[:, t, k:k + T], pc("w_bconv", 4 * k + t), qkB[:, t, :], ALU.mult, ALU.add)
                        if k < 3:
                            ins.then_inc(dve_step, 1)
                            dve.wait_ge(dve_step, step())
                    ins.then_inc(conv_b, 1)
                elif kind == "ml":
                    h = s[1]
                    segs = (0, 512, 896, 1152)
                    dve.wait_ge(ml_m_mm, h + 1)
                    if h >= 2:
                        dve.wait_ge(ml_o_mm, h - 1)
                    for b in range(NB):
                        w = T - P * b
                        TS(PM[h % 2][:, segs[b]:segs[b] + w], bank[0][:, b * P:T], colB[:, 4 * b + h:4 * b + h + 1], 0.0,
                           ALU.add, ALU.min).then_inc(ml_w, 1)
                    dve.wait_ge(ml_e, h + 1)
                    for b in range(NB):
                        TT(PM[h % 2][:, segs[b]:segs[b] + P], PM[h % 2][:, segs[b]:segs[b] + P], cc("tri"), ALU.mult).then_inc(dve_step, 1)
                        dve.wait_ge(dve_step, step())
                    for b in range(NB):
                        w = T - P * b
                        dve.wait_ge(ml_s_mm, 4 * h + b + 1)
                        seg = PM[h % 2][:, segs[b]:segs[b] + w]
                        STT(seg, bank[1 + (4 * h + b) % 2][:, 0:w], HD ** -0.5, seg, ALU.mult, ALU.mult).then_inc(ml_p, 1)
                elif kind == "ml_o":
                    h = s[1]
                    dve.wait_ge(ml_o_mm, h + 1)
                    CP(Oh[:].rearrange("p b e -> p (b e)"), bank[3][:, 0:260]).then_inc(ml_o_s, 1)
                    dve.wait_ge(ml_o_s, h + 1)
                    den = Oh[:, :, HD:HD + 1].rearrange("p b o -> p (b o)")
                    STT(denB, den, -1.0, den, ALU.mult, ALU.max).then_inc(dve_step, 1)
                    dve.wait_ge(dve_step, step())
                    em = colB[:, 16:32].rearrange("p (b h) -> p b h", h=4)[:, :, h:h + 1].rearrange("p b o -> p (b o)")
                    TT(denB, denB, em, ALU.max).then_inc(dve_step, 1)
                    dve.wait_ge(dve_step, step())
                    dve.reciprocal(recB, denB).then_inc(dve_step, 1)
                    dve.wait_ge(dve_step, step())
                    TT(onB[:, :, h, :], Oh[:, :, 0:HD], wide(recB, HD), ALU.mult).then_inc(dve_step, 1)
                    dve.wait_ge(dve_step, step())
                elif kind == "qk_norm":
                    i = s[1]
                    dve.wait_ge(nrm_rs, i + 3)
                    dst = (qT if i < 4 else kT)[:, i % 4, :]
                    STT(dst, dst, gq8 if i < 4 else pc("g_ak"), scr[i % 2][:], ALU.mult, ALU.mult).then_inc(nrm_done, 1)
                    dve.wait_ge(nrm_done, i + 3)
                    dve.engine_nop().then_inc(qk_done, 1)
                elif kind == "yb_norm":
                    o16 = onB[:].rearrange("p b h e -> p (b h) e")
                    q16 = sqB[:].rearrange("p b h e -> p (b h) e")
                    TT(q16, o16, o16, ALU.mult).then_inc(dve_step, 1)
                    dve.wait_ge(dve_step, step())
                    dve.tensor_reduce(msB, q16, AX.X, ALU.add).then_inc(dve_step, 1)
                    dve.wait_ge(dve_step, step())
                    TS(msB, msB, 1.0 / HD, EPS, ALU.mult, ALU.add).then_inc(yb_var, 1)
                    dve.wait_ge(yb_rs, 1)
                    TT(o16, o16, wide(rsB, HD), ALU.mult).then_inc(yb_n, 1)
                elif kind == "yb":
                    p = s[1]
                    dve.wait_ge(tile_done, upto(s))
                    STT(bo[:, p, :], at_ring(s)[:], pc("g_out", 4 + p), bo[:, p, :], ALU.mult, ALU.mult).then_inc(bank_free(s), 1)
                elif kind == "fox_s":
                    u = s[1]
                    qb, h = fox[u]
                    n = (qb + 1) * P
                    dve.wait_ge(fox_s_mm, u + 1)
                    dve.tensor_reduce(nmx[:, u % 4:u % 4 + 1], bank[u % 2][:, 0:n], AX.X, ALU.max, negate=True).then_inc(fox_m, 1)
                elif kind == "fox_t":
                    u = s[1]
                    qb, h = fox[u]
                    n = (qb + 1) * P
                    dve.wait_ge(fox_t_mm, u + 1)
                    if u >= 2:
                        dve.wait_ge(fox_v_mm, u - 1)
                    CP(PTs[u % 2][:, 0:n], bank[2 + u % 2][:, 0:n]).then_inc(fox_pt, 1)
                elif kind == "ya":
                    qb = s[1]
                    dve.wait_ge(fox_v_mm, AH * (qb + 1))
                    dve.reciprocal(recA, rsum[:, 8 * (qb % 2):8 * (qb % 2) + 8]).then_inc(dve_step, 1)
                    dve.wait_ge(dve_step, step())
                    if qb >= 1:
                        dve.wait_ge(tile_done, upto(("ya", qb - 1)))
                    TT(on[:], v3(bank[4 + qb % 2][:], HD), wide(recA, HD), ALU.mult).then_inc(fox_o_free, 1)
                    dve.wait_ge(fox_o_free, qb + 1)
                    TT(sqA[:], on[:], on[:], ALU.mult).then_inc(dve_step, 1)
                    dve.wait_ge(dve_step, step())
                    dve.tensor_reduce(msA, sqA[:], AX.X, ALU.add).then_inc(dve_step, 1)
                    dve.wait_ge(dve_step, step())
                    TS(msA, msA, 1.0 / HD, EPS, ALU.mult, ALU.add).then_inc(ya_var, 1)
                    dve.wait_ge(ya_rs, qb + 1)
                    TT(on[:], on[:], wide(rsA, HD), ALU.mult).then_inc(ya_n, 1)
                    dve.wait_ge(tile_done, upto(s))
                    TT(yt[:], v3(at_ring(s)[:], P), wide(pc("g_out", 0, 4), P), ALU.mult).then_inc(bank_free(s), 1)
                    dve.wait_ge(ya_hi, qb + 1)
                    t = slice(qb * P, qb * P + P)
                    low(hH[:, 0:4, t], yt[:], hL[:, 0:4, t]).then_inc(y_lo, 1)
                    dve.wait_ge(y_lo, 4 + qb + 1)
                elif kind == "y_split":
                    i = s[1]
                    dve.wait_ge(ys_hi, i + 1)
                    low(hH[:, 4 + i, :], (bo if i < 2 else cg)[:, i % 2, :], hL[:, 4 + i, :]).then_inc(y_lo, 1)
                elif kind == "norm":
                    i = s[1]
                    dve.wait_ge(n_rs, i + 1)
                    if i == 1:
                        dve.wait_ge(tile_done, upto(("up", FT - 1)))

                    def lower(j):
                        dve.wait_ge(n_hi, KD * i + j + 1)
                        low(hH[:, j, :], hb[j % 2][:], hL[:, j, :]).then_inc(n_lo, 1)

                    for j in range(KD):
                        if j >= 2:
                            if KD * i + j - 1 > 0:
                                dve.wait_ge(n_lo, KD * i + j - 1)
                        STT(hb[j % 2][:], xT[:, j, :], pc(("g_ffn", "g_in2")[i], j), rsn[:], ALU.mult, ALU.mult).then_inc(normed, 1)
                        if j >= 1:
                            lower(j - 1)
                    lower(KD - 1)
                    if i == 0:
                        for z in zp:
                            ins = dve.memset(z[:, 0:2], 0.0)
                        ins.then_inc(zp_zero, 1)
                        dve.wait_ge(zp_zero, 1)
                elif kind in ("gate", "up"):
                    i = s[1]
                    g = 0 if kind == "gate" else FT
                    z = zp[(0 if kind == "gate" else 2) + i % 2]
                    dst = (cvg if kind == "gate" else cvu)[i % 2]
                    dve.wait_ge(bank_free(s), drains(s))
                    if i >= 2:
                        if i >= 2:
                            dve.wait_ge(hidden, i - 1)
                    TS(dst[:], z[:, 0:T], pc("w_fconv", g + i), pc("b_fconv", g + i), ALU.mult, ALU.add).then_inc(dve_step, 1)
                    dve.wait_ge(dve_step, step())
                    STT(dst[:], z[:, 1:T + 1], pc("w_fconv", 44 + g + i), dst[:], ALU.mult, ALU.add).then_inc(dve_step, 1)
                    dve.wait_ge(dve_step, step())
                    STT(dst[:], z[:, 2:T + 2], pc("w_fconv", 88 + g + i), dst[:], ALU.mult, ALU.add).then_inc(
                        (conv_g if kind == "gate" else conv_u), 1)
                    if kind == "up":
                        dve.wait_ge(conv_u, i + 1)
                        dve.wait_ge(silu_ready, i + 1)
                        if i >= 2:
                            dve.wait_ge(hid_lo, i - 1)
                        TT(hid[i % 2][:], cvg[i % 2][:], cvu[i % 2][:], ALU.mult).then_inc(hidden, 1)
                        if i >= 1:
                            if i >= 1:
                                dve.wait_ge(hid_hi, i)
                            low(hidH[:, (i - 1) % HSLOT, :], hid[(i - 1) % 2][:], hidL[:, (i - 1) % HSLOT, :]).then_inc(hid_lo, 1)
                elif kind == "hid_flush":
                    dve.wait_ge(hid_hi, FT)
                    low(hidH[:, (FT - 1) % HSLOT, :], hid[(FT - 1) % 2][:], hidL[:, (FT - 1) % HSLOT, :]).then_inc(hid_lo, 1)
                elif kind == "down":
                    half, j = s[1:]
                    dve.wait_ge(tile_done, upto(s))
                    if half == 1:
                        dve.wait_ge(bank_free(("down", 0, j)), drains(("down", 0, j)))
                    TT(xT[:, j, :], xT[:, j, :], at_ring(s)[:], ALU.add).then_inc(bank_free(s), 1)
                elif kind == "rope_tables":
                    dve.wait_ge(pos_in, 16)
                    CP(angT[:], posI[:]).then_inc(dve_step, 1)
                    dve.wait_ge(dve_step, step())
                    TS(angT[:], angT[:], cc("freq"), None, ALU.mult).then_inc(dve_step, 1)
                    dve.wait_ge(dve_step, step())
                    two_pi = 2 * np.pi
                    parts = [6.28125, float(np.float32(two_pi - 6.28125)), 0.0]
                    parts[2] = float(two_pi - parts[0] - parts[1])
                    magic = 1.5 * 2.0 ** 23
                    for which in range(2):
                        turn = cosT if which == 0 else sqn[0]
                        if which == 0:
                            TS(cosT[:], angT[:], 1.0 / two_pi, magic, ALU.mult, ALU.add).then_inc(dve_step, 1)
                            dve.wait_ge(dve_step, step())
                        else:
                            TS(sqn[0][:], angT[:], 1.0 / two_pi, 0.25, ALU.mult, ALU.add).then_inc(dve_step, 1)
                            dve.wait_ge(dve_step, step())
                            TS(sqn[0][:], sqn[0][:], magic, None, ALU.add).then_inc(dve_step, 1)
                            dve.wait_ge(dve_step, step())
                        TS(turn[:], turn[:], -magic, None, ALU.add).then_inc(dve_step, 1)
                        dve.wait_ge(dve_step, step())
                        dst = rotT if which == 0 else angT
                        src = angT
                        for part in parts:
                            STT(dst[:], turn[:], -part, src[:], ALU.mult, ALU.add).then_inc(dve_step, 1)
                            dve.wait_ge(dve_step, step())
                            src = dst
                        if which == 1:
                            TS(dst[:], dst[:], cc("halfpi"), None, ALU.add).then_inc(dve_step, 1)
                            dve.wait_ge(dve_step, step())
                        TS(dst[:], dst[:], 3.1415925, -3.1415925, ALU.min, ALU.max).then_inc(rot_ready, 1)
                        dve.wait_ge(rot_ready, which + 1)
                    dve.wait_ge(sin_ready, 1)
                    TS(sinT[:], sinT[:], cc("sign"), None, ALU.mult).then_inc(dve_step, 1)
                    dve.wait_ge(dve_step, step())
                    dve.wait_ge(lam_in, 16)
                    lv = lamv[:].rearrange("p (a b) d -> p a b d", b=2)
                    for m in range(2):
                        TT(lamm[:, m, :], lv[:, m, 0, :], lv[:, m, 1, :], ALU.mult).then_inc(dve_step, 1)
                        dve.wait_ge(dve_step, step())
                        dve.tensor_reduce(lams[:, m:m + 1], lamm[:, m, :], AX.X, ALU.add).then_inc(lam_s, 1)
                    dve.wait_ge(lam_e, 1)
                    TT(nlam, lame[:, 1:2], lame[:, 0:1], ALU.subtract).then_inc(dve_step, 1)
                    dve.wait_ge(dve_step, step())
                    TS(nlam, nlam, -LAMBDA_INIT, None, ALU.add).then_inc(lam_done, 1)
                    dve.wait_ge(lam_done, 1)
                    dve.wait_ge(cos_ready, 1)
                elif kind in ("dq", "dk", "qr", "kr"):
                    n = {"dq": 0, "dk": 4, "kr": 8, "qr": 9}[kind] + s[1]
                    sc = {"dq": HD ** -0.5, "dk": 1.0, "qr": MLA_SCALE, "kr": 1.0}[kind]
                    dst = {"dq": lambda: dq[:, s[1], :], "dk": lambda: dk[:, s[1], :], "qr": lambda: qr[:, s[1], :], "kr": lambda: kr[:]}[kind]()
                    dve.wait_ge(rope_z, n + 1)
                    STT(dst, at_ring(s)[:], sc, cosT[:], ALU.mult, ALU.mult).then_inc(bank_free(s), 1)
                    STT(zs[n % 2][:], zs[n % 2][:], sc, sinT[:], ALU.mult, ALU.mult).then_inc(dve_step, 1)
                    dve.wait_ge(dve_step, step())
                    dve.wait_ge(bank_free(s), drains(s))
                    TT(dst, dst, zs[n % 2][:], ALU.add).then_inc(rope_done, 1)
                elif kind == "dv":
                    i = s[1]
                    half, e = i // 2, i % 2
                    dve.wait_ge(tile_done, upto(s))
                    CP(dv[:, 2 * e:2 * e + 2, 256 * half:256 * half + 256], v3(at_ring(s)[:], 256)).then_inc(bank_free(s), 1)
                elif kind == "dif_s":
                    u = s[1]
                    qb, h = dif[u]
                    n = (qb + 1) * P
                    for m in range(2):
                        dve.wait_ge(dif_s_mm, 2 * u + m + 1)
                        dve.tensor_reduce(nmx[:, 2 * (u % 2) + m:2 * (u % 2) + m + 1], bank[m][:, 0:n], AX.X, ALU.max,
                                          negate=True).then_inc(dif_m, 1)
                elif kind == "dif_t":
                    u = s[1]
                    qb, h = dif[u]
                    n = (qb + 1) * P
                    dve.wait_ge(dif_e, 2 * u + 2)
                    r0, r1 = (rsum2[:, 8 * (qb % 2) + 4 * m + h:8 * (qb % 2) + 4 * m + h + 1] for m in range(2))
                    w, rc = wgt2[:, u % 2:u % 2 + 1], rec2[:, u % 2:u % 2 + 1]
                    dve.reciprocal(rc, r1).then_inc(dve_step, 1)
                    dve.wait_ge(dve_step, step())
                    TS(w, r0, rc, nlam, ALU.mult, ALU.mult).then_inc(dve_step, 1)
                    dve.wait_ge(dve_step, step())
                    a, b = P2[2 * (u % 2)], P2[2 * (u % 2) + 1]
                    STT(a[:, 0:n], b[:, 0:n], w, a[:, 0:n], ALU.mult, ALU.add).then_inc(dif_c, 1)
                    dve.wait_ge(dif_t_mm, u + 1)
                    if u >= 2:
                        dve.wait_ge(dif_v_mm, u - 1)
                    CP(PT2[u % 2][:, 0:n], bank[2 + u % 2][:, 0:n]).then_inc(dif_pt, 1)
                elif kind == "mla_s":
                    u = s[1]
                    qb, h = mla[u]
                    n = (qb + 1) * P
                    dve.wait_ge(mla_s_mm, u + 1)
                    dve.tensor_reduce(nmx[:, u % 4:u % 4 + 1], bank[u % 2][:, 0:n], AX.X, ALU.max, negate=True).then_inc(mla_m, 1)
                elif kind == "mla_t":
                    u = s[1]
                    qb, h = mla[u]
                    n = (qb + 1) * P
                    dve.wait_ge(mla_t_mm, u + 1)
                    if u >= 2:
                        dve.wait_ge(mla_v_mm, u - 1)
                    CP(PT2[u % 2][:, 0:n], bank[2 + u % 2][:, 0:n]).then_inc(mla_pt, 1)
                elif kind in ("yd", "ym"):
                    qb = s[1]
                    o_free, v_mm = (dif_o_free, dif_v_mm) if kind == "yd" else (mla_o_free, mla_v_mm)
                    dve.wait_ge(v_mm, 4 * (qb + 1))
                    at = (8 if kind == "yd" else 4) * (qb % 2)
                    dve.reciprocal(rec2, rsum2[:, at:at + 4]).then_inc(dve_step, 1)
                    dve.wait_ge(dve_step, step())
                    if qb >= 1:
                        dve.wait_ge(tile_done, upto((kind, qb - 1)))
                    elif kind == "ym":
                        dve.wait_ge(tile_done, upto(("yd", NB - 1)))
                    TT(on2[:], v3(bank[4 + qb % 2][:], P), wide(rec2, P), ALU.mult).then_inc(o_free, 1)
                    dve.wait_ge(o_free, qb + 1)
                    if kind == "yd":
                        TT(sq2[:], on2[:], on2[:], ALU.mult).then_inc(dve_step, 1)
                        dve.wait_ge(dve_step, step())
                        dve.tensor_reduce(ms2, sq2[:], AX.X, ALU.add).then_inc(dve_step, 1)
                        dve.wait_ge(dve_step, step())
                        TS(ms2, ms2, 1.0 / P, EPS, ALU.mult, ALU.add).then_inc(yd_var, 1)
                        dve.wait_ge(yd_rs, qb + 1)
                        TT(on2[:], on2[:], wide(rs2, P), ALU.mult).then_inc(yd_n, 1)
                    else:
                        dve.engine_nop().then_inc(ym_n, 1)
                    dve.wait_ge(tile_done, upto(s))
                    t = slice(qb * P, qb * P + P)
                    gate = sdg if kind == "yd" else smg
                    first = 0 if kind == "yd" else 4
                    dve.wait_ge(bank_free(("dg" if kind == "yd" else "mg", 3)), drains(("dg" if kind == "yd" else "mg", 3)))
                    dve.wait_ge(bank_free(("dg" if kind == "yd" else "mg", 2)), drains(("dg" if kind == "yd" else "mg", 2)))
                    if kind == "yd":
                        STT(yt2[:], v3(at_ring(s)[:], P), gsub, gate[:, :, t], ALU.mult, ALU.mult).then_inc(bank_free(s), 1)
                    else:
                        TT(yt2[:], v3(at_ring(s)[:], P), gate[:, :, t], ALU.mult).then_inc(bank_free(s), 1)
                    n = qb + (0 if kind == "yd" else NB)
                    dve.wait_ge(o_hi, n + 1)
                    low(oH[:, first:first + 4, t], yt2[:], oL[:, first:first + 4, t]).then_inc(o_lo, 1)
                    dve.wait_ge(o_lo, n + 1)
                elif kind == "lat_norm":
                    i = s[1]
                    dve.wait_ge(lat_rs, i + 1)
                    for n in ((0, 1, 2), (3, 4))[i]:
                        g = pc("g_cq2", n) if i == 0 else pc("g_ckv", n - 3)
                        STT(lat[:, n, :], lat[:, n, :], g, rsn[:], ALU.mult, ALU.mult).then_inc(lat_t, 1)
                    for n in ((0, 1, 2), (3, 4))[i]:
                        dve.wait_ge(lat_hi, n + 1)
                        low(latHq[n][:], lat[:, n, :], latLq[n][:]).then_inc(lat_lo, 1)
                elif kind in ("pd", "pm"):
                    i = s[1]
                    dve.wait_ge(tile_done, upto(s))
                    dve.wait_ge(bank_free(("gd" if kind == "pd" else "gm", i)), drains(("gd" if kind == "pd" else "gm", i)))
                    dst = (mt if kind == "pd" else mt2)[i % 2]
                    src = (sgd if kind == "pd" else sgm)[i % 2]
                    if kind == "pm":
                        if i >= 2:
                            dve.wait_ge(m_lo, i - 1)
                    elif i >= 2:
                        if i >= 2:
                            dve.wait_ge(merged, i - 1)
                    TT(dst[:], at_ring(s)[:], src[:], ALU.mult).then_inc((gated_d if kind == "pd" else gated_m), 1)
                    dve.wait_ge((gated_d if kind == "pd" else gated_m), i + 1)
                    if kind == "pd":
                        dve.engine_nop().then_inc(bank_free(s), 1)
                    else:
                        TT(mt2[i % 2][:], mt[i % 2][:], mt2[i % 2][:], ALU.add).then_inc(bank_free(s), 1)
                        dve.wait_ge(bank_free(s), drains(s))
                        dve.engine_nop().then_inc(merged, 1)
                        if i >= 1:
                            if i >= 1:
                                dve.wait_ge(m_hi, i)
                            low(mH[:, i - 1, :], mt2[(i - 1) % 2][:], mL[:, i - 1, :]).then_inc(m_lo, 1)
                elif kind == "m_flush":
                    dve.wait_ge(m_hi, KD)
                    low(mH[:, KD - 1, :], mt2[(KD - 1) % 2][:], mL[:, KD - 1, :]).then_inc(m_lo, 1)
                elif kind == "final":
                    dve.wait_ge(ssf_ready, 16)
                    dve.tensor_reduce(sst, v3(ssf, 4), AX.X, ALU.add).then_inc(dve_step, 1)
                    dve.wait_ge(dve_step, step())
                    TS(sst, sst, 1.0 / D, EPS, ALU.mult, ALU.add).then_inc(f_var, 1)
                    dve.wait_ge(f_rs, 1)
                    dve.wait_ge(gfin_in, 16)
                    for b in range(NB):
                        STT(xo[:, b, :], xo[:, b, :], rsf[:, b:b + 1], gfin[:], ALU.mult, ALU.mult).then_inc(out_ready, 1)


def kernel(**inputs):
    import numpy as _np
    import concourse.bacc as _bacc
    from concourse import mybir as _mybir
    from concourse.bass_utils import run_bass_kernel_spmd as _run

    a = {k: _np.asarray(v) for k, v in inputs.items()}
    w_in, b_in = a["w_in"][0], a["b_in"][0]

    par = _np.zeros((P, NPC), _np.float32)

    def cols(name, v):
        at, n = PCOL[name]
        par[:, at:at + n] = v.reshape(n, P).T

    cols("g_mix", a["norm_mix_g"][0])
    cols("g_ffn", a["norm_ffn_g"][0])
    cols("g_in2", a["norm_in_2"][0])
    cols("g_out", a["out_g"][0])
    for name, at, n in (("b_aq", OFF_AQ, 512), ("b_ak", OFF_AK, 512), ("b_bqk", OFF_BQK, 512), ("b_bo", OFF_BO, 256),
                        ("b_cq", OFF_CQ, 256), ("b_cf", OFF_CF, 256), ("b_cg", OFF_CG, 256)):
        cols(name, b_in[at:at + n])
    cols("g_cq2", a["mla_q_norm_2"][0])
    cols("g_ckv", a["mla_kv_norm_2"][0])
    cols("lb", a["lb_logits"][0])
    cols("w_bconv", a["b_conv_w"][0].reshape(-1))
    cols("g_sub", a["diff_subln_2"][0])
    cols("g_aq", _np.concatenate([a["a_q_g"][0]] * 2))
    cols("g_ak", _np.concatenate([a["a_k_g"][0]] * 2))
    cols("w_fconv", a["ffn_conv_w"][0].reshape(-1))
    cols("b_fconv", a["ffn_conv_b"][0])
    w_gate = _np.zeros((P, KD, 96), _np.float32)
    for row, at, n in ((0, OFF_AF, AH), (32, OFF_BI, BH), (64, OFF_BF, BH)):
        w_gate[:, :, row:row + n] = w_in[:, at:at + n].reshape(KD, P, n).transpose(1, 0, 2)
        par[row:row + n, PCOL["b_gate"][0]] = b_in[at:at + n]
    lam = _np.concatenate([a[f"diff_lambda_{v}_2"][0] for v in ("q1", "k1", "q2", "k2")])

    send = [("x", a["x"][0]), ("w_in", w_in), ("b_in", b_in), ("w_gate", w_gate), ("w_out", a["w_out"][0]),
            ("w_up", a["w_up"][0]), ("w_down", a["w_down"][0]), ("pos", a["positions_2"][0]), ("w_in2", a["w_in_2"][0]),
            ("lam", lam), ("w_uq", a["w_uq_2"][0]), ("w_ukv", a["w_ukv_2"][0]), ("w_pd", a["w_proj_diff_2"][0]),
            ("w_pm", a["w_proj_mla_2"][0]), ("w_out2", a["w_out_2"][0]), ("g_fin", a["norm_final_2"]), ("par", par),
            ("con", constant_table())]
    nc = _bacc.Bacc("TRN2", target_bir_lowering=False, num_devices=1, dynamic_dma_scratch_size=1024)
    arrays, args = {}, []
    for name, v in send:
        v = _np.ascontiguousarray(v)
        arrays[f"in_{name}"] = v
        args.append(nc.dram_tensor(f"in_{name}", v.shape, _mybir.dt.from_np(v.dtype), kind="ExternalInput").ap())
    args.append(nc.dram_tensor("out_0", (T, D), F32, kind="ExternalOutput").ap())
    two_blocks(nc, *args)
    r = _run(nc, [arrays], core_ids=[0])
    return r.results[0]["out_0"].reshape(1, T, D)
```

```python
from contextlib import ExitStack

import numpy as np

import concourse.bass as bass
from concourse import mybir

F32 = mybir.dt.float32
F32R = mybir.dt.float32r
BF16 = mybir.dt.bfloat16
I32 = mybir.dt.int32
ACT = mybir.ActivationFunctionType
ALU = mybir.AluOpType
AX = mybir.AxisListType

P = 128
T = 512
NB = T // P
D = 1024
KD = D // P
HD = 64
AH, BH, CH = 8, 4, 4
LC = 16
NC = T // LC
DFF = 2816
FT = DFF // P
FHALF = (12, FT - 12)
HSLOT = 14
EPS = 1e-6
NEG = -1e30
LAMBDA_INIT = 0.2
MLA_SCALE = 192.0 ** -0.5
SLOT = 2048
KIB = 1024

OFF_AQ, OFF_AK, OFF_AV, OFF_AF, OFF_BQK, OFF_BV, OFF_BI, OFF_BF, OFF_BO, OFF_CQ, OFF_CF, OFF_CI, OFF_CG, _ = (
    int(v) for v in np.cumsum([0, 512, 512, 512, 8, 512, 256, 4, 4, 256, 256, 256, 256, 256]))
OFF_DQ, OFF_DK, OFF_DV, OFF_DG, OFF_CQ2, OFF_CKV, OFF_KR, OFF_MG, OFF_GD, OFF_GM, _ = (
    int(v) for v in np.cumsum([0, 512, 512, 512, 512, 384, 256, 64, 512, 1024, 1024]))

PCOL = {}
for _name, _n in [("g_ffn", 8), ("g_in2", 8), ("g_out", 8), ("b_aq", 4), ("b_ak", 4), ("b_bqk", 4),
                  ("b_bo", 2), ("b_cq", 2), ("b_cf", 2), ("b_cg", 2), ("g_cq2", 3), ("g_ckv", 2), ("lb", 2),
                  ("w_bconv", 16), ("g_sub", 1), ("g_aq", 1), ("g_ak", 1), ("b_gate", 1), ("w_fconv", 132),
                  ("b_fconv", 44)]:
    PCOL[_name] = (sum(n for _, n in PCOL.values()), _n)
NPC = sum(n for _, n in PCOL.values())

CCOL = {}
for _name, _n in [("ident", 128), ("ones", 128), ("blk", 128), ("neg", 128), ("tri", 128), ("chunk", 128),
                  ("rep", 128), ("win", 96), ("inchunk", 8), ("sel", 8), ("eps", 1), ("freq", 1), ("sign", 1), ("halfpi", 1)]:
    CCOL[_name] = (sum(n for _, n in CCOL.values()), _n)
NCC = sum(n for _, n in CCOL.values())


def constant_table():
    t = np.zeros((P, NCC), np.float32)
    r, c = np.arange(P)[:, None], np.arange(P)[None, :]

    def put(name, value):
        at, n = CCOL[name]
        t[:value.shape[0], at:at + n] = value

    put("ident", np.float32(r == c))
    put("ones", np.ones((P, P), np.float32))
    put("blk", np.float32(r // HD == c // HD))
    put("neg", np.where(c > r, np.float32(NEG), np.float32(0)))
    put("tri", np.float32(r <= c))
    put("chunk", np.float32((r // LC == c // LC) & (r <= c)))
    put("rep", np.float32(np.arange(64)[:, None] % 32 == c % LC))
    put("win", np.float32(np.arange(96)[None, :] == LC - 1 + 32 * (r // HD)))
    put("inchunk", np.float32(r // LC == np.arange(8)[None, :]))
    put("sel", np.float32((r < 72) & (r % 32 == np.arange(8)[None, :])))
    put("eps", np.full((P, 1), EPS, np.float32))
    half = np.arange(0, 64, 2, dtype=np.float32)
    freq = np.float32(10000.0) ** (-half / np.float32(64))
    put("freq", np.tile(freq, 4)[:, None].astype(np.float32))
    put("sign", np.where(r % 64 < 32, np.float32(-1), np.float32(1)))
    put("halfpi", np.full((P, 1), np.pi / 2, np.float32))
    return t


def two_blocks(nc, x_d, w_in_d, b_in_d, w_gate_d, w_out_d, w_up_d, w_down_d, pos_d, w_in2_d, lam_d, w_uq_d, w_ukv_d,
               w_pd_d, w_pm_d, w_out2_d, g_mix_d, g_fin_d, par_d, con_d, out_d):
    ctx = ExitStack()
    with ctx:
        base = 1152

        def sb(name, shape, dt, kib):
            return nc.alloc_sbuf_tensor_at(name, shape, dt, offset=base + int(round(kib * KIB)))

        def sem(name):
            return ctx.enter_context(nc.semaphore(name))

        con_in, par_in, gmix_in, bias_in, lam_in, pos_in, xres_in, gfin_in = (
            sem(n) for n in ("con_in", "par_in", "gmix_in", "bias_in", "lam_in", "pos_in", "xres_in", "gfin_in"))
        hi_done, split_done = (sem(n) for n in ("hi_done", "split_done"))
        act_step, dve_step = (sem(n) for n in ("act_step", "dve_step"))
        x_in = [sem(f"x_in{b}") for b in range(NB)]
        x_rs, x_h, h_hi = (sem(n) for n in ("x_rs", "x_h", "h_hi"))
        lb_d, lb_e, nbcf_ready, mask_ready = (sem(n) for n in ("lb_d", "lb_e", "nbcf_ready", "mask_ready"))
        gate_ln, gate_m, gate_rows, gate_cols, gate_cols_out, negC_ready = (
            sem(n) for n in ("gate_ln", "gate_m", "gate_rows", "gate_cols", "gate_cols_out", "negC_ready"))
        hg_a, hg_a_used, hg_q, hg_att_s, hg_kdT_mm, hg_kdT_s = (
            sem(n) for n in ("hg_a", "hg_a_used", "hg_q", "hg_att_s", "hg_kdT_mm", "hg_kdT_s"))
        hg_vx, hg_u_mm, hg_u_s, hg_scan, hg_rep_mm, hg_dm, hg_o_mm, hg_n, hg_done = (
            sem(n) for n in ("hg_vx", "hg_u_mm", "hg_u_s", "hg_scan", "hg_rep_mm", "hg_dm", "hg_o_mm", "hg_n", "hg_done"))
        nrm_sq, nrm_mm, nrm_rs, nrm_done, qk_done = (sem(n) for n in ("nrm_sq", "nrm_mm", "nrm_rs", "nrm_done", "qk_done"))
        conv_b, qkB_ready, ml_m_mm, ml_w, ml_e, ml_s_mm, ml_p, ml_o_mm, ml_o_s = (
            sem(n) for n in ("conv_b", "qkB_ready", "ml_m_mm", "ml_w", "ml_e", "ml_s_mm", "ml_p", "ml_o_mm", "ml_o_s"))
        yb_var, yb_rs, yb_n = (sem(n) for n in ("yb_var", "yb_rs", "yb_n"))
        fox_s_mm, fox_m, fox_e, fox_t_mm, fox_pt, fox_v_mm, fox_o_free = (
            sem(n) for n in ("fox_s_mm", "fox_m", "fox_e", "fox_t_mm", "fox_pt", "fox_v_mm", "fox_o_free"))
        ya_var, ya_rs, ya_n, ya_hi, ys_hi, y_lo = (sem(n) for n in ("ya_var", "ya_rs", "ya_n", "ya_hi", "ys_hi", "y_lo"))
        n_sq, n_mm, n_rs, col_mm, n_hi, n_lo = (sem(n) for n in ("n_sq", "n_mm", "n_rs", "col_mm", "n_hi", "n_lo"))
        gate_on, gd_z, gm_z, gd_on, gm_on = (sem(n) for n in ("gate_on", "gd_z", "gm_z", "gd_on", "gm_on"))
        zp_zero, conv_g, conv_u, silu_ready, hidden, hid_hi, hid_lo = (
            sem(n) for n in ("zp_zero", "conv_g", "conv_u", "silu_ready", "hidden", "hid_hi", "hid_lo"))
        rot_ready, sin_ready, cos_ready, lam_s, lam_e, lam_done, rope_z, rope_done = (
            sem(n) for n in ("rot_ready", "sin_ready", "cos_ready", "lam_s", "lam_e", "lam_done", "rope_z", "rope_done"))
        dif_s_mm, dif_m, dif_e, dif_c, dif_t_mm, dif_pt, dif_v_mm, dif_o_free = (
            sem(n) for n in ("dif_s_mm", "dif_m", "dif_e", "dif_c", "dif_t_mm", "dif_pt", "dif_v_mm", "dif_o_free"))
        yd_var, yd_rs, yd_n = (sem(n) for n in ("yd_var", "yd_rs", "yd_n"))
        lat_sq, lat_mm, lat_rs, lat_t, lat_hi, lat_lo = (sem(n) for n in ("lat_sq", "lat_mm", "lat_rs", "lat_t", "lat_hi", "lat_lo"))
        mla_s_mm, mla_m, mla_e, mla_t_mm, mla_pt, mla_v_mm, mla_o_free, ym_n = (
            sem(n) for n in ("mla_s_mm", "mla_m", "mla_e", "mla_t_mm", "mla_pt", "mla_v_mm", "mla_o_free", "ym_n"))
        o_hi, o_lo = (sem(n) for n in ("o_hi", "o_lo"))
        gated_d, gated_m, merged, m_hi, m_lo = (sem(n) for n in ("gated_d", "gated_m", "merged", "m_hi", "m_lo"))
        ssf_ready, xo_g, f_var, f_rs, out_act, out_dve, out_done = (
            sem(n) for n in ("ssf_ready", "xo_g", "f_var", "f_rs", "out_act", "out_dve", "out_done"))
        raw_in = [sem(f"raw_in{i}") for i in range(2)]
        tile_done = sem("tile_done")
        ring_free = [sem(f"ring_free{i}") for i in range(2)]

        raw = [sb(f"w_raw{i}", [P, SLOT], F32, 8 * i) for i in range(2)]
        whi = [sb(f"w_hi{i}", [P, SLOT], F32R, 16 + 8 * i) for i in range(3)]
        wlo = [sb(f"w_lo{i}", [P, SLOT], F32R, 40 + 8 * i) for i in range(3)]
        hH = sb("act_hi", [P, KD, T], F32R, 64)
        hL = sb("act_lo", [P, KD, T], F32R, 80)
        con = sb("con", [P, NCC], F32, 96)
        par = sb("par", [P, NPC], F32, 100)
        small = sb("small", [P, 300], F32, 101.25)
        selb = sb("selb", [P, 8], BF16, 102.4375)
        identb = sb("identb", [P, P], BF16, 102.5)
        maskb = sb("maskb", [P, P], BF16, 102.75)
        M = 104
        xtok = sb("xtok", [P, NB, D], F32, M + 28)
        htok = sb("htok", [P, NB, D], F32, M + 44)
        gmix = sb("gmix", [P, D], F32, M)
        U = sb("U", [P, HD, NC], F32, M)
        Gx = sb("Gx", [P, HD // 2, NC], F32, M + 8)
        Ab = [sb(f"Ab{i}", [P, 2, T], F32, M + 12 + 4 * i) for i in range(2)]
        Vx = [sb(f"Vx{i}", [P, 8, HD], F32, M + 12 + 2 * i) for i in range(4)]
        kd = sb("kd", [P, 2, NC, LC], F32, M + 20)
        kdT = sb("kdT", [P, 2, NB, P], F32, M + 24)
        qT = sb("qT", [P, 4, T], F32, M + 28)
        kT = sb("kT", [P, 4, T], F32, M + 36)
        av = sb("av", [P, NB, T], F32, M + 44)
        bqk = sb("bqk", [P, 4, T + 3], F32, M + 52)
        qkB = sb("qkB", [P, 4, T], F32, M + 60.25)
        bv = sb("bv", [P, NB, BH, HD + 1], F32, M + 68.25)
        bo = sb("bo", [P, 2, T], F32, M + 72.5)
        cq = sb("cq", [P, 2, NC, LC + 1], F32, M + 76.5)
        cf = sb("cf", [P, 2, NC, LC], F32, M + 80.75)
        ck = sb("ck", [P, 2, NC, LC], F32, M + 84.75)
        ci = sb("ci", [P, NB, 256], F32, M + 88.75)
        cg = sb("cg", [P, 2, T], F32, M + 92.75)
        bias_t = sb("bias_t", [P, 1024], F32, M + 96.75)
        gz = sb("gz", [96, T], F32, M + 100.75)
        g1 = sb("g1", [96, T], F32, M + 102.75)
        g2 = sb("g2", [96, T], F32, M + 104.75)
        g3 = sb("g3", [96, T], F32, M + 106.75)
        negC = sb("negC", [8, T], F32, M + 108.75)
        negB = sb("negB", [P, T], BF16, M + 110.75)
        negT = sb("negT", [8, T], BF16, M + 111.75)
        scr = [sb(f"scr{i}", [P, T], F32, M + 113.75 + 2 * i) for i in range(2)]
        Dm = [sb(f"Dm{i}", [P, NB, P], F32, M + 80.75 + 2 * i) for i in range(2)]
        attS = sb("attS", [64, 2, T], F32, M + 84.75)
        PM = [sb(f"PM{i}", [P, 1280], F32, M + 5 * i) for i in range(2)]
        Oh = sb("Oh", [P, NB, HD + 1], F32, M + 12)
        onB = sb("onB", [P, NB, BH, HD], F32, M + 14)
        sqB = sb("sqB", [P, NB, BH, HD], F32, M + 18)
        Pf = [sb(f"Pf{i}", [P, T], F32, M + 52 + 2 * i) for i in range(2)]
        PTs = [sb(f"PTs{i}", [P, T], F32, M + 56 + 2 * i) for i in range(2)]
        on = sb("on", [P, AH, HD], F32, M + 60)
        sqA = sb("sqA", [P, AH, HD], F32, M + 62)
        yt = sb("yt", [P, 4, P], F32, M + 64)
        xT = sb("xT", [P, KD, T], F32, M)
        xres = sb("xres", [P, NB, D], F32, M + 76.5)
        sqn = [sb(f"sqn{i}", [P, T], F32, M + 16 + 2 * i) for i in range(2)]
        rsn = sb("rsn", [P, T], F32, M + 20)
        hidH = sb("hidH", [P, HSLOT, T], F32R, M + 26)
        hidL = sb("hidL", [P, HSLOT, T], F32R, M + 54)
        zp = [sb(f"zp{i}", [P, T + 2], F32, M + 82 + 2.25 * i) for i in range(4)]
        cvg = [sb(f"cvg{i}", [P, T], F32, M + 91 + 2 * i) for i in range(2)]
        cvu = [sb(f"cvu{i}", [P, T], F32, M + 95 + 2 * i) for i in range(2)]
        hid = [sb(f"hid{i}", [P, T], F32, M + 99 + 2 * i) for i in range(2)]
        cosT = sb("cosT", [P, T], F32, M + 104)
        sinT = sb("sinT", [P, T], F32, M + 106)
        posI = sb("posI", [P, T], I32, M + 108)
        angT = sb("angT", [P, T], F32, M + 110)
        rotT = sb("rotT", [P, T], F32, M + 112)
        dq = sb("dq", [P, 4, T], F32, M + 26)
        dk = sb("dk", [P, 4, T], F32, M + 34)
        dv = sb("dv", [P, NB, T], F32, M + 42)
        sdg = sb("sdg", [P, 4, T], F32, M + 50)
        oH = sb("oH", [P, KD, T], F32R, M + 58)
        oL = sb("oL", [P, KD, T], F32R, M + 74)
        yt2 = sb("yt2", [P, 4, P], F32, M + 90)
        PT2 = [sb(f"PT2{i}", [P, T], F32, M + 92 + 2 * i) for i in range(2)]
        kr = sb("kr", [P, T], F32, M + 96)
        cosR = sb("cosR", [P, T], F32, M + 98)
        sinR = sb("sinR", [P, T], F32, M + 100)
        P2 = [sb(f"P2{i}", [P, T], F32, M + 108 + 2 * i) for i in range(4)]
        rsl = sb("rsl", [P, T], F32, M + 98)
        zs = sqn
        on2 = sb("on2", [P, 4, P], F32, M + 22)
        sq2 = sb("sq2", [P, 4, P], F32, M + 24)
        qn = sb("qn", [P, 4, T], F32, M + 26)
        kn = sb("kn", [P, 4, T], F32, M + 34)
        mv = sb("mv", [P, NB, T], F32, M + 42)
        qr = sb("qr", [P, 2, T], F32, M + 50)
        Pm = [sb(f"Pm{i}", [P, T], F32, M + 54 + 2 * i) for i in range(2)]
        smg = sb("smg", [P, 4, T], F32, M + 108)
        latH = [sb(f"latH{i}", [P, T], F32R, M + (66, 68, 70, 72, 102)[i]) for i in range(5)]
        latS = [sb(f"latS{i}", [P, T], F32, M + (66, 68, 70, 72, 102)[i]) for i in range(5)]
        lat = [sb(f"lat{i}", [P, T], F32, M + (82, 84, 86, 88, 116)[i]) for i in range(5)]
        latL = [sb(f"latL{i}", [P, T], F32R, M + (82, 84, 86, 88, 116)[i]) for i in range(5)]
        mH = sb("mH", [P, KD, T], F32R, M + 26)
        mL = sb("mL", [P, KD, T], F32R, M + 42)
        sgd = [sb(f"sgd{i}", [P, T], F32, M + 92 + 2 * i) for i in range(2)]
        sgm = [sb(f"sgm{i}", [P, T], F32, M + 96 + 2 * i) for i in range(2)]
        mt = [sb(f"mt{i}", [P, T], F32, M + 100 + 2 * i) for i in range(2)]
        mt2 = [sb(f"mt2{i}", [P, T], F32, M + 108 + 2 * i) for i in range(2)]
        xo = sb("xo", [P, NB, D], F32, M + 58)
        gfin = sb("gfin", [P, D], F32, M + 74)
        lamv = sb("lamv", [P, 4, HD], F32, M + 117.75)
        assert M + 118.75 <= (nc.sbuf_usable_end - base) / KIB

        ring = [ctx.enter_context(nc.psum_tensor(f"ring{i}", [P, T], F32)) for i in range(2)]
        bank = [ctx.enter_context(nc.psum_tensor(f"bank{i}", [P, T], F32)) for i in range(6)]

        def cc(name, r=slice(0, P)):
            at, n = CCOL[name]
            return con[r, at:at + n]

        def pc(name, i=0, n=1, r=slice(0, P)):
            return par[r, PCOL[name][0] + i:PCOL[name][0] + i + n]

        ident = cc("ident")
        sm_at = [0]

        def sm(n):
            at = sm_at[0]
            sm_at[0] += n
            assert sm_at[0] <= 300
            return small[:, at:at + n]

        ss_x, var_x, rs_x = sm(4), sm(4), sm(4)
        rs_col = sm(4)
        lbd, lbe, lbr, lbp, lb, lb1 = (sm(2) for _ in range(6))
        nbcf = sm(2)
        gq8 = sm(1)
        colB = sm(32)
        denB, recB = sm(4), sm(4)
        msB, rsB = sm(16), sm(16)
        nmx = sm(4)
        rsum = sm(16)
        recA, msA, rsA = sm(8), sm(8), sm(8)
        rsum2, rec2, wgt2 = sm(16), sm(4), sm(2)
        ms2, rs2 = sm(4), sm(4)
        lams = sm(2)
        lame = sm(2)
        nlam = sm(1)
        gsub = sm(1)
        ssf = sm(16)
        sst, rsf = sm(4), sm(4)
        lamm = sb("lamm", [P, 2, HD], F32, M + 108)

        chunks = []
        chunk_of = {}

        def chunk(name, *areas):
            parts, at = [], 0
            for sources in areas:
                if not isinstance(sources, list):
                    sources = [sources]
                nk, n = sources[0].shape[1], sum(src.shape[2] for src in sources)
                parts.append((at, nk, n, sources))
                at += nk * n
            assert at <= SLOT
            chunk_of[name] = len(chunks)
            chunks.append((name, parts, at))

        tiles = []
        tile_at = {}
        last_use = {}

        def tile(name, of=None):
            tile_at[name] = len(tiles)
            tiles.append(name)
            if of is not None:
                last_use[chunk_of[of]] = len(tiles) - 1

        k_in = w_in_d.rearrange("(k p) n -> p k n", p=P)
        k_out = w_out_d.rearrange("(k p) n -> p k n", p=P)
        k_up = w_up_d.rearrange("(k p) n -> p k n", p=P)
        k_down = w_down_d.rearrange("(k p) n -> p k n", p=P)
        k_in2 = w_in2_d.rearrange("(k p) n -> p k n", p=P)
        k_uq = w_uq_d.rearrange("(k p) (h n) -> p k h n", p=P, h=4)
        k_ukv = w_ukv_d.rearrange("(k p) n -> p k n", p=P)
        k_pd = w_pd_d.rearrange("(k p) n -> p k n", p=P)
        k_pm = w_pm_d.rearrange("(k p) n -> p k n", p=P)
        k_out2 = w_out2_d.rearrange("(k p) n -> p k n", p=P)

        order = []

        def stage(*s):
            order.append(s)

        for b in range(NB + 1):
            if b < NB:
                stage("x_norm", b)
            if b >= 1:
                for half in range(2):
                    tile(("x", b - 1, half))
                    stage("x", b - 1, half)
        stage("params")

        def in_chunk(name, at):
            chunk(name, k_in[:, :, at:at + 256])

        in_chunk("c_f", OFF_CF)
        in_chunk("c_q", OFF_CQ)
        chunk("gates", w_gate_d)
        for i in range(2):
            in_chunk(f"b_qk{i}", OFF_BQK + 256 * i)
        in_chunk("c_g", OFF_CG)
        in_chunk("c_i", OFF_CI)
        in_chunk("b_v", OFF_BV)
        for kind, at in (("a_q", OFF_AQ), ("a_k", OFF_AK), ("a_v", OFF_AV)):
            for i in range(2):
                in_chunk(f"{kind}{i}", at + 256 * i)
        in_chunk("b_o", OFF_BO)

        def in_tile(kind, i, of):
            tile((kind, i), of)
            stage(kind, i)

        att = iter(range(LC - 1, -1, -1))
        in_tile("c_f", 0, "c_f")
        in_tile("c_f", 1, "c_f")
        in_tile("c_q", 0, "c_q")
        in_tile("c_q", 1, "c_q")
        stage("hg_begin")

        def attend(n):
            for _ in range(n):
                stage("hg_att", next(att))

        in_tile("gates", 0, "gates")
        attend(2)
        in_tile("b_qk", 0, "b_qk0")
        attend(3)
        in_tile("b_qk", 1, "b_qk0")
        attend(3)
        in_tile("b_qk", 2, "b_qk1")
        attend(3)
        in_tile("b_qk", 3, "b_qk1")
        attend(3)
        in_tile("c_g", 0, "c_g")
        attend(2)
        stage("gate_math")
        in_tile("c_g", 1, "c_g")
        stage("hg_att_out")
        stage("hg_kdT", 0)
        stage("hg_kdT", 1)
        in_tile("c_i", 0, "c_i")
        stage("gate_cols")
        stage("conv", 0)
        in_tile("c_i", 1, "c_i")

        def values(p, blocks):
            for b in blocks:
                stage("hg_u", p, b)

        def spread(p):
            for hh in range(2):
                stage("hg_rep", p, hh)

        values(0, (0, 1))
        spread(0)
        in_tile("b_v", 0, "b_v")
        values(0, (2, 3))
        stage("hg_scan", 0)
        in_tile("b_v", 1, "b_v")
        stage("conv", 1)
        stage("hg_o", 0)
        in_tile("a_q", 0, "a_q0")
        stage("hg_y", 0)
        values(1, (0, 1))
        in_tile("a_q", 1, "a_q0")
        values(1, (2, 3))
        spread(1)
        stage("hg_scan", 1)
        in_tile("a_q", 2, "a_q1")
        stage("conv", 2)
        stage("hg_o", 1)
        in_tile("a_q", 3, "a_q1")
        stage("hg_y", 1)
        stage("conv", 3)
        for i in range(8):
            kind, t = ("a_k", "a_v")[i // 4], i % 4
            in_tile(kind, t, f"{kind}{t // 2}")
            if i % 2 == 0:
                stage("ml", i // 2)
            else:
                stage("ml_o", i // 2)
            stage("qk_norm", i)
        stage("yb_norm")
        for half in range(2):
            chunk(f"wo_b{half}", k_out[:, 4:8, 512 * half:512 * half + 512])
        for half in range(2):
            chunk(f"wo_a{half}", k_out[:, 0:4, 512 * half:512 * half + 512])
        fill = [[("b_o", 0)], [("b_o", 1)], [("yb", 0), ("yb", 1)], [("y_split", i) for i in range(4)]]
        fill += [[("wo_b", j)] for j in range(KD)]
        fill_at = dict(zip((1, 4, 7, 8, 10, 13, 16, 19, 22, 25, 28), fill))
        fill_of = {"b_o": lambda j: "b_o", "yb": lambda j: None, "wo_b": lambda j: f"wo_b{j // 4}"}

        def fillers(group):
            for f in group:
                if f[0] in fill_of:
                    tile(f, fill_of[f[0]](f[1]))
                stage(*f)

        fox = [(qb, h) for qb in range(NB) for h in range(AH)]
        for u in range(len(fox)):
            if u == 0:
                stage("fox_s", 0)
            if u + 1 < len(fox):
                stage("fox_s", u + 1)
            fillers(fill_at.get(u, []))
            stage("fox_t", u)
            if u >= 1:
                stage("fox_v", u - 1)
            if u % AH == 2 and u > AH:
                tile(("ya", u // AH - 1))
                stage("ya", u // AH - 1)
        stage("fox_v", len(fox) - 1)
        fillers(fill[-1])
        tile(("ya", NB - 1))
        stage("ya", NB - 1)

        def sums(i, j):
            stage("n_sum", i, j)

        for j in range(KD):
            tile(("wo_a", j), f"wo_a{j // 4}")
            stage("wo_a", j)
            if j >= 1:
                sums(0, j - 1)
            stage("n_sq", 0, j)
            if j < KD // 2:
                stage("n_split", 0, j)
        for j in range(KD // 2, KD):
            stage("n_split", 0, j)

        def up_pair(c):
            for kind, at in (("gate", 0), ("up", DFF)):
                chunk(f"{kind}{c}", k_up[:, :, at + 256 * c:at + 256 * c + 256])
                for i in (2 * c, 2 * c + 1):
                    tile((kind, i), f"{kind}{c}")
                    stage(kind, i)
                    if (kind, i) == ("gate", 0):
                        sums(0, KD - 1)

        def down_half(half):
            k0, nk = half * FHALF[0], FHALF[half]
            for j in range(KD):
                chunk(f"down{half}{j}", k_down[:, k0:k0 + nk, P * j:P * j + P])
                tile(("down", half, j), f"down{half}{j}")
                stage("down", half, j)
                if half == 1:
                    if j >= 1:
                        sums(1, j - 1)
                    stage("n_sq", 1, j)
                    stage("n_split", 1, j)

        for c in range(FT // 2):
            up_pair(c)
            if 2 * c == FHALF[0]:
                down_half(0)
        stage("hid_flush")
        stage("rope_tables")
        down_half(1)
        def in2_chunk(name, *areas):
            chunk(name, *[[k_in2[:, :, at:at + n] for at, n in area] for area in areas])

        for kind, at in (("dq", OFF_DQ), ("dk", OFF_DK), ("dv", OFF_DV)):
            for c in range(2):
                in2_chunk(f"{kind}{c}", [(at + 256 * c, 256)])
            for i in range(4):
                in_tile(kind, i, f"{kind}{i // 2}")
                if (kind, i) == ("dq", 0):
                    sums(1, KD - 1)
                if (kind, i) == ("dk", 3):
                    stage("rs_col")
        for c in range(2):
            in2_chunk(f"dg{c}", [(OFF_DG + 256 * c, 256)])
        in2_chunk("cq0", [(OFF_CQ2, 256)])
        in2_chunk("cq1", [(OFF_CQ2 + 256, P)], [(OFF_KR, 64)] * 2)
        in2_chunk("ckv", [(OFF_CKV, 256)])
        dif = [(qb, h) for qb in range(NB) for h in range(4)]

        def attention(name, units, tag, fill_at):
            for u in range(len(units)):
                if u == 0:
                    stage(name + "_s", 0)
                if u + 1 < len(units):
                    stage(name + "_s", u + 1)
                for f in fill_at.get(u, []):
                    if f[0] == "lat_norm":
                        tile(f)
                        stage(*f)
                    else:
                        in_tile(*f)
                stage(name + "_t", u)
                if u >= 1:
                    stage(name + "_v", u - 1)
                if u % 4 == 2 and u > 4:
                    tile((tag, u // 4 - 1))
                    stage(tag, u // 4 - 1)
            stage(name + "_v", len(units) - 1)
            tile((tag, NB - 1))
            stage(tag, NB - 1)

        lats = [("lat", i, ("cq0", "cq0", "cq1", "ckv", "ckv")[i]) for i in range(5)]
        attention("dif", dif, "yd", {
            0: [("dg", 0, "dg0")], 1: [("dg", 1, "dg0")], 3: [("dg", 2, "dg1")], 4: [("dg", 3, "dg1")], 6: lats[0:1], 8: lats[1:2],
            9: lats[2:3], 11: [("kr", 0, "cq1")], 12: [("lat_norm", 0)], 13: lats[3:4], 14: lats[4:5], 15: [("lat_norm", 1)]})
        chunk("uqn", *[k_uq[:, :, h, 0:128] for h in range(4)])
        chunk("uqr", [k_uq[:, :, h, 128:192] for h in range(4)])
        chunk("ukv", k_ukv)
        for i in range(4):
            in_tile("qn", i, "uqn")
        for i in range(2):
            in_tile("qr", i, "uqr")
        for i in range(4):
            in_tile("kn", i, "ukv")
        for i in range(4):
            in_tile("mv", i, "ukv")
        for c in range(2):
            in2_chunk(f"mg{c}", [(OFF_MG + 256 * c, 256)])
        mla = [(qb, h) for qb in range(NB) for h in range(4)]
        attention("mla", mla, "ym", {u: [("mg", i, f"mg{i // 2}")] for i, u in enumerate((0, 1, 3, 4))})
        for c in range(4):
            chunk(f"gd{c}", k_in2[:, :, OFF_GD + 256 * c:OFF_GD + 256 * c + 256])
            chunk(f"gm{c}", k_in2[:, :, OFF_GM + 256 * c:OFF_GM + 256 * c + 256])
            chunk(f"pj{c}", k_pd[:, :, 256 * c:256 * c + 256], k_pm[:, :, 256 * c:256 * c + 256])
            for kind, of in (("gd", f"gd{c}"), ("gm", f"gm{c}"), ("pd", f"pj{c}"), ("pm", f"pj{c}")):
                for i in (2 * c, 2 * c + 1):
                    tile((kind, i), of)
                    stage(kind, i)
        stage("m_flush")
        for c in range(4):
            chunk(f"w_out2{c}", k_out2[:, :, 256 * c:256 * c + 256])
            for i in range(2):
                tile(("out", c, i), f"w_out2{c}")
                stage("out", c, i)
        stage("final")

        def upto(name):
            return tile_at[name] + 1

        def bank_free(name):
            return ring_free[tile_at[name] % 2]

        def drains(name):
            return tile_at[name] // 2 + 1

        def at_ring(name):
            return ring[tile_at[name] % 2]

        def v3(ap, b):
            return ap.rearrange("p (a b) -> p a b", b=b)

        def nslot(i, j):
            return (j + KD // 2) % KD if i == 0 else j

        def score(b):
            return (bank[1][:, 0:T], bank[2][:, 0:T - P], bank[5][:, 0:T - 2 * P], bank[2][:, T - P:T])[b]

        HG = {("u", p, b): p * NB + b for p in range(2) for b in range(NB)}

        block = ctx.enter_context(nc.Block())

        @block.sync
        def _(sp):
            x_b = x_d.rearrange("(b p) d -> p b d", p=P)
            for b in range(NB):
                sp.dma_start(xtok[:, b, :], x_b[:, b, :]).then_inc(x_in[b], 16)
                if b == 0:
                    sp.dma_start(con[:], con_d).then_inc(con_in, 16)
                    sp.dma_start(gmix[:], g_mix_d.partition_broadcast(P)).then_inc(gmix_in, 16)
            sp.dma_start(par[:], par_d).then_inc(par_in, 16)
            for c, (name, parts, n) in enumerate(chunks):
                if name == "wo_b0":
                    sp.wait_ge(hg_done, 2)
                    sp.dma_start(xres[:], x_b).then_inc(xres_in, 16)
                if c >= 2:
                    sp.wait_ge(split_done, c - 1)
                for at, nk, w, sources in parts:
                    dst = raw[c % 2][:, at:at + nk * w].rearrange("p (k n) -> p k n", k=nk)
                    col = 0
                    for src in sources:
                        sp.dma_start(dst[:, :, col:col + src.shape[2]], src).then_inc(raw_in[c % 2], 16)
                        col += src.shape[2]
                if c == 0:
                    for i, (at, w) in enumerate(((OFF_AV, 512), (OFF_BV, 256), (OFF_CI, 256))):
                        to = (0, 512, 768)[i]
                        sp.dma_start(bias_t[:, to:to + w], b_in_d[at:at + w].partition_broadcast(P)).then_inc(bias_in, 16)
                    sp.dma_start(lamv[:].rearrange("p a b -> p (a b)"), lam_d.partition_broadcast(P)).then_inc(lam_in, 16)
                if name == f"down0{KD - 1}":
                    sp.dma_start(posI[:], pos_d.partition_broadcast(P)).then_inc(pos_in, 16)
            sp.wait_ge(tile_done, upto(("pm", KD - 1)))
            sp.dma_start(gfin[:], g_fin_d.partition_broadcast(P)).then_inc(gfin_in, 16)
            for b in (0, 2, 1, 3):
                sp.wait_ge(out_act if b < 2 else out_dve, b % 2 + 1)
                sp.dma_start(out_d.rearrange("(b p) d -> p b d", p=P)[:, b, :], xo[:, b, :]).then_inc(out_done, 16)
            sp.wait_ge(out_done, 16 * NB)

        @block.gpsimd
        def _(pool):
            landed = [0, 0]
            for c, (name, parts, n) in enumerate(chunks):
                landed[c % 2] += 16 * sum(len(sources) for _, _, _, sources in parts)
                pool.wait_ge(raw_in[c % 2], landed[c % 2])
                if c >= 3:
                    pool.wait_ge(tile_done, last_use[c - 3] + 1)
                pool.tensor_scalar(whi[c % 3][:, 0:n], raw[c % 2][:, 0:n], 1.0, 0.0, ALU.mult, ALU.add).then_inc(hi_done, 1)
                pool.wait_ge(hi_done, c + 1)
                pool.tensor_tensor(wlo[c % 3][:, 0:n], raw[c % 2][:, 0:n], whi[c % 3][:, 0:n].bitcast(F32),
                                   ALU.subtract).then_inc(split_done, 1)

        @block.tensor
        def _(pe):
            def weights(of, part=0):
                c = chunk_of[of]
                at, nk, n, _ = chunks[c][1][part]
                pe.wait_ge(split_done, c + 1)
                return [w[c % 3][:, at:at + nk * n].rearrange("p (k n) -> p k n", k=nk) for w in (whi, wlo)]

            def product(out, pairs, last=True, before=None):
                for n, ((ah, al), (bh, bl)) in enumerate(pairs):
                    if before is not None:
                        before(n)
                    pe.matmul(out, ah, bh, start=(n == 0), stop=False)
                    pe.matmul(out, ah, bl, start=False, stop=False)
                    mm = pe.matmul(out, al, bh, start=False, stop=(last and n == len(pairs) - 1))
                return mm

            def open_bank(name):
                n = tile_at[name]
                if n >= 2:
                    pe.wait_ge(ring_free[n % 2], n // 2)
                return ring[n % 2]

            def channels(name, of, col, acts, nk=KD, part=0, before=None, turn=0):
                out = open_bank(name)
                wh, wl = weights(of, part)
                ah, al = acts
                pairs = [((wh[:, k, col:col + P], wl[:, k, col:col + P]), (ah[:, (k + turn) % KD, :], al[:, (k + turn) % KD, :]))
                         for k in range(nk)]
                product(out[:], pairs, before=before).then_inc(tile_done, 1)

            def tokens(name, of, i, acts):
                out = open_bank(name)
                wh, wl = weights(of)
                ah, al = acts
                for s in range(2):
                    b = 2 * i + s
                    pairs = [((ah[:, k, b * P:b * P + P], al[:, k, b * P:b * P + P]), (wh[:, k, :], wl[:, k, :])) for k in range(KD)]
                    mm = product(out[:, 256 * s:256 * s + 256], pairs)
                mm.then_inc(tile_done, 1)

            act = (hH, hL)
            for s in order:
                kind = s[0]
                if kind == "x":
                    b, half = s[1:]
                    pe.wait_ge(con_in, 16)
                    pe.wait_ge(x_h, b + 1)
                    out = open_bank(s)
                    for j in range(4):
                        mm = pe.transpose(out[:, j * P:j * P + P], htok[:, b, (4 * half + j) * P:(4 * half + j + 1) * P], ident)
                    mm.then_inc(tile_done, 1)
                elif kind in ("c_f", "c_q", "c_g", "b_o", "gates"):
                    if s == ("c_f", 0):
                        for half in range(2):
                            pe.wait_ge(bank_free(("x", NB - 1, half)), drains(("x", NB - 1, half)))
                    channels((kind, s[1]), kind, P * s[1], act)
                elif kind in ("b_qk", "a_q", "a_k"):
                    channels((kind, s[1]), f"{kind}{s[1] // 2}", P * (s[1] % 2), act)
                elif kind in ("c_i", "b_v"):
                    tokens((kind, s[1]), kind, s[1], act)
                elif kind == "a_v":
                    tokens((kind, s[1]), f"a_v{s[1] // 2}", s[1] % 2, act)
                elif kind == "gate_cols":
                    pe.wait_ge(gate_rows, 2)
                    for n, src in enumerate((g1, g3)):
                        for b in range(NB):
                            mm = pe.transpose(bank[2][:, 16 * n + 4 * b:16 * n + 4 * b + 4], src[32:36, b * P:b * P + P],
                                              con[32:36, 32:36])
                    mm.then_inc(gate_cols, 1)
                elif kind == "hg_att":
                    j = s[1]
                    n = LC - 1 - j
                    pe.wait_ge(hg_a, n + 1)
                    first = 0 if n == 0 else j
                    row = CCOL["win"][0] + LC - 1 - j
                    for p in range(2):
                        mm = pe.matmul(v3(bank[p][0:64, :], LC)[:, :, first:], con[:, row:row + 64],
                                       v3(Ab[n % 2][:, p, :], LC)[:, :, first:], start=(n == 0), stop=(n == LC - 1))
                    mm.then_inc(hg_a_used, 1)
                elif kind == "hg_kdT":
                    p = s[1]
                    pe.wait_ge(hg_q, 1)
                    for b in range(NB):
                        mm = pe.transpose(bank[4 + p][:, b * P:b * P + P], kd[:, p, 8 * b:8 * b + 8, :], ident)
                    mm.then_inc(hg_kdT_mm, 1)
                elif kind == "hg_rep":
                    p, hh = s[1:]
                    n = 2 * p + hh
                    pe.wait_ge(hg_att_s, 2)
                    if n == 0:
                        pe.wait_ge(gate_cols_out, 1)
                    if n >= 2:
                        pe.wait_ge(hg_dm, n - 1)
                    pe.matmul(bank[2 + hh][:], cc("rep", slice(32 * hh, 32 * hh + LC)), attS[32 * hh:32 * hh + LC, p, :],
                              start=True, stop=True).then_inc(hg_rep_mm, 1)
                elif kind == "hg_u":
                    p, b = s[1:]
                    n = HG["u", p, b]
                    pe.wait_ge(hg_kdT_s, 2)
                    pe.wait_ge(hg_vx, n + 1)
                    if n >= 2:
                        pe.wait_ge(hg_u_s, n - 1)
                    for hh in range(2):
                        mm = pe.matmul(bank[4 + n % 2][64 * hh:64 * hh + 64, :], kdT[:, p, b, 64 * hh:64 * hh + 64],
                                       Vx[2 * (n % 2) + hh][:], start=True, stop=True)
                    mm.then_inc(hg_u_mm, 1)
                elif kind == "hg_o":
                    p = s[1]
                    pe.wait_ge(hg_scan, p + 1)
                    pe.wait_ge(hg_dm, 2 * p + 2)
                    for hh in range(2):
                        r = slice(64 * hh, 64 * hh + 64)
                        for b in range(NB):
                            pe.matmul(bank[p][r, b * P:b * P + P], ci[:, b, (2 * p + hh) * HD:(2 * p + hh + 1) * HD],
                                      Dm[hh][:, b, :], start=True, stop=False)
                            for c in range(max(8 * b, 1), 8 * b + 8):
                                mm = pe.matmul(bank[p][r, c * LC:c * LC + LC], U[r, :, c - 1], cq[r, p, c, 0:LC],
                                               start=False, stop=(c == 8 * b + 7))
                    mm.then_inc(hg_o_mm, 1)
                elif kind in ("hg_y", "qk_norm"):
                    n = s[1] + (2 if kind == "qk_norm" else 0)
                    pe.wait_ge(nrm_sq, n + 1)
                    if n <= 1:
                        pe.wait_ge(hg_u_s, NB * (n + 1))
                    if n >= 1:
                        pe.wait_ge(nrm_rs, n)
                    pe.matmul(bank[4][:], cc("blk"), scr[n % 2][:], start=True, stop=True).then_inc(nrm_mm, 1)
                elif kind == "ml":
                    h = s[1]
                    r = slice(64 * (h % 2), 64 * (h % 2) + 64)
                    if h == 0:
                        pe.wait_ge(hg_done, 2)
                        pe.wait_ge(hg_dm, 4)
                        pe.wait_ge(hg_u_s, 2 * NB)
                        pe.wait_ge(qkB_ready, 4)
                        pe.wait_ge(gate_rows, 2)
                    if h >= 1:
                        pe.wait_ge(ml_w, 4 * h)
                    pe.matmul(bank[0][:], con[32:36, 32 + h:33 + h].broadcast_to([4, P]), g2[32:36, :],
                              start=True, stop=True).then_inc(ml_m_mm, 1)
                    for b in range(NB):
                        if h >= 1:
                            pe.wait_ge(ml_p, 4 * h)
                        pe.matmul(score(b), qkB[r, 2 + h // 2, b * P:b * P + P], qkB[r, h // 2, b * P:T],
                                  start=True, stop=True).then_inc(ml_s_mm, 1)
                elif kind == "ml_o":
                    h = s[1]
                    pe.wait_ge(ml_p, 4 * h + 4)
                    if h >= 1:
                        pe.wait_ge(ml_o_s, h)
                    for tb in range(NB):
                        for b in range(tb + 1):
                            at = (0, 512, 896, 1152)[b] + (tb - b) * P
                            mm = pe.matmul(bank[3][:, 65 * tb:65 * tb + 65], PM[h % 2][:, at:at + P], bv[:, b, h, :],
                                           start=(b == 0), stop=(b == tb))
                    mm.then_inc(ml_o_mm, 1)
                elif kind == "yb":
                    p = s[1]
                    out = open_bank(("yb", p))
                    pe.wait_ge(yb_n, 1)
                    for b in range(NB):
                        mm = pe.transpose(out[:, b * P:b * P + P], onB[:, b, 2 * p:2 * p + 2, :], ident)
                    mm.then_inc(tile_done, 1)
                elif kind == "fox_s":
                    u = s[1]
                    qb, h = fox[u]
                    n = (qb + 1) * P
                    r = slice(64 * (h % 2), 64 * (h % 2) + 64)
                    if u == 0:
                        pe.wait_ge(qk_done, 8)
                        pe.wait_ge(negC_ready, 3)
                        pe.wait_ge(bank_free(("a_v", 2)), drains(("a_v", 2)))
                        pe.wait_ge(bank_free(("a_v", 3)), drains(("a_v", 3)))
                        pe.wait_ge(mask_ready, 3)
                        pe.wait_ge(ml_p, 16)
                        pe.wait_ge(ml_o_s, 4)
                    if u >= 2:
                        pe.wait_ge(fox_e, u - 1)
                    out = bank[u % 2]
                    pe.matmul(out[:, 0:n], qT[r, h // 2, qb * P:qb * P + P], kT[r, h // 2, 0:n], start=True, stop=False)
                    pe.matmul(out[:, 0:n], selb[:, h:h + 1].broadcast_to([P, P]), negB[:, 0:n], start=False, stop=False)
                    pe.matmul(out[:, qb * P:n], identb[:], maskb[:], start=False, stop=True).then_inc(fox_s_mm, 1)
                elif kind == "fox_t":
                    u = s[1]
                    qb, h = fox[u]
                    pe.wait_ge(fox_e, u + 1)
                    if u >= 2:
                        pe.wait_ge(fox_pt, u - 1)
                    for b in range(qb + 1):
                        mm = pe.transpose(bank[2 + u % 2][:, b * P:b * P + P], Pf[u % 2][:, b * P:b * P + P], ident)
                    mm.then_inc(fox_t_mm, 1)
                elif kind == "fox_v":
                    u = s[1]
                    qb, h = fox[u]
                    pe.wait_ge(fox_pt, u + 1)
                    if u == 0:
                        pe.wait_ge(nrm_rs, 10)
                    if h == 0:
                        if qb >= 2:
                            pe.wait_ge(fox_o_free, qb - 1)
                    for b in range(qb + 1):
                        mm = pe.matmul(bank[4 + qb % 2][:, HD * h:HD * h + HD], PTs[u % 2][:, b * P:b * P + P],
                                       av[:, b, HD * h:HD * h + HD], start=(b == 0), stop=(b == qb))
                    mm.then_inc(fox_v_mm, 1)
                elif kind == "ya":
                    qb = s[1]
                    out = open_bank(("ya", qb))
                    pe.wait_ge(ya_n, qb + 1)
                    for j in range(4):
                        mm = pe.transpose(out[:, j * P:j * P + P], on[:, 2 * j:2 * j + 2, :], ident)
                    mm.then_inc(tile_done, 1)
                elif kind == "wo_b":
                    j = s[1]
                    if j == 0:
                        pe.wait_ge(y_lo, 4)
                        pe.wait_ge(xres_in, 16)
                    out = open_bank(s)
                    wh, wl = weights(f"wo_b{j // 4}")
                    col = P * (j % 4)
                    product(out[:], [((wh[:, k, col:col + P], wl[:, k, col:col + P]), (hH[:, 4 + k, :], hL[:, 4 + k, :])) for k in range(4)],
                            last=False)
                    for b in range(NB):
                        mm = pe.matmul(out[:, b * P:b * P + P], xres[:, b, j * P:j * P + P], ident, start=False, stop=(b == NB - 1))
                    mm.then_inc(tile_done, 1)
                elif kind == "wo_a":
                    j = s[1]
                    if j == 0:
                        pe.wait_ge(y_lo, 4 + NB)
                    channels(s, f"wo_a{j // 4}", P * (j % 4), act, nk=4)
                elif kind == "n_sum":
                    i, j = s[1:]
                    pe.wait_ge(n_sq, KD * i + j + 1)
                    if j == 0 and i == 0:
                        pe.wait_ge(fox_e, len(fox))
                    elif j == 0:
                        pe.wait_ge(n_rs, 1)
                    pe.matmul(bank[0][:], cc("ones"), sqn[j % 2][:], start=(j == 0), stop=(j == KD - 1)).then_inc(n_mm, 1)
                elif kind == "rs_col":
                    pe.wait_ge(n_rs, 2)
                    for b in range(NB):
                        mm = pe.matmul(bank[5][:, b:b + 1], rsn[:, b * P:b * P + P], con[:, 0:1], start=True, stop=True)
                    mm.then_inc(col_mm, 1)
                elif kind in ("gate", "up"):
                    def first(k):
                        pe.wait_ge(n_lo, k + 1)
                    channels(s, f"{kind}{s[1] // 2}", P * (s[1] % 2), act, before=first if s == ("gate", 0) else None, turn=KD // 2)
                elif kind == "down":
                    half, j = s[1:]
                    k0, nk = half * FHALF[0], FHALF[half]
                    pe.wait_ge(hid_lo, k0 + nk)
                    out = open_bank(s)
                    wh, wl = weights(f"down{half}{j}")
                    product(out[:], [((wh[:, k, :], wl[:, k, :]), (hidH[:, (k0 + k) % HSLOT, :], hidL[:, (k0 + k) % HSLOT, :]))
                                     for k in range(nk)]).then_inc(tile_done, 1)
                elif kind in ("dq", "dk", "dg", "mg", "gd", "gm"):
                    def first(k):
                        pe.wait_ge(n_lo, KD + k + 1)
                    channels(s, f"{kind}{s[1] // 2}", P * (s[1] % 2), act, before=first if s == ("dq", 0) else None)
                elif kind == "dv":
                    tokens(s, f"dv{s[1] // 2}", s[1] % 2, act)
                elif kind == "lat":
                    i = s[1]
                    channels(s, ("cq0", "cq0", "cq1", "ckv", "ckv")[i], (0, P, 0, 0, P)[i], act)
                elif kind == "kr":
                    channels(s, "cq1", 0, act, part=1)
                elif kind == "lat_norm":
                    which = ((0, 1, 2), (3, 4))[s[1]]
                    out = open_bank(s)
                    pe.wait_ge(lat_sq, which[-1] + 1)
                    for n in which:
                        mm = pe.matmul(out[:], cc("ones"), latS[n][:], start=(n == which[0]), stop=(n == which[-1]))
                    mm.then_inc(tile_done, 1)
                elif kind in ("qn", "qr", "kn"):
                    i = s[1]
                    if kind == "qn" and i == 0:
                        pe.wait_ge(lat_lo, 5)
                    out = open_bank(s)
                    if kind == "qn":
                        wh, wl = weights("uqn", i)
                        st = [(wh[:, k, :], wl[:, k, :]) for k in range(3)]
                    elif kind == "qr":
                        wh, wl = weights("uqr")
                        st = [(wh[:, k, P * i:P * i + P], wl[:, k, P * i:P * i + P]) for k in range(3)]
                    else:
                        wh, wl = weights("ukv")
                        st = [(wh[:, k, 256 * i:256 * i + P], wl[:, k, 256 * i:256 * i + P]) for k in range(2)]
                    first = 3 if kind == "kn" else 0
                    product(out[:], [(w, (latH[first + k][:], latL[first + k][:])) for k, w in enumerate(st)]).then_inc(tile_done, 1)
                elif kind == "mv":
                    b = s[1]
                    out = open_bank(s)
                    wh, wl = weights("ukv")
                    of = [w.rearrange("p k (h n) -> p k h n", h=4) for w in (wh, wl)]
                    t = slice(b * P, b * P + P)
                    product(v3(out[:], P), [((latH[3 + k][:, t], latL[3 + k][:, t]), (of[0][:, k, :, P:256], of[1][:, k, :, P:256]))
                                     for k in range(2)]).then_inc(tile_done, 1)
                elif kind == "dif_s":
                    u = s[1]
                    qb, h = dif[u]
                    n = (qb + 1) * P
                    if u == 0:
                        pe.wait_ge(rope_done, 8)
                        pe.wait_ge(n_rs, 2)
                    for m in range(2):
                        r = slice(64 * m, 64 * m + 64)
                        if 2 * u + m - 1 > 0:
                            pe.wait_ge(dif_e, 2 * u + m - 1)
                        pe.matmul(bank[m][:, 0:n], dq[r, h, qb * P:qb * P + P], dk[r, h, 0:n], start=True, stop=False)
                        pe.matmul(bank[m][:, qb * P:n], identb[:], maskb[:], start=False, stop=True).then_inc(dif_s_mm, 1)
                elif kind == "dif_t":
                    u = s[1]
                    qb, h = dif[u]
                    pe.wait_ge(dif_c, u + 1)
                    if u >= 2:
                        pe.wait_ge(dif_pt, u - 1)
                    for b in range(qb + 1):
                        mm = pe.transpose(bank[2 + u % 2][:, b * P:b * P + P], P2[2 * (u % 2)][:, b * P:b * P + P], ident)
                    mm.then_inc(dif_t_mm, 1)
                elif kind in ("dif_v", "mla_v"):
                    u = s[1]
                    qb, h = dif[u]
                    name = kind[:3]
                    vals = dv if name == "dif" else mv
                    pt, o_free, v_mm = (dif_pt, dif_o_free, dif_v_mm) if name == "dif" else (mla_pt, mla_o_free, mla_v_mm)
                    pe.wait_ge(pt, u + 1)
                    if h == 0:
                        if qb >= 2:
                            pe.wait_ge(o_free, qb - 1)
                    if u == 0 and name == "dif":
                        pe.wait_ge(bank_free(("dv", 3)), drains(("dv", 3)))
                    for b in range(qb + 1):
                        mm = pe.matmul(bank[4 + qb % 2][:, P * h:P * h + P], PT2[u % 2][:, b * P:b * P + P],
                                       vals[:, b, P * h:P * h + P], start=(b == 0), stop=(b == qb))
                    mm.then_inc(v_mm, 1)
                elif kind in ("yd", "ym"):
                    qb = s[1]
                    out = open_bank(s)
                    pe.wait_ge((yd_n if kind == "yd" else ym_n), qb + 1)
                    for h in range(4):
                        mm = pe.transpose(out[:, h * P:h * P + P], on2[:, h, :], ident)
                    mm.then_inc(tile_done, 1)
                elif kind == "mla_s":
                    u = s[1]
                    qb, h = mla[u]
                    n = (qb + 1) * P
                    r = slice(64 * (h % 2), 64 * (h % 2) + 64)
                    if u == 0:
                        for b in range(2, 4):
                            pe.wait_ge(bank_free(("mv", b)), drains(("mv", b)))
                        pe.wait_ge(rope_done, 11)
                    if u >= 2:
                        pe.wait_ge(mla_e, u - 1)
                    out = bank[u % 2]
                    pe.matmul(out[:, 0:n], qn[:, h, qb * P:qb * P + P], kn[:, h, 0:n], start=True, stop=False)
                    pe.matmul(out[:, 0:n], qr[r, h // 2, qb * P:qb * P + P], kr[r, 0:n], start=False, stop=False)
                    pe.matmul(out[:, qb * P:n], identb[:], maskb[:], start=False, stop=True).then_inc(mla_s_mm, 1)
                elif kind == "mla_t":
                    u = s[1]
                    qb, h = mla[u]
                    pe.wait_ge(mla_e, u + 1)
                    if u >= 2:
                        pe.wait_ge(mla_pt, u - 1)
                    for b in range(qb + 1):
                        mm = pe.transpose(bank[2 + u % 2][:, b * P:b * P + P], Pm[u % 2][:, b * P:b * P + P], ident)
                    mm.then_inc(mla_t_mm, 1)
                elif kind in ("pd", "pm"):
                    i = s[1]
                    if s == ("pd", 0):
                        pe.wait_ge(o_lo, 2 * NB)
                    at = 0 if kind == "pd" else 4
                    channels(s, f"pj{i // 2}", P * (i % 2), (oH[:, at:at + 4, :], oL[:, at:at + 4, :]), nk=4, part=0 if kind == "pd" else 1)
                elif kind == "out":
                    c, i = s[1:]
                    out = open_bank(s)
                    wh, wl = weights(f"w_out2{c}")
                    if c == 0 and i == 0:
                        pe.wait_ge(m_lo, KD)
                    for e in range(2):
                        b = 2 * i + e
                        t = slice(b * P, b * P + P)
                        to = out[:, 256 * e:256 * e + 256]
                        product(to, [((mH[:, k, t], mL[:, k, t]), (wh[:, k, :], wl[:, k, :])) for k in range(KD)], last=False)
                        for j in range(2):
                            mm = pe.matmul(out[:, 256 * e + P * j:256 * e + P * j + P], xT[:, 2 * c + j, t], ident, start=False, stop=(j == 1))
                    mm.then_inc(tile_done, 1)

        @block.scalar
        def _(act):
            steps = [0]

            def step():
                steps[0] += 1
                return steps[0]

            A = act.activation
            for s in order:
                kind = s[0]
                if kind == "x_norm":
                    b = s[1]
                    act.wait_ge(x_in[b], 16)
                    A(htok[:, b, :], xtok[:, b, :], ACT.Square, accum_out=ss_x[:, b:b + 1]).then_inc(act_step, 1)
                    act.wait_ge(act_step, step())
                    act.wait_ge(con_in, 16)
                    A(var_x[:, b:b + 1], ss_x[:, b:b + 1], ACT.Ln, bias=cc("eps"), scale=1.0 / D).then_inc(act_step, 1)
                    act.wait_ge(act_step, step())
                    A(rs_x[:, b:b + 1], var_x[:, b:b + 1], ACT.Exp, scale=-0.5).then_inc(x_rs, 1)
                elif kind == "x":
                    b, half = s[1:]
                    act.wait_ge(tile_done, upto(s))
                    A(hH[:, 4 * half:4 * half + 4, b * P:b * P + P], v3(at_ring(s)[:], P), ACT.Identity).then_inc(h_hi, 1)
                elif kind == "params":
                    act.wait_ge(par_in, 16)
                    act.wait_ge(lb_d, 1)
                    A(lbe, lbd, ACT.Exp).then_inc(lb_e, 1)
                elif kind == "c_f":
                    p = s[1]
                    act.wait_ge(nbcf_ready, 1)
                    act.wait_ge(tile_done, upto(s))
                    A(cf[:, p].rearrange("p c t -> p (c t)"), at_ring(s)[:], ACT.Sigmoid, bias=pc("b_cf", p))
                    A(ck[:, p].rearrange("p c t -> p (c t)"), at_ring(s)[:], ACT.Sigmoid, bias=nbcf[:, p:p + 1], scale=-1.0).then_inc(bank_free(s), 1)
                elif kind == "c_q":
                    p = s[1]
                    act.wait_ge(tile_done, upto(s))
                    A(cq[:, p, :, 0:LC], v3(at_ring(s)[:], LC), ACT.Silu, bias=pc("b_cq", p)).then_inc(bank_free(s), 1)
                elif kind == "c_g":
                    act.wait_ge(tile_done, upto(s))
                    A(cg[:, s[1], :], at_ring(s)[:], ACT.Silu, bias=pc("b_cg", s[1])).then_inc(bank_free(s), 1)
                elif kind == "b_o":
                    act.wait_ge(tile_done, upto(s))
                    A(bo[:, s[1], :], at_ring(s)[:], ACT.Sigmoid, bias=pc("b_bo", s[1])).then_inc(bank_free(s), 1)
                elif kind == "gates":
                    act.wait_ge(tile_done, upto(s))
                    A(gz[:], at_ring(s)[0:96, :], ACT.Identity, bias=pc("b_gate", r=slice(0, 96))).then_inc(bank_free(s), 1)
                elif kind == "gate_math":
                    act.wait_ge(bank_free(("gates", 0)), drains(("gates", 0)))
                    A(g1[:], gz[:], ACT.Abs).then_inc(act_step, 1)
                    act.wait_ge(act_step, step())
                    A(g1[:], g1[:], ACT.Exp, scale=-1.0).then_inc(act_step, 1)
                    act.wait_ge(act_step, step())
                    A(g1[:], g1[:], ACT.Ln, bias=1.0).then_inc(gate_ln, 1)
                    act.wait_ge(gate_m, 1)
                    A(g3[32:36, :], g3[32:36, :], ACT.Exp, scale=-1.0).then_inc(gate_rows, 1)
                elif kind in ("b_qk", "a_q", "a_k"):
                    i = s[1]
                    dst, b = {"b_qk": (bqk[:, i, 3:T + 3], "b_bqk"), "a_q": (qT[:, i, :], "b_aq"), "a_k": (kT[:, i, :], "b_ak")}[kind]
                    act.wait_ge(tile_done, upto(s))
                    A(dst, at_ring(s)[:], ACT.Identity, bias=pc(b, i)).then_inc(bank_free(s), 1)
                elif kind == "hg_att_out":
                    act.wait_ge(hg_a_used, LC)
                    act.wait_ge(hg_q, 1)
                    for p in range(2):
                        A(attS[:, p, :], bank[p][0:64, :], ACT.Identity).then_inc(hg_att_s, 1)
                elif kind == "hg_kdT":
                    p = s[1]
                    act.wait_ge(hg_kdT_mm, p + 1)
                    A(kdT[:, p].rearrange("p b d -> p (b d)"), bank[4 + p][:], ACT.Identity).then_inc(hg_kdT_s, 1)
                elif kind == "hg_u":
                    p, b = s[1:]
                    n = HG["u", p, b]
                    act.wait_ge(hg_u_mm, n + 1)
                    if p == 1:
                        act.wait_ge(hg_o_mm, 1)
                    A(U[:, :, 8 * b:8 * b + 8], bank[4 + n % 2][:].rearrange("p (c e) -> p e c", e=HD), ACT.Identity).then_inc(hg_u_s, 1)
                elif kind in ("hg_y", "qk_norm"):
                    i = s[1]
                    n = i + (2 if kind == "qk_norm" else 0)
                    if n >= 2:
                        act.wait_ge(nrm_done, n - 1)
                    if kind == "hg_y":
                        act.wait_ge(hg_o_mm, i + 1)
                        src = bank[i][:]
                    else:
                        src = (qT if i < 4 else kT)[:, i % 4, :]
                        act.wait_ge(bank_free(("a_q" if i < 4 else "a_k", i % 4)), drains(("a_q" if i < 4 else "a_k", i % 4)))
                    A(scr[n % 2][:], src, ACT.Square).then_inc(nrm_sq, 1)
                    act.wait_ge(nrm_mm, n + 1)
                    A(scr[n % 2][:], bank[4][:], ACT.Ln, bias=cc("eps"), scale=1.0 / HD).then_inc(act_step, 1)
                    act.wait_ge(act_step, step())
                    A(scr[n % 2][:], scr[n % 2][:], ACT.Exp, scale=-0.5).then_inc(nrm_rs, 1)
                elif kind == "conv":
                    t = s[1]
                    act.wait_ge(conv_b, t + 1)
                    A(qkB[:, t, :], qkB[:, t, :], ACT.Silu).then_inc(qkB_ready, 1)
                elif kind == "ml":
                    h = s[1]
                    act.wait_ge(ml_w, 4 * h + 4)
                    A(PM[h % 2][:], PM[h % 2][:], ACT.Exp).then_inc(ml_e, 1)
                elif kind == "yb_norm":
                    act.wait_ge(yb_var, 1)
                    A(msB, msB, ACT.Ln).then_inc(act_step, 1)
                    act.wait_ge(act_step, step())
                    A(rsB, msB, ACT.Exp, scale=-0.5).then_inc(yb_rs, 1)
                elif kind == "fox_s":
                    u = s[1]
                    qb, h = fox[u]
                    n = (qb + 1) * P
                    act.wait_ge(fox_m, u + 1)
                    if u >= 2:
                        act.wait_ge(fox_t_mm, u - 1)
                    A(Pf[u % 2][:, 0:n], bank[u % 2][:, 0:n], ACT.Exp, bias=nmx[:, u % 4:u % 4 + 1],
                      accum_out=rsum[:, 8 * (qb % 2) + h:8 * (qb % 2) + h + 1]).then_inc(fox_e, 1)
                elif kind == "ya":
                    qb = s[1]
                    act.wait_ge(ya_var, qb + 1)
                    A(msA, msA, ACT.Ln).then_inc(act_step, 1)
                    act.wait_ge(act_step, step())
                    A(rsA, msA, ACT.Exp, scale=-0.5).then_inc(ya_rs, 1)
                    act.wait_ge(bank_free(s), drains(s))
                    A(hH[:, 0:4, qb * P:qb * P + P], yt[:], ACT.Identity).then_inc(ya_hi, 1)
                elif kind == "y_split":
                    i = s[1]
                    src = (bo if i < 2 else cg)[:, i % 2, :]
                    if i == 0:
                        act.wait_ge(bank_free(("yb", 0)), drains(("yb", 0)))
                        act.wait_ge(bank_free(("yb", 1)), drains(("yb", 1)))
                        act.wait_ge(hg_done, 2)
                        act.wait_ge(tile_done, upto(("a_v", 3)))
                    A(hH[:, 4 + i, :], src, ACT.Identity).then_inc(ys_hi, 1)
                elif kind == "wo_b":
                    j = s[1]
                    act.wait_ge(tile_done, upto(s))
                    A(xT[:, j, :], at_ring(s)[:], ACT.Identity).then_inc(bank_free(s), 1)
                elif kind == "n_sq":
                    i, j = s[1:]
                    src = ("wo_a", j) if i == 0 else ("down", 1, j)
                    act.wait_ge(bank_free(src), drains(src))
                    if KD * i + j >= 2:
                        act.wait_ge(n_mm, KD * i + j - 1)
                    A(sqn[j % 2][:], xT[:, j, :], ACT.Square).then_inc(n_sq, 1)
                elif kind == "n_split":
                    i, j = s[1:]
                    if i == 0 and j == KD // 2:
                        act.wait_ge(tile_done, upto(("wo_a", KD - 1)))
                    A(hH[:, nslot(i, j), :], xT[:, j, :], ACT.Identity, scale=pc(("g_ffn", "g_in2")[i], j)).then_inc(n_hi, 1)
                elif kind == "n_sum":
                    i, j = s[1:]
                    if j == KD - 1:
                        act.wait_ge(n_mm, KD * i + KD)
                        A(rsn[:], bank[0][:], ACT.Ln, bias=cc("eps"), scale=1.0 / D).then_inc(act_step, 1)
                        act.wait_ge(act_step, step())
                        A(rsn[:], rsn[:], ACT.Exp, scale=-0.5).then_inc(n_rs, 1)
                elif kind == "up":
                    i = s[1]
                    act.wait_ge(conv_g, i + 1)
                    A(cvg[i % 2][:], cvg[i % 2][:], ACT.Silu).then_inc(silu_ready, 1)
                    if i >= 1:
                        act.wait_ge(hidden, i)
                        A(hidH[:, (i - 1) % HSLOT, :], hid[(i - 1) % 2][:], ACT.Identity).then_inc(hid_hi, 1)
                elif kind == "hid_flush":
                    act.wait_ge(hidden, FT)
                    A(hidH[:, (FT - 1) % HSLOT, :], hid[(FT - 1) % 2][:], ACT.Identity).then_inc(hid_hi, 1)
                elif kind == "rope_tables":
                    act.wait_ge(rot_ready, 1)
                    A(sinT[:], rotT[:], ACT.Sin).then_inc(sin_ready, 1)
                    act.wait_ge(rot_ready, 2)
                    A(cosT[:], angT[:], ACT.Sin).then_inc(cos_ready, 1)
                    act.wait_ge(lam_s, 2)
                    A(lame, lams, ACT.Exp).then_inc(lam_e, 1)
                elif kind in ("dq", "dk", "qr", "kr"):
                    n = {"dq": 0, "dk": 4, "kr": 8, "qr": 9}[kind] + s[1]
                    act.wait_ge(tile_done, upto(s))
                    if n >= 2:
                        act.wait_ge(rope_done, n - 1)
                    z, o = zs[n % 2], at_ring(s)
                    for g in range(4):
                        f = g ^ 1
                        ins = A(z[32 * g:32 * g + 32, :], o[32 * f:32 * f + 32, :], ACT.Identity)
                    ins.then_inc(rope_z, 1)
                elif kind in ("dg", "mg"):
                    i = s[1]
                    act.wait_ge(bank_free(s), drains(s))
                    gate = (sdg if kind == "dg" else smg)[:, i, :]
                    A(gate, gate, ACT.Silu).then_inc(gate_on, 1)
                elif kind == "dif_s":
                    u = s[1]
                    qb, h = dif[u]
                    n = (qb + 1) * P
                    if u == 0:
                        act.wait_ge(lam_done, 1)
                        act.wait_ge(cos_ready, 1)
                    for m in range(2):
                        act.wait_ge(dif_m, 2 * u + m + 1)
                        if m == 0:
                            if u >= 2:
                                act.wait_ge(dif_t_mm, u - 1)
                            if u >= 2:
                                act.wait_ge(dif_c, u - 1)
                        A(P2[2 * (u % 2) + m][:, 0:n], bank[m][:, 0:n], ACT.Exp, bias=nmx[:, 2 * (u % 2) + m:2 * (u % 2) + m + 1],
                          accum_out=rsum2[:, 8 * (qb % 2) + 4 * m + h:8 * (qb % 2) + 4 * m + h + 1]).then_inc(dif_e, 1)
                elif kind == "yd":
                    qb = s[1]
                    act.wait_ge(yd_var, qb + 1)
                    A(ms2, ms2, ACT.Ln).then_inc(act_step, 1)
                    act.wait_ge(act_step, step())
                    A(rs2, ms2, ACT.Exp, scale=-0.5).then_inc(yd_rs, 1)
                    act.wait_ge(bank_free(s), drains(s))
                    A(oH[:, 0:4, qb * P:qb * P + P], yt2[:], ACT.Identity).then_inc(o_hi, 1)
                elif kind == "ym":
                    qb = s[1]
                    act.wait_ge(bank_free(s), drains(s))
                    if qb == 0:
                        act.wait_ge(tile_done, upto(("mv", 3)))
                    A(oH[:, 4:8, qb * P:qb * P + P], yt2[:], ACT.Identity).then_inc(o_hi, 1)
                elif kind == "lat":
                    i = s[1]
                    act.wait_ge(bank_free(s), drains(s))
                    A(latS[i][:], lat[i][:], ACT.Square).then_inc(lat_sq, 1)
                elif kind == "lat_norm":
                    i = s[1]
                    act.wait_ge(tile_done, upto(s))
                    if i == 0:
                        act.wait_ge(rope_done, 9)
                    else:
                        act.wait_ge(lat_t, 3)
                    A(rsl[:], at_ring(s)[:], ACT.Ln, bias=cc("eps"), scale=1.0 / (384, 256)[i]).then_inc(bank_free(s), 1)
                    act.wait_ge(bank_free(s), drains(s))
                    A(rsl[:], rsl[:], ACT.Exp, scale=-0.5).then_inc(lat_rs, 1)
                    for n in ((0, 1, 2), (3, 4))[i]:
                        act.wait_ge(lat_t, n + 1)
                        A(latH[n][:], lat[n][:], ACT.Identity).then_inc(lat_hi, 1)
                elif kind in ("qn", "kn"):
                    act.wait_ge(tile_done, upto(s))
                    A((qn if kind == "qn" else kn)[:, s[1], :], at_ring(s)[:], ACT.Identity, scale=MLA_SCALE if kind == "qn" else 1.0).then_inc(bank_free(s), 1)
                elif kind == "mv":
                    act.wait_ge(tile_done, upto(s))
                    A(mv[:, s[1], :], at_ring(s)[:], ACT.Identity).then_inc(bank_free(s), 1)
                elif kind == "mla_s":
                    u = s[1]
                    qb, h = mla[u]
                    n = (qb + 1) * P
                    act.wait_ge(mla_m, u + 1)
                    if u >= 2:
                        act.wait_ge(mla_t_mm, u - 1)
                    A(Pm[u % 2][:, 0:n], bank[u % 2][:, 0:n], ACT.Exp, bias=nmx[:, u % 4:u % 4 + 1],
                      accum_out=rsum2[:, 4 * (qb % 2) + h:4 * (qb % 2) + h + 1]).then_inc(mla_e, 1)
                elif kind in ("gd", "gm"):
                    i = s[1]
                    act.wait_ge(bank_free(s), drains(s))
                    gate = (sgd if kind == "gd" else sgm)[i % 2][:]
                    A(gate, gate, ACT.Sigmoid).then_inc(gd_on if kind == "gd" else gm_on, 1)
                elif kind == "pm":
                    i = s[1]
                    if i >= 1:
                        if i >= 1:
                            act.wait_ge(merged, i)
                        A(mH[:, i - 1, :], mt2[(i - 1) % 2][:], ACT.Identity).then_inc(m_hi, 1)
                elif kind == "m_flush":
                    act.wait_ge(merged, KD)
                    A(mH[:, KD - 1, :], mt2[(KD - 1) % 2][:], ACT.Identity).then_inc(m_hi, 1)
                elif kind == "out":
                    c, i = s[1:]
                    act.wait_ge(tile_done, upto(s))
                    A(xo[:, 2 * i:2 * i + 2, 256 * c:256 * c + 256], v3(at_ring(s)[:], 256), ACT.Identity).then_inc(bank_free(s), 1)
                    act.wait_ge(bank_free(s), drains(s))
                    for e in range(2):
                        b = 2 * i + e
                        A(sqn[e][:, 0:256], xo[:, b, 256 * c:256 * c + 256], ACT.Square,
                          accum_out=ssf[:, 4 * b + c:4 * b + c + 1]).then_inc(ssf_ready, 1)
                    act.wait_ge(ssf_ready, 4 * c + 2 * i + 2)
                elif kind == "final":
                    act.wait_ge(f_var, 1)
                    A(sst, sst, ACT.Ln).then_inc(act_step, 1)
                    act.wait_ge(act_step, step())
                    A(rsf, sst, ACT.Exp, scale=-0.5).then_inc(f_rs, 1)
                    act.wait_ge(f_rs, 1)
                    act.wait_ge(xo_g, NB * D // 512)
                    for b in range(2):
                        A(xo[:, b, :], xo[:, b, :], ACT.Identity, scale=rsf[:, b:b + 1]).then_inc(out_act, 1)

        @block.vector
        def _(dve):
            steps = [0]

            def step():
                steps[0] += 1
                return steps[0]

            TT, TS, STT, CP = dve.tensor_tensor, dve.tensor_scalar, dve.scalar_tensor_tensor, dve.tensor_copy

            def wide(ap, n):
                return ap.unsqueeze(2).broadcast_to([ap.shape[0], ap.shape[1], n])

            def low(hi, full, dst):
                return TT(dst, full, hi.bitcast(F32), ALU.subtract)

            for s in order:
                kind = s[0]
                if kind == "x_norm":
                    b = s[1]
                    dve.wait_ge(x_rs, b + 1)
                    dve.wait_ge(gmix_in, 16)
                    STT(htok[:, b, :], xtok[:, b, :], rs_x[:, b:b + 1], gmix[:], ALU.mult, ALU.mult).then_inc(x_h, 1)
                elif kind == "x":
                    b, half = s[1:]
                    k = slice(4 * half, 4 * half + 4)
                    dve.wait_ge(h_hi, 2 * b + half + 1)
                    low(hH[:, k, b * P:b * P + P], v3(at_ring(s)[:], P), hL[:, k, b * P:b * P + P]).then_inc(bank_free(s), 1)
                elif kind == "params":
                    dve.wait_ge(par_in, 16)
                    TT(lbd, pc("lb", 0, 2), pc("lb", 0, 2), ALU.subtract).then_inc(lb_d, 1)
                    TS(nbcf, pc("b_cf", 0, 2), -1.0, None, ALU.mult).then_inc(nbcf_ready, 1)
                    TS(gq8, pc("g_aq"), HD ** -0.5, None, ALU.mult).then_inc(dve_step, 1)
                    dve.wait_ge(dve_step, step())
                    TS(gsub, pc("g_sub"), 1.0 - LAMBDA_INIT, None, ALU.mult).then_inc(dve_step, 1)
                    dve.wait_ge(dve_step, step())
                    CP(identb[:], cc("ident")).then_inc(mask_ready, 1)
                    CP(maskb[:], cc("neg")).then_inc(mask_ready, 1)
                    CP(selb[:], cc("sel")).then_inc(mask_ready, 1)
                    dve.wait_ge(lb_e, 1)
                    dve.reciprocal(lbr, lbe).then_inc(dve_step, 1)
                    dve.wait_ge(dve_step, step())
                    TT(lbp, lbe, lbr, ALU.mult).then_inc(dve_step, 1)
                    dve.wait_ge(dve_step, step())
                    TT(lb, lbp, lbp, ALU.subtract).then_inc(dve_step, 1)
                    dve.wait_ge(dve_step, step())
                    TS(lb, lb, 0.0, None, ALU.max).then_inc(dve_step, 1)
                    dve.wait_ge(dve_step, step())
                    TS(lb1, lb, -1.0, 1.0, ALU.mult, ALU.add).then_inc(dve_step, 1)
                    dve.wait_ge(dve_step, step())
                elif kind == "hg_begin":
                    for p in range(2):
                        dve.wait_ge(bank_free(("c_f", p)), drains(("c_f", p)))
                        dve.wait_ge(bank_free(("c_q", p)), drains(("c_q", p)))
                        TS(cf[:, p], cf[:, p], lb1[:, p:p + 1], lb[:, p:p + 1], ALU.mult, ALU.add).then_inc(dve_step, 1)
                        dve.wait_ge(dve_step, step())
                        TS(ck[:, p], ck[:, p], lb1[:, p:p + 1], None, ALU.mult).then_inc(dve_step, 1)
                        dve.wait_ge(dve_step, step())
                    dve.memset(cq[:, :, :, LC:LC + 1], 1.0).then_inc(dve_step, 1)
                    dve.wait_ge(dve_step, step())
                elif kind == "c_i":
                    i = s[1]
                    if i == 0:
                        dve.wait_ge(bias_in, 48)
                    dve.wait_ge(tile_done, upto(s))
                    TT(ci[:, 2 * i:2 * i + 2, :], v3(at_ring(s)[:], 256),
                            bias_t[:, 768:1024].unsqueeze(1).broadcast_to([P, 2, 256]), ALU.add).then_inc(bank_free(s), 1)
                elif kind == "b_v":
                    i = s[1]
                    if i == 0:
                        dve.wait_ge(tile_done, upto(("x", NB - 1, 1)))
                        dve.memset(bv[:, :, :, HD:HD + 1], 1.0).then_inc(dve_step, 1)
                        dve.wait_ge(dve_step, step())
                    dve.wait_ge(tile_done, upto(s))
                    for e in range(2):
                        ins = TT(bv[:, 2 * i + e, :, 0:HD], v3(at_ring(s)[:, 256 * e:256 * e + 256], HD), v3(bias_t[:, 512:768], HD), ALU.add)
                    ins.then_inc(bank_free(s), 1)
                elif kind == "a_v":
                    i = s[1]
                    half, e = i // 2, i % 2
                    dve.wait_ge(tile_done, upto(s))
                    TT(av[:, 2 * e:2 * e + 2, 256 * half:256 * half + 256], v3(at_ring(s)[:], 256),
                            bias_t[:, 256 * half:256 * half + 256].unsqueeze(1).broadcast_to([P, 2, 256]), ALU.add).then_inc(bank_free(s), 1)
                elif kind == "gate_math":
                    dve.wait_ge(gate_ln, 1)
                    STT(g2[:], gz[:], 0.0, g1[:], ALU.min, ALU.subtract).then_inc(dve_step, 1)
                    dve.wait_ge(dve_step, step())
                    dve.memset(g1[:], 1.0).then_inc(dve_step, 1)
                    dve.wait_ge(dve_step, step())
                    dve.tensor_tensor_scan(g3[:], g1[:], g2[:], 0.0, ALU.mult, ALU.add).then_inc(dve_step, 1)
                    dve.wait_ge(dve_step, step())
                    dve.memset(negB[:], 0.0).then_inc(dve_step, 1)
                    dve.wait_ge(dve_step, step())
                    TS(negC[:], g3[0:8, :], -1.0, None, ALU.mult).then_inc(dve_step, 1)
                    dve.wait_ge(dve_step, step())
                    for part in range(3):
                        CP(negT[:], negC[:]).then_inc(dve_step, 1)
                        dve.wait_ge(dve_step, step())
                        CP(negB[32 * part:32 * part + 8, :], negT[:]).then_inc(negC_ready, 1)
                        dve.wait_ge(negC_ready, part + 1)
                        if part < 2:
                            TT(negC[:], negC[:], negT[:], ALU.subtract).then_inc(dve_step, 1)
                            dve.wait_ge(dve_step, step())
                    CP(g3[32:36, :], g3[64:68, :]).then_inc(dve_step, 1)
                    dve.wait_ge(dve_step, step())
                    TT(gz[32:36, :], gz[32:36, :], g3[32:36, :], ALU.subtract).then_inc(dve_step, 1)
                    dve.wait_ge(dve_step, step())
                    dve.tensor_tensor_scan(g2[32:36, :], g1[32:36, :], gz[32:36, :], -3e38, ALU.mult, ALU.max).then_inc(dve_step, 1)
                    dve.wait_ge(dve_step, step())
                    CP(g1[32:36, :], gz[32:36, :]).then_inc(dve_step, 1)
                    dve.wait_ge(dve_step, step())
                    TT(g3[32:36, :], g3[32:36, :], g2[32:36, :], ALU.add).then_inc(gate_m, 1)
                    dve.wait_ge(gate_m, 1)
                    TS(g2[32:36, :], g2[32:36, :], -1.0, None, ALU.mult).then_inc(gate_rows, 1)
                elif kind == "gate_cols":
                    dve.wait_ge(gate_cols, 1)
                    CP(colB, bank[2][:, 0:32]).then_inc(gate_cols_out, 1)
                elif kind == "hg_att":
                    j = s[1]
                    n = LC - 1 - j
                    if n >= 2:
                        dve.wait_ge(hg_a_used, n - 1)
                    q64 = cq[:].rearrange("p h c t -> p (h c) t")
                    f64 = cf[:].rearrange("p h c t -> p (h c) t")
                    k64 = ck[:].rearrange("p h c t -> p (h c) t")
                    d64 = kd[:].rearrange("p h c t -> p (h c) t")
                    t0 = 0 if n == 0 else j
                    TT(Ab[n % 2][:].rearrange("p h (c t) -> p (h c) t", t=LC)[:, :, t0:], q64[:, :, t0:LC],
                       k64[:, :, j:j + 1].broadcast_to([P, 64, LC - t0]), ALU.mult).then_inc(hg_a, 1)
                    TT(d64[:, :, j:j + 1], q64[:, :, LC:LC + 1], k64[:, :, j:j + 1], ALU.mult).then_inc(dve_step, 1)
                    dve.wait_ge(dve_step, step())
                    dve.wait_ge(hg_a, n + 1)
                    m = LC + 1 - j
                    ins = TT(q64[:, :, j:LC + 1], q64[:, :, j:LC + 1], f64[:, :, j:j + 1].broadcast_to([P, 64, m]), ALU.mult)
                    if j == 0:
                        ins.then_inc(hg_q, 1)
                        dve.wait_ge(hg_q, 1)
                        for p in range(2):
                            dve.memset(cq[:, p, 0, LC:LC + 1], 0.0).then_inc(dve_step, 1)
                            dve.wait_ge(dve_step, step())
                    else:
                        ins.then_inc(dve_step, 1)
                        dve.wait_ge(dve_step, step())
                elif kind == "hg_rep":
                    p, hh = s[1:]
                    n = 2 * p + hh
                    dve.wait_ge(hg_rep_mm, n + 1)
                    if p >= 1:
                        dve.wait_ge(hg_o_mm, p)
                    TT(Dm[hh][:], v3(bank[2 + hh][:], P), cc("chunk").unsqueeze(1).broadcast_to([P, NB, P]), ALU.mult).then_inc(hg_dm, 1)
                elif kind == "hg_u":
                    p, b = s[1:]
                    n = HG["u", p, b]
                    if n >= 2:
                        dve.wait_ge(hg_u_mm, n - 1)
                    if n == 0:
                        dve.wait_ge(hg_a_used, LC)
                    for hh in range(2):
                        c = (2 * p + hh) * HD
                        ins = TT(Vx[2 * (n % 2) + hh][:], ci[:, b, c:c + HD].unsqueeze(1).broadcast_to([P, 8, HD]),
                                 wide(cc("inchunk"), HD), ALU.mult)
                    ins.then_inc(hg_vx, 1)
                elif kind == "hg_scan":
                    p = s[1]
                    CP(Gx[:], cq[:, p, :, LC:LC + 1].rearrange("p c o -> p o c").broadcast_to([P, HD // 2, NC])).then_inc(dve_step, 1)
                    dve.wait_ge(dve_step, step())
                    dve.wait_ge(hg_u_s, NB * (p + 1))
                    g = Gx[:].rearrange("p e c -> p (e c)")
                    for e in range(2):
                        u = U[:, 32 * e:32 * e + 32, :].rearrange("p e c -> p (e c)")
                        ins = dve.tensor_tensor_scan(u, g, u, 0.0, ALU.mult, ALU.add)
                        if e == 0:
                            ins.then_inc(dve_step, 1)
                            dve.wait_ge(dve_step, step())
                    ins.then_inc(hg_scan, 1)
                    dve.wait_ge(hg_scan, p + 1)
                elif kind == "hg_y":
                    p = s[1]
                    dve.wait_ge(nrm_rs, p + 1)
                    TT(scr[p][:], bank[p][:], scr[p][:], ALU.mult).then_inc(hg_n, 1)
                    dve.wait_ge(hg_n, p + 1)
                    STT(cg[:, p, :], scr[p][:], pc("g_out", 6 + p), cg[:, p, :], ALU.mult, ALU.mult).then_inc(nrm_done, 1)
                    dve.wait_ge(nrm_done, p + 1)
                    dve.engine_nop().then_inc(hg_done, 1)
                elif kind == "conv":
                    t = s[1]
                    if t == 0:
                        dve.memset(bqk[:, :, 0:3], 0.0).then_inc(dve_step, 1)
                        dve.wait_ge(dve_step, step())
                    dve.wait_ge(bank_free(("b_qk", t)), drains(("b_qk", t)))
                    TS(qkB[:, t, :], bqk[:, t, 0:T], pc("w_bconv", t), None, ALU.mult).then_inc(dve_step, 1)
                    dve.wait_ge(dve_step, step())
                    for k in range(1, 4):
                        ins = STT(qkB[:, t, :], bqk[:, t, k:k + T], pc("w_bconv", 4 * k + t), qkB[:, t, :], ALU.mult, ALU.add)
                        if k < 3:
                            ins.then_inc(dve_step, 1)
                            dve.wait_ge(dve_step, step())
                    ins.then_inc(conv_b, 1)
                elif kind == "ml":
                    h = s[1]
                    segs = (0, 512, 896, 1152)
                    dve.wait_ge(ml_m_mm, h + 1)
                    if h >= 2:
                        dve.wait_ge(ml_o_mm, h - 1)
                    for b in range(NB):
                        w = T - P * b
                        TS(PM[h % 2][:, segs[b]:segs[b] + w], bank[0][:, b * P:T], colB[:, 4 * b + h:4 * b + h + 1], 0.0,
                           ALU.add, ALU.min).then_inc(ml_w, 1)
                    dve.wait_ge(ml_e, h + 1)
                    for b in range(NB):
                        TT(PM[h % 2][:, segs[b]:segs[b] + P], PM[h % 2][:, segs[b]:segs[b] + P], cc("tri"), ALU.mult).then_inc(dve_step, 1)
                        dve.wait_ge(dve_step, step())
                    for b in range(NB):
                        w = T - P * b
                        dve.wait_ge(ml_s_mm, 4 * h + 4)
                        seg = PM[h % 2][:, segs[b]:segs[b] + w]
                        STT(seg, score(b), HD ** -0.5, seg, ALU.mult, ALU.mult).then_inc(ml_p, 1)
                elif kind == "ml_o":
                    h = s[1]
                    dve.wait_ge(ml_o_mm, h + 1)
                    CP(Oh[:].rearrange("p b e -> p (b e)"), bank[3][:, 0:260]).then_inc(ml_o_s, 1)
                    dve.wait_ge(ml_o_s, h + 1)
                    den = Oh[:, :, HD:HD + 1].rearrange("p b o -> p (b o)")
                    STT(denB, den, -1.0, den, ALU.mult, ALU.max).then_inc(dve_step, 1)
                    dve.wait_ge(dve_step, step())
                    em = colB[:, 16:32].rearrange("p (b h) -> p b h", h=4)[:, :, h:h + 1].rearrange("p b o -> p (b o)")
                    TT(denB, denB, em, ALU.max).then_inc(dve_step, 1)
                    dve.wait_ge(dve_step, step())
                    dve.reciprocal(recB, denB).then_inc(dve_step, 1)
                    dve.wait_ge(dve_step, step())
                    TT(onB[:, :, h, :], Oh[:, :, 0:HD], wide(recB, HD), ALU.mult).then_inc(dve_step, 1)
                    dve.wait_ge(dve_step, step())
                elif kind == "qk_norm":
                    i = s[1]
                    dve.wait_ge(nrm_rs, i + 3)
                    dst = (qT if i < 4 else kT)[:, i % 4, :]
                    STT(dst, dst, gq8 if i < 4 else pc("g_ak"), scr[i % 2][:], ALU.mult, ALU.mult).then_inc(nrm_done, 1)
                    dve.wait_ge(nrm_done, i + 3)
                    dve.engine_nop().then_inc(qk_done, 1)
                elif kind == "yb_norm":
                    o16 = onB[:].rearrange("p b h e -> p (b h) e")
                    q16 = sqB[:].rearrange("p b h e -> p (b h) e")
                    TT(q16, o16, o16, ALU.mult).then_inc(dve_step, 1)
                    dve.wait_ge(dve_step, step())
                    dve.tensor_reduce(msB, q16, AX.X, ALU.add).then_inc(dve_step, 1)
                    dve.wait_ge(dve_step, step())
                    TS(msB, msB, 1.0 / HD, EPS, ALU.mult, ALU.add).then_inc(yb_var, 1)
                    dve.wait_ge(yb_rs, 1)
                    TT(o16, o16, wide(rsB, HD), ALU.mult).then_inc(yb_n, 1)
                elif kind == "yb":
                    p = s[1]
                    dve.wait_ge(tile_done, upto(s))
                    STT(bo[:, p, :], at_ring(s)[:], pc("g_out", 4 + p), bo[:, p, :], ALU.mult, ALU.mult).then_inc(bank_free(s), 1)
                elif kind == "fox_s":
                    u = s[1]
                    qb, h = fox[u]
                    n = (qb + 1) * P
                    dve.wait_ge(fox_s_mm, u + 1)
                    dve.tensor_reduce(nmx[:, u % 4:u % 4 + 1], bank[u % 2][:, 0:n], AX.X, ALU.max, negate=True).then_inc(fox_m, 1)
                elif kind == "fox_t":
                    u = s[1]
                    qb, h = fox[u]
                    n = (qb + 1) * P
                    dve.wait_ge(fox_t_mm, u + 1)
                    if u >= 2:
                        dve.wait_ge(fox_v_mm, u - 1)
                    CP(PTs[u % 2][:, 0:n], bank[2 + u % 2][:, 0:n]).then_inc(fox_pt, 1)
                elif kind == "ya":
                    qb = s[1]
                    dve.wait_ge(fox_v_mm, AH * (qb + 1))
                    dve.reciprocal(recA, rsum[:, 8 * (qb % 2):8 * (qb % 2) + 8]).then_inc(dve_step, 1)
                    dve.wait_ge(dve_step, step())
                    if qb >= 1:
                        dve.wait_ge(tile_done, upto(("ya", qb - 1)))
                    TT(on[:], v3(bank[4 + qb % 2][:], HD), wide(recA, HD), ALU.mult).then_inc(fox_o_free, 1)
                    dve.wait_ge(fox_o_free, qb + 1)
                    TT(sqA[:], on[:], on[:], ALU.mult).then_inc(dve_step, 1)
                    dve.wait_ge(dve_step, step())
                    dve.tensor_reduce(msA, sqA[:], AX.X, ALU.add).then_inc(dve_step, 1)
                    dve.wait_ge(dve_step, step())
                    TS(msA, msA, 1.0 / HD, EPS, ALU.mult, ALU.add).then_inc(ya_var, 1)
                    dve.wait_ge(ya_rs, qb + 1)
                    TT(on[:], on[:], wide(rsA, HD), ALU.mult).then_inc(ya_n, 1)
                    dve.wait_ge(tile_done, upto(s))
                    TT(yt[:], v3(at_ring(s)[:], P), wide(pc("g_out", 0, 4), P), ALU.mult).then_inc(bank_free(s), 1)
                    dve.wait_ge(ya_hi, qb + 1)
                    t = slice(qb * P, qb * P + P)
                    low(hH[:, 0:4, t], yt[:], hL[:, 0:4, t]).then_inc(y_lo, 1)
                    dve.wait_ge(y_lo, 4 + qb + 1)
                elif kind == "y_split":
                    i = s[1]
                    dve.wait_ge(ys_hi, i + 1)
                    low(hH[:, 4 + i, :], (bo if i < 2 else cg)[:, i % 2, :], hL[:, 4 + i, :]).then_inc(y_lo, 1)
                elif kind == "wo_a":
                    j = s[1]
                    dve.wait_ge(tile_done, upto(s))
                    dve.wait_ge(bank_free(("wo_b", j)), drains(("wo_b", j)))
                    TT(xT[:, j, :], xT[:, j, :], at_ring(s)[:], ALU.add).then_inc(bank_free(s), 1)
                elif kind == "n_split":
                    i, j = s[1:]
                    src = ("wo_a", j) if i == 0 else ("down", 1, j)
                    dve.wait_ge(bank_free(src), drains(src))
                    dve.wait_ge(n_hi, KD * i + j + 1)
                    at = nslot(i, j)
                    STT(hL[:, at, :], xT[:, j, :], pc(("g_ffn", "g_in2")[i], j), hH[:, at, :].bitcast(F32),
                        ALU.mult, ALU.subtract).then_inc(n_lo, 1)
                elif kind in ("gate", "up"):
                    i = s[1]
                    g = 0 if kind == "gate" else FT
                    z = zp[(0 if kind == "gate" else 2) + i % 2]
                    dst = (cvg if kind == "gate" else cvu)[i % 2]
                    if s == ("gate", 0):
                        for pad in zp:
                            pad_zero = dve.memset(pad[:, 0:2], 0.0)
                        pad_zero.then_inc(zp_zero, 1)
                        dve.wait_ge(zp_zero, 1)
                        dve.wait_ge(n_rs, 1)
                    dve.wait_ge(tile_done, upto(s))
                    if i >= 2:
                        dve.wait_ge(conv_g if kind == "gate" else conv_u, i - 1)
                        dve.wait_ge(hidden, i - 1)
                    TT(z[:, 2:T + 2], at_ring(s)[:], rsn[:], ALU.mult).then_inc(bank_free(s), 1)
                    dve.wait_ge(bank_free(s), drains(s))
                    TS(dst[:], z[:, 0:T], pc("w_fconv", g + i), pc("b_fconv", g + i), ALU.mult, ALU.add).then_inc(dve_step, 1)
                    dve.wait_ge(dve_step, step())
                    STT(dst[:], z[:, 1:T + 1], pc("w_fconv", 44 + g + i), dst[:], ALU.mult, ALU.add).then_inc(dve_step, 1)
                    dve.wait_ge(dve_step, step())
                    STT(dst[:], z[:, 2:T + 2], pc("w_fconv", 88 + g + i), dst[:], ALU.mult, ALU.add).then_inc(
                        conv_g if kind == "gate" else conv_u, 1)
                    if kind == "up":
                        dve.wait_ge(conv_u, i + 1)
                        dve.wait_ge(silu_ready, i + 1)
                        if i >= 2:
                            dve.wait_ge(hid_lo, i - 1)
                        TT(hid[i % 2][:], cvg[i % 2][:], cvu[i % 2][:], ALU.mult).then_inc(hidden, 1)
                        if i >= 1:
                            dve.wait_ge(hid_hi, i)
                            low(hidH[:, (i - 1) % HSLOT, :], hid[(i - 1) % 2][:], hidL[:, (i - 1) % HSLOT, :]).then_inc(hid_lo, 1)
                elif kind == "hid_flush":
                    dve.wait_ge(hid_hi, FT)
                    low(hidH[:, (FT - 1) % HSLOT, :], hid[(FT - 1) % 2][:], hidL[:, (FT - 1) % HSLOT, :]).then_inc(hid_lo, 1)
                elif kind == "down":
                    half, j = s[1:]
                    dve.wait_ge(tile_done, upto(s))
                    if half == 1:
                        dve.wait_ge(bank_free(("down", 0, j)), drains(("down", 0, j)))
                    TT(xT[:, j, :], xT[:, j, :], at_ring(s)[:], ALU.add).then_inc(bank_free(s), 1)
                elif kind == "rope_tables":
                    dve.wait_ge(pos_in, 16)
                    CP(angT[:], posI[:]).then_inc(dve_step, 1)
                    dve.wait_ge(dve_step, step())
                    TS(angT[:], angT[:], cc("freq"), None, ALU.mult).then_inc(dve_step, 1)
                    dve.wait_ge(dve_step, step())
                    two_pi = 2 * np.pi
                    parts = [6.28125, float(np.float32(two_pi - 6.28125)), 0.0]
                    parts[2] = float(two_pi - parts[0] - parts[1])
                    magic = 1.5 * 2.0 ** 23
                    for which in range(2):
                        turn = cosT if which == 0 else sqn[0]
                        if which == 0:
                            TS(cosT[:], angT[:], 1.0 / two_pi, magic, ALU.mult, ALU.add).then_inc(dve_step, 1)
                            dve.wait_ge(dve_step, step())
                        else:
                            TS(sqn[0][:], angT[:], 1.0 / two_pi, 0.25, ALU.mult, ALU.add).then_inc(dve_step, 1)
                            dve.wait_ge(dve_step, step())
                            TS(sqn[0][:], sqn[0][:], magic, None, ALU.add).then_inc(dve_step, 1)
                            dve.wait_ge(dve_step, step())
                        TS(turn[:], turn[:], -magic, None, ALU.add).then_inc(dve_step, 1)
                        dve.wait_ge(dve_step, step())
                        dst = rotT if which == 0 else angT
                        src = angT
                        for part in parts:
                            STT(dst[:], turn[:], -part, src[:], ALU.mult, ALU.add).then_inc(dve_step, 1)
                            dve.wait_ge(dve_step, step())
                            src = dst
                        if which == 1:
                            TS(dst[:], dst[:], cc("halfpi"), None, ALU.add).then_inc(dve_step, 1)
                            dve.wait_ge(dve_step, step())
                        TS(dst[:], dst[:], 3.1415925, -3.1415925, ALU.min, ALU.max).then_inc(rot_ready, 1)
                        dve.wait_ge(rot_ready, which + 1)
                    dve.wait_ge(sin_ready, 1)
                    TS(sinT[:], sinT[:], cc("sign"), None, ALU.mult).then_inc(dve_step, 1)
                    dve.wait_ge(dve_step, step())
                    dve.wait_ge(lam_in, 16)
                    lv = lamv[:].rearrange("p (a b) d -> p a b d", b=2)
                    for m in range(2):
                        TT(lamm[:, m, :], lv[:, m, 0, :], lv[:, m, 1, :], ALU.mult).then_inc(dve_step, 1)
                        dve.wait_ge(dve_step, step())
                        dve.tensor_reduce(lams[:, m:m + 1], lamm[:, m, :], AX.X, ALU.add).then_inc(lam_s, 1)
                    dve.wait_ge(lam_e, 1)
                    TT(nlam, lame[:, 1:2], lame[:, 0:1], ALU.subtract).then_inc(dve_step, 1)
                    dve.wait_ge(dve_step, step())
                    TS(nlam, nlam, -LAMBDA_INIT, None, ALU.add).then_inc(lam_done, 1)
                    dve.wait_ge(lam_done, 1)
                    dve.wait_ge(cos_ready, 1)
                elif kind in ("dq", "dk", "qr", "kr"):
                    n = {"dq": 0, "dk": 4, "kr": 8, "qr": 9}[kind] + s[1]
                    sc = {"dq": HD ** -0.5, "dk": 1.0, "qr": MLA_SCALE, "kr": 1.0}[kind]
                    dst = kr[:] if kind == "kr" else {"dq": dq, "dk": dk, "qr": qr}[kind][:, s[1], :]
                    if n == 0:
                        dve.wait_ge(n_rs, 2)
                        TT(cosR[:], cosT[:], rsn[:], ALU.mult).then_inc(dve_step, 1)
                        dve.wait_ge(dve_step, step())
                        TT(sinR[:], sinT[:], rsn[:], ALU.mult).then_inc(dve_step, 1)
                        dve.wait_ge(dve_step, step())
                    c, sn = (cosT, sinT) if kind == "qr" else (cosR, sinR)
                    dve.wait_ge(rope_z, n + 1)
                    STT(dst, at_ring(s)[:], sc, c[:], ALU.mult, ALU.mult).then_inc(bank_free(s), 1)
                    STT(zs[n % 2][:], zs[n % 2][:], sc, sn[:], ALU.mult, ALU.mult).then_inc(dve_step, 1)
                    dve.wait_ge(dve_step, step())
                    dve.wait_ge(bank_free(s), drains(s))
                    TT(dst, dst, zs[n % 2][:], ALU.add).then_inc(rope_done, 1)
                elif kind == "rs_col":
                    dve.wait_ge(col_mm, 1)
                    CP(rs_col, bank[5][:, 0:NB]).then_inc(dve_step, 1)
                    dve.wait_ge(dve_step, step())
                elif kind == "dv":
                    i = s[1]
                    half, e = i // 2, i % 2
                    dve.wait_ge(tile_done, upto(s))
                    for b in (2 * e, 2 * e + 1):
                        at = 256 * (b % 2)
                        ins = TS(dv[:, b, 256 * half:256 * half + 256], at_ring(s)[:, at:at + 256], rs_col[:, b:b + 1], None, ALU.mult)
                    ins.then_inc(bank_free(s), 1)
                elif kind in ("dg", "mg", "lat"):
                    i = s[1]
                    dst = lat[i][:] if kind == "lat" else (sdg if kind == "dg" else smg)[:, i, :]
                    dve.wait_ge(tile_done, upto(s))
                    TT(dst, at_ring(s)[:], rsn[:], ALU.mult).then_inc(bank_free(s), 1)
                elif kind in ("gd", "gm"):
                    i = s[1]
                    dve.wait_ge(tile_done, upto(s))
                    if i >= 2:
                        dve.wait_ge(gated_d if kind == "gd" else gated_m, i - 1)
                    TT((sgd if kind == "gd" else sgm)[i % 2][:], at_ring(s)[:], rsn[:], ALU.mult).then_inc(bank_free(s), 1)
                elif kind == "dif_s":
                    u = s[1]
                    qb, h = dif[u]
                    n = (qb + 1) * P
                    for m in range(2):
                        dve.wait_ge(dif_s_mm, 2 * u + m + 1)
                        dve.tensor_reduce(nmx[:, 2 * (u % 2) + m:2 * (u % 2) + m + 1], bank[m][:, 0:n], AX.X, ALU.max,
                                          negate=True).then_inc(dif_m, 1)
                elif kind == "dif_t":
                    u = s[1]
                    qb, h = dif[u]
                    n = (qb + 1) * P
                    dve.wait_ge(dif_e, 2 * u + 2)
                    r0, r1 = (rsum2[:, 8 * (qb % 2) + 4 * m + h:8 * (qb % 2) + 4 * m + h + 1] for m in range(2))
                    w, rc = wgt2[:, u % 2:u % 2 + 1], rec2[:, u % 2:u % 2 + 1]
                    dve.reciprocal(rc, r1).then_inc(dve_step, 1)
                    dve.wait_ge(dve_step, step())
                    TS(w, r0, rc, nlam, ALU.mult, ALU.mult).then_inc(dve_step, 1)
                    dve.wait_ge(dve_step, step())
                    a, b = P2[2 * (u % 2)], P2[2 * (u % 2) + 1]
                    STT(a[:, 0:n], b[:, 0:n], w, a[:, 0:n], ALU.mult, ALU.add).then_inc(dif_c, 1)
                    dve.wait_ge(dif_t_mm, u + 1)
                    if u >= 2:
                        dve.wait_ge(dif_v_mm, u - 1)
                    CP(PT2[u % 2][:, 0:n], bank[2 + u % 2][:, 0:n]).then_inc(dif_pt, 1)
                elif kind == "mla_s":
                    u = s[1]
                    qb, h = mla[u]
                    n = (qb + 1) * P
                    dve.wait_ge(mla_s_mm, u + 1)
                    dve.tensor_reduce(nmx[:, u % 4:u % 4 + 1], bank[u % 2][:, 0:n], AX.X, ALU.max, negate=True).then_inc(mla_m, 1)
                elif kind == "mla_t":
                    u = s[1]
                    qb, h = mla[u]
                    n = (qb + 1) * P
                    dve.wait_ge(mla_t_mm, u + 1)
                    if u >= 2:
                        dve.wait_ge(mla_v_mm, u - 1)
                    CP(PT2[u % 2][:, 0:n], bank[2 + u % 2][:, 0:n]).then_inc(mla_pt, 1)
                elif kind in ("yd", "ym"):
                    qb = s[1]
                    o_free, v_mm = (dif_o_free, dif_v_mm) if kind == "yd" else (mla_o_free, mla_v_mm)
                    dve.wait_ge(v_mm, 4 * (qb + 1))
                    at = (8 if kind == "yd" else 4) * (qb % 2)
                    dve.reciprocal(rec2, rsum2[:, at:at + 4]).then_inc(dve_step, 1)
                    dve.wait_ge(dve_step, step())
                    if qb >= 1:
                        dve.wait_ge(tile_done, upto((kind, qb - 1)))
                    elif kind == "ym":
                        dve.wait_ge(tile_done, upto(("yd", NB - 1)))
                    TT(on2[:], v3(bank[4 + qb % 2][:], P), wide(rec2, P), ALU.mult).then_inc(o_free, 1)
                    dve.wait_ge(o_free, qb + 1)
                    if kind == "yd":
                        TT(sq2[:], on2[:], on2[:], ALU.mult).then_inc(dve_step, 1)
                        dve.wait_ge(dve_step, step())
                        dve.tensor_reduce(ms2, sq2[:], AX.X, ALU.add).then_inc(dve_step, 1)
                        dve.wait_ge(dve_step, step())
                        TS(ms2, ms2, 1.0 / P, EPS, ALU.mult, ALU.add).then_inc(yd_var, 1)
                        dve.wait_ge(yd_rs, qb + 1)
                        TT(on2[:], on2[:], wide(rs2, P), ALU.mult).then_inc(yd_n, 1)
                    else:
                        dve.engine_nop().then_inc(ym_n, 1)
                    dve.wait_ge(tile_done, upto(s))
                    t = slice(qb * P, qb * P + P)
                    gate = sdg if kind == "yd" else smg
                    first = 0 if kind == "yd" else 4
                    dve.wait_ge(gate_on, 4 if kind == "yd" else 8)
                    if kind == "yd":
                        STT(yt2[:], v3(at_ring(s)[:], P), gsub, gate[:, :, t], ALU.mult, ALU.mult).then_inc(bank_free(s), 1)
                    else:
                        TT(yt2[:], v3(at_ring(s)[:], P), gate[:, :, t], ALU.mult).then_inc(bank_free(s), 1)
                    n = qb + (0 if kind == "yd" else NB)
                    dve.wait_ge(o_hi, n + 1)
                    low(oH[:, first:first + 4, t], yt2[:], oL[:, first:first + 4, t]).then_inc(o_lo, 1)
                    dve.wait_ge(o_lo, n + 1)
                elif kind == "lat_norm":
                    i = s[1]
                    dve.wait_ge(lat_rs, i + 1)
                    for n in ((0, 1, 2), (3, 4))[i]:
                        g = pc("g_cq2", n) if i == 0 else pc("g_ckv", n - 3)
                        STT(lat[n][:], lat[n][:], g, rsl[:], ALU.mult, ALU.mult).then_inc(lat_t, 1)
                    for n in ((0, 1, 2), (3, 4))[i]:
                        dve.wait_ge(lat_hi, n + 1)
                        low(latH[n][:], lat[n][:], latL[n][:]).then_inc(lat_lo, 1)
                elif kind in ("pd", "pm"):
                    i = s[1]
                    dve.wait_ge(tile_done, upto(s))
                    dve.wait_ge(gd_on if kind == "pd" else gm_on, i + 1)
                    dst = (mt if kind == "pd" else mt2)[i % 2]
                    src = (sgd if kind == "pd" else sgm)[i % 2]
                    if kind == "pm":
                        if i >= 2:
                            dve.wait_ge(m_lo, i - 1)
                    elif i >= 2:
                        if i >= 2:
                            dve.wait_ge(merged, i - 1)
                    TT(dst[:], at_ring(s)[:], src[:], ALU.mult).then_inc((gated_d if kind == "pd" else gated_m), 1)
                    dve.wait_ge((gated_d if kind == "pd" else gated_m), i + 1)
                    if kind == "pd":
                        dve.engine_nop().then_inc(bank_free(s), 1)
                    else:
                        TT(mt2[i % 2][:], mt[i % 2][:], mt2[i % 2][:], ALU.add).then_inc(bank_free(s), 1)
                        dve.wait_ge(bank_free(s), drains(s))
                        dve.engine_nop().then_inc(merged, 1)
                        if i >= 1:
                            if i >= 1:
                                dve.wait_ge(m_hi, i)
                            low(mH[:, i - 1, :], mt2[(i - 1) % 2][:], mL[:, i - 1, :]).then_inc(m_lo, 1)
                elif kind == "m_flush":
                    dve.wait_ge(m_hi, KD)
                    low(mH[:, KD - 1, :], mt2[(KD - 1) % 2][:], mL[:, KD - 1, :]).then_inc(m_lo, 1)
                elif kind == "out":
                    c, i = s[1:]
                    dve.wait_ge(gfin_in, 16)
                    dve.wait_ge(ssf_ready, 4 * c + 2 * i + 2)
                    at = slice(256 * c, 256 * c + 256)
                    TT(xo[:, 2 * i:2 * i + 2, at], xo[:, 2 * i:2 * i + 2, at], gfin[:, at].unsqueeze(1).broadcast_to([P, 2, 256]),
                       ALU.mult).then_inc(xo_g, 1)
                elif kind == "final":
                    dve.tensor_reduce(sst, v3(ssf, 4), AX.X, ALU.add).then_inc(dve_step, 1)
                    dve.wait_ge(dve_step, step())
                    TS(sst, sst, 1.0 / D, EPS, ALU.mult, ALU.add).then_inc(f_var, 1)
                    dve.wait_ge(f_rs, 1)
                    dve.wait_ge(xo_g, NB * D // 512)
                    for b in range(2, NB):
                        TS(xo[:, b, :], xo[:, b, :], rsf[:, b:b + 1], None, ALU.mult).then_inc(out_dve, 1)


def kernel(**inputs):
    import numpy as _np
    import concourse.bacc as _bacc
    from concourse import mybir as _mybir
    from concourse.bass_utils import run_bass_kernel_spmd as _run

    a = {k: _np.asarray(v) for k, v in inputs.items()}
    w_in, b_in = a["w_in"][0], a["b_in"][0]

    par = _np.zeros((P, NPC), _np.float32)

    def cols(name, v):
        at, n = PCOL[name]
        par[:, at:at + n] = v.reshape(n, P).T

    cols("g_ffn", a["norm_ffn_g"][0])
    cols("g_in2", a["norm_in_2"][0])
    cols("g_out", a["out_g"][0])
    for name, at, n in (("b_aq", OFF_AQ, 512), ("b_ak", OFF_AK, 512), ("b_bqk", OFF_BQK, 512), ("b_bo", OFF_BO, 256),
                        ("b_cq", OFF_CQ, 256), ("b_cf", OFF_CF, 256), ("b_cg", OFF_CG, 256)):
        cols(name, b_in[at:at + n])
    cols("g_cq2", a["mla_q_norm_2"][0])
    cols("g_ckv", a["mla_kv_norm_2"][0])
    cols("lb", a["lb_logits"][0])
    cols("w_bconv", a["b_conv_w"][0].reshape(-1))
    cols("g_sub", a["diff_subln_2"][0])
    cols("g_aq", _np.concatenate([a["a_q_g"][0]] * 2))
    cols("g_ak", _np.concatenate([a["a_k_g"][0]] * 2))
    cols("w_fconv", a["ffn_conv_w"][0].reshape(-1))
    cols("b_fconv", a["ffn_conv_b"][0])
    w_gate = _np.zeros((P, KD, P), _np.float32)
    for row, at, n in ((0, OFF_AF, AH), (32, OFF_BI, BH), (64, OFF_BF, BH)):
        w_gate[:, :, row:row + n] = w_in[:, at:at + n].reshape(KD, P, n).transpose(1, 0, 2)
        par[row:row + n, PCOL["b_gate"][0]] = b_in[at:at + n]
    lam = _np.concatenate([a[f"diff_lambda_{v}_2"][0] for v in ("q1", "k1", "q2", "k2")])

    send = [("x", a["x"][0]), ("w_in", w_in), ("b_in", b_in), ("w_gate", w_gate), ("w_out", a["w_out"][0]),
            ("w_up", a["w_up"][0]), ("w_down", a["w_down"][0]), ("pos", a["positions_2"][0]), ("w_in2", a["w_in_2"][0]),
            ("lam", lam), ("w_uq", a["w_uq_2"][0]), ("w_ukv", a["w_ukv_2"][0]), ("w_pd", a["w_proj_diff_2"][0]),
            ("w_pm", a["w_proj_mla_2"][0]), ("w_out2", a["w_out_2"][0]), ("g_mix", a["norm_mix_g"][0]), ("g_fin", a["norm_final_2"]), ("par", par),
            ("con", constant_table())]
    nc = _bacc.Bacc("TRN2", target_bir_lowering=False, num_devices=1, dynamic_dma_scratch_size=1024)
    arrays, args = {}, []
    for name, v in send:
        v = _np.ascontiguousarray(v)
        arrays[f"in_{name}"] = v
        args.append(nc.dram_tensor(f"in_{name}", v.shape, _mybir.dt.from_np(v.dtype), kind="ExternalInput").ap())
    args.append(nc.dram_tensor("out_0", (T, D), F32, kind="ExternalOutput").ap())
    two_blocks(nc, *args)
    r = _run(nc, [arrays], core_ids=[0])
    return r.results[0]["out_0"].reshape(1, T, D)
```

```python
from contextlib import ExitStack

import numpy as np

import concourse.bass as bass
from concourse import mybir

F32 = mybir.dt.float32
F32R = mybir.dt.float32r
BF16 = mybir.dt.bfloat16
I32 = mybir.dt.int32
ACT = mybir.ActivationFunctionType
ALU = mybir.AluOpType
AX = mybir.AxisListType

P = 128
T = 512
NB = T // P
D = 1024
KD = D // P
HD = 64
AH, BH, CH = 8, 4, 4
LC = 16
NC = T // LC
DFF = 2816
FT = DFF // P
FHALF = (12, FT - 12)
HSLOT = 14
EPS = 1e-6
NEG = -1e30
LAMBDA_INIT = 0.2
MLA_SCALE = 192.0 ** -0.5
SLOT = 2048
KIB = 1024

OFF_AQ, OFF_AK, OFF_AV, OFF_AF, OFF_BQK, OFF_BV, OFF_BI, OFF_BF, OFF_BO, OFF_CQ, OFF_CF, OFF_CI, OFF_CG, _ = (
    int(v) for v in np.cumsum([0, 512, 512, 512, 8, 512, 256, 4, 4, 256, 256, 256, 256, 256]))
OFF_DQ, OFF_DK, OFF_DV, OFF_DG, OFF_CQ2, OFF_CKV, OFF_KR, OFF_MG, OFF_GD, OFF_GM, _ = (
    int(v) for v in np.cumsum([0, 512, 512, 512, 512, 384, 256, 64, 512, 1024, 1024]))

PCOL = {}
for _name, _n in [("g_ffn", 8), ("g_in2", 8), ("g_out", 8), ("b_aq", 4), ("b_ak", 4), ("b_bqk", 4),
                  ("b_bo", 2), ("b_cq", 2), ("b_cf", 2), ("b_cg", 2), ("g_cq2", 3), ("g_ckv", 2), ("lb", 2),
                  ("w_bconv", 16), ("g_sub", 1), ("g_aq", 1), ("g_ak", 1), ("b_gate", 1), ("w_fconv", 132),
                  ("b_fconv", 44)]:
    PCOL[_name] = (sum(n for _, n in PCOL.values()), _n)
NPC = sum(n for _, n in PCOL.values())

CCOL = {}
for _name, _n in [("ident", 128), ("eps", 1), ("ones", 128), ("blk", 128), ("neg", 128), ("tri", 128), ("chunk", 128),
                  ("rep", 128), ("win", 96), ("inchunk", 8), ("sel", 8), ("freq", 1), ("sign", 1), ("halfpi", 1)]:
    CCOL[_name] = (sum(n for _, n in CCOL.values()), _n)
NCC = sum(n for _, n in CCOL.values())


def constant_table():
    t = np.zeros((P, NCC), np.float32)
    r, c = np.arange(P)[:, None], np.arange(P)[None, :]

    def put(name, value):
        at, n = CCOL[name]
        t[:value.shape[0], at:at + n] = value

    put("ident", np.float32(r == c))
    put("ones", np.ones((P, P), np.float32))
    put("blk", np.float32(r // HD == c // HD))
    put("neg", np.where(c > r, np.float32(NEG), np.float32(0)))
    put("tri", np.float32(r <= c))
    put("chunk", np.float32((r // LC == c // LC) & (r <= c)))
    put("rep", np.float32(np.arange(64)[:, None] % 32 == c % LC))
    put("win", np.float32(np.arange(96)[None, :] == LC - 1 + 32 * (r // HD)))
    put("inchunk", np.float32(r // LC == np.arange(8)[None, :]))
    put("sel", np.float32((r < 72) & (r % 32 == np.arange(8)[None, :])))
    put("eps", np.full((P, 1), EPS, np.float32))
    half = np.arange(0, 64, 2, dtype=np.float32)
    freq = np.float32(10000.0) ** (-half / np.float32(64))
    put("freq", np.tile(freq, 4)[:, None].astype(np.float32))
    put("sign", np.where(r % 64 < 32, np.float32(-1), np.float32(1)))
    put("halfpi", np.full((P, 1), np.pi / 2, np.float32))
    return t


def two_blocks(nc, x_d, w_in_d, b_in_d, w_gate_d, w_out_d, w_up_d, w_down_d, pos_d, w_in2_d, lam_d, w_uq_d, w_ukv_d,
               w_pd_d, w_pm_d, w_out2_d, g_mix_d, g_fin_d, par_d, con_d, out_d):
    ctx = ExitStack()
    with ctx:
        base = 1152

        def sb(name, shape, dt, kib):
            return nc.alloc_sbuf_tensor_at(name, shape, dt, offset=base + int(round(kib * KIB)))

        def sem(name):
            return ctx.enter_context(nc.semaphore(name))

        con_in, con_rest_in, par_in, gmix_in, bias_in, lam_in, pos_in, xres_in, gfin_in = (
            sem(n) for n in ("con_in", "con_rest_in", "par_in", "gmix_in", "bias_in", "lam_in", "pos_in", "xres_in", "gfin_in"))
        hi_done, split_done = (sem(n) for n in ("hi_done", "split_done"))
        act_step, dve_step = (sem(n) for n in ("act_step", "dve_step"))
        x_in = [sem(f"x_in{b}") for b in range(NB)]
        zeros_ready = sem("zeros_ready")
        x_rs, x_gain, x_h, x_mm, h_hi, h_lo = (sem(n) for n in ("x_rs", "x_gain", "x_h", "x_mm", "h_hi", "h_lo"))
        lb_d, lb_e, nbcf_ready, mask_ready = (sem(n) for n in ("lb_d", "lb_e", "nbcf_ready", "mask_ready"))
        gate_ln, gate_m, gate_rows, gate_cols, gate_cols_out, negC_ready = (
            sem(n) for n in ("gate_ln", "gate_m", "gate_rows", "gate_cols", "gate_cols_out", "negC_ready"))
        hg_a, hg_a_used, hg_q, hg_att_s, hg_kdT_mm, hg_kdT_s = (
            sem(n) for n in ("hg_a", "hg_a_used", "hg_q", "hg_att_s", "hg_kdT_mm", "hg_kdT_s"))
        hg_vx, hg_u_mm, hg_u_s, hg_scan, hg_rep_mm, hg_dm, hg_o_mm, hg_n, hg_done = (
            sem(n) for n in ("hg_vx", "hg_u_mm", "hg_u_s", "hg_scan", "hg_rep_mm", "hg_dm", "hg_o_mm", "hg_n", "hg_done"))
        nrm_sq, nrm_mm, nrm_rs, nrm_done, qk_done = (sem(n) for n in ("nrm_sq", "nrm_mm", "nrm_rs", "nrm_done", "qk_done"))
        conv_b, qkB_ready, ml_m_mm, ml_w, ml_e, ml_s_mm, ml_p, ml_o_mm, ml_o_s = (
            sem(n) for n in ("conv_b", "qkB_ready", "ml_m_mm", "ml_w", "ml_e", "ml_s_mm", "ml_p", "ml_o_mm", "ml_o_s"))
        yb_var, yb_rs, yb_n = (sem(n) for n in ("yb_var", "yb_rs", "yb_n"))
        fox_s_mm, fox_m, fox_e, fox_t_mm, fox_pt, fox_v_mm, fox_o_free = (
            sem(n) for n in ("fox_s_mm", "fox_m", "fox_e", "fox_t_mm", "fox_pt", "fox_v_mm", "fox_o_free"))
        ya_sq, ya_var, ya_rs, ya_n, ya_hi, ys_hi, y_lo = (sem(n) for n in ("ya_sq", "ya_var", "ya_rs", "ya_n", "ya_hi", "ys_hi", "y_lo"))
        n_sq, n_acc, n_mm, n_rs, col_mm, n_hi, n_lo = (sem(n) for n in ("n_sq", "n_acc", "n_mm", "n_rs", "col_mm", "n_hi", "n_lo"))
        gate_on, gd_on, gm_on = (sem(n) for n in ("gate_on", "gd_on", "gm_on"))
        zp_zero, conv_g, conv_u, silu_ready, hidden, hid_hi, hid_lo = (
            sem(n) for n in ("zp_zero", "conv_g", "conv_u", "silu_ready", "hidden", "hid_hi", "hid_lo"))
        rot_ready, sin_ready, cos_ready, lam_s, lam_e, lam_done, rope_z, rope_done = (
            sem(n) for n in ("rot_ready", "sin_ready", "cos_ready", "lam_s", "lam_e", "lam_done", "rope_z", "rope_done"))
        dif_s_mm, dif_m, dif_e, dif_c, dif_t_mm, dif_pt, dif_v_mm, dif_o_free = (
            sem(n) for n in ("dif_s_mm", "dif_m", "dif_e", "dif_c", "dif_t_mm", "dif_pt", "dif_v_mm", "dif_o_free"))
        yd_sq, yd_rs, yd_n = (sem(n) for n in ("yd_sq", "yd_rs", "yd_n"))
        lat_sq, lat_rs, lat_t, lat_hi, lat_lo = (sem(n) for n in ("lat_sq", "lat_rs", "lat_t", "lat_hi", "lat_lo"))
        mla_s_mm, mla_m, mla_e, mla_t_mm, mla_pt, mla_v_mm, mla_o_free = (
            sem(n) for n in ("mla_s_mm", "mla_m", "mla_e", "mla_t_mm", "mla_pt", "mla_v_mm", "mla_o_free"))
        o_hi, o_lo = (sem(n) for n in ("o_hi", "o_lo"))
        gated_d, gated_m, merged, m_hi, m_lo = (sem(n) for n in ("gated_d", "gated_m", "merged", "m_hi", "m_lo"))
        ssf_ready, xo_g, f_var, f_rs, out_act, out_dve, out_done = (
            sem(n) for n in ("ssf_ready", "xo_g", "f_var", "f_rs", "out_act", "out_dve", "out_done"))
        raw_in = [sem(f"raw_in{i}") for i in range(2)]
        tile_done = sem("tile_done")
        ring_free = [sem(f"ring_free{i}") for i in range(2)]

        raw = [sb(f"w_raw{i}", [P, SLOT], F32, 8 * i) for i in range(2)]
        whi = [sb(f"w_hi{i}", [P, SLOT], F32R, 16 + 8 * i) for i in range(3)]
        wlo = [sb(f"w_lo{i}", [P, SLOT], F32R, 40 + 8 * i) for i in range(3)]
        hH = sb("act_hi", [P, KD, T], F32R, 64)
        hL = sb("act_lo", [P, KD, T], F32R, 80)
        con = sb("con", [P, NCC], F32, 96)
        par = sb("par", [P, NPC], F32, 100)
        small = sb("small", [P, 300], F32, 101.25)
        selb = sb("selb", [P, 8], BF16, 102.4375)
        identb = sb("identb", [P, P], BF16, 102.5)
        maskb = sb("maskb", [P, P], BF16, 102.75)
        M = 104
        xtok = sb("xtok", [P, NB, D], F32, M + 28)
        htok = sb("htok", [P, NB, D], F32, M + 44)
        zeros = sb("zeros", [P, T], BF16, M + 113.75)
        sqx = sb("sqx", [P, NB, D], F32, M + 12)
        gmix = sb("gmix", [P, D], F32, M)
        U = sb("U", [P, HD, NC], F32, M)
        Gx = sb("Gx", [P, HD // 2, NC], F32, M + 8)
        Ab = [sb(f"Ab{i}", [P, 2, T], F32, M + 12 + 4 * i) for i in range(2)]
        Vx = [sb(f"Vx{i}", [P, 8, HD], F32, M + 12 + 2 * i) for i in range(4)]
        kd = sb("kd", [P, 2, NC, LC], F32, M + 20)
        kdT = sb("kdT", [P, 2, NB, P], F32, M + 24)
        qT = sb("qT", [P, 4, T], F32, M + 28)
        kT = sb("kT", [P, 4, T], F32, M + 36)
        av = sb("av", [P, NB, T], F32, M + 44)
        bqk = sb("bqk", [P, 4, T + 3], F32, M + 52)
        qkB = sb("qkB", [P, 4, T], F32, M + 60.25)
        bv = sb("bv", [P, NB, BH, HD + 1], F32, M + 68.25)
        bo = sb("bo", [P, 2, T], F32, M + 72.5)
        cq = sb("cq", [P, 2, NC, LC + 1], F32, M + 76.5)
        cf = sb("cf", [P, 2, NC, LC], F32, M + 80.75)
        ck = sb("ck", [P, 2, NC, LC], F32, M + 84.75)
        ci = sb("ci", [P, NB, 256], F32, M + 88.75)
        cg = sb("cg", [P, 2, T], F32, M + 92.75)
        bias_t = sb("bias_t", [P, 1024], F32, M + 96.75)
        gz = sb("gz", [96, T], F32, M + 100.75)
        g1 = sb("g1", [96, T], F32, M + 102.75)
        g2 = sb("g2", [96, T], F32, M + 104.75)
        g3 = sb("g3", [96, T], F32, M + 106.75)
        negC = sb("negC", [8, T], F32, M + 108.75)
        negB = sb("negB", [P, T], BF16, M + 110.75)
        negT = sb("negT", [8, T], BF16, M + 111.75)
        scr = [sb(f"scr{i}", [P, T], F32, M + 113.75 + 2 * i) for i in range(2)]
        Dm = [sb(f"Dm{i}", [P, NB, P], F32, M + 80.75 + 2 * i) for i in range(2)]
        attS = sb("attS", [64, 2, T], F32, M + 84.75)
        PM = [sb(f"PM{i}", [P, 1280], F32, M + 5 * i) for i in range(2)]
        Oh = sb("Oh", [P, NB, HD + 1], F32, M + 12)
        onB = sb("onB", [P, NB, BH, HD], F32, M + 14)
        sqB = sb("sqB", [P, NB, BH, HD], F32, M + 18)
        Pf = [sb(f"Pf{i}", [P, T], F32, M + 52 + 2 * i) for i in range(2)]
        PTs = [sb(f"PTs{i}", [P, T], F32, M + 56 + 2 * i) for i in range(2)]
        on = sb("on", [P, AH, HD], F32, M + 60)
        sqA = sb("sqA", [P, AH, HD], F32, M + 62)
        yt = sb("yt", [P, 4, P], F32, M + 64)
        xT = sb("xT", [P, KD, T], F32, M)
        xres = sb("xres", [P, NB, D], F32, M + 76.5)
        sqn = [sb(f"sqn{i}", [P, T], F32, M + 16 + 2 * i) for i in range(2)]
        rsn = sb("rsn", [P, T], F32, M + 20)
        sacc = sb("sacc", [P, T], F32, M + 22)
        hidH = sb("hidH", [P, HSLOT, T], F32R, M + 26)
        hidL = sb("hidL", [P, HSLOT, T], F32R, M + 54)
        zp = [sb(f"zp{i}", [P, T + 2], F32, M + 82 + 2.25 * i) for i in range(4)]
        cvg = [sb(f"cvg{i}", [P, T], F32, M + 91 + 2 * i) for i in range(2)]
        cvu = [sb(f"cvu{i}", [P, T], F32, M + 95 + 2 * i) for i in range(2)]
        hid = [sb(f"hid{i}", [P, T], F32, M + 99 + 2 * i) for i in range(2)]
        cosT = sb("cosT", [P, T], F32, M + 104)
        sinT = sb("sinT", [P, T], F32, M + 106)
        posI = sb("posI", [P, T], I32, M + 108)
        angT = sb("angT", [P, T], F32, M + 110)
        rotT = sb("rotT", [P, T], F32, M + 112)
        dq = sb("dq", [P, 4, T], F32, M + 26)
        dk = sb("dk", [P, 4, T], F32, M + 34)
        dv = sb("dv", [P, NB, T], F32, M + 42)
        sdg = sb("sdg", [P, 4, T], F32, M + 50)
        oH = sb("oH", [P, KD, T], F32R, M + 58)
        oL = sb("oL", [P, KD, T], F32R, M + 74)
        yt2 = sb("yt2", [P, 4, P], F32, M + 90)
        PT2 = [sb(f"PT2{i}", [P, T], F32, M + 92 + 2 * i) for i in range(2)]
        kr = sb("kr", [P, T], F32, M + 96)
        cosR = sb("cosR", [P, T], F32, M + 98)
        sinR = sb("sinR", [P, T], F32, M + 100)
        P2 = [sb(f"P2{i}", [P, T], F32, M + 108 + 2 * i) for i in range(4)]
        rsl = sb("rsl", [P, T], F32, M + 98)
        zs = sqn
        on2 = sb("on2", [P, 4, P], F32, M + 22)
        sq2 = sb("sq2", [P, 4, P], F32, M + 24)
        qn = sb("qn", [P, 4, T], F32, M + 26)
        kn = sb("kn", [P, 4, T], F32, M + 34)
        mv = sb("mv", [P, NB, T], F32, M + 42)
        qr = sb("qr", [P, 2, T], F32, M + 108)
        Pm = [sb(f"Pm{i}", [P, T], F32, M + 112 + 2 * i) for i in range(2)]
        smg = sb("smg", [P, 4, T], F32, M + 50)
        latH = [sb(f"latH{i}", [P, T], F32R, M + (66, 68, 70, 72, 102)[i]) for i in range(5)]
        latS = [sb(f"latS{i}", [P, T], F32, M + (66, 68, 70, 72, 102)[i]) for i in range(5)]
        lat = [sb(f"lat{i}", [P, T], F32, M + (82, 84, 86, 88, 116)[i]) for i in range(5)]
        latL = [sb(f"latL{i}", [P, T], F32R, M + (82, 84, 86, 88, 116)[i]) for i in range(5)]
        mH = sb("mH", [P, KD, T], F32R, M + 26)
        mL = sb("mL", [P, KD, T], F32R, M + 42)
        sgd = [sb(f"sgd{i}", [P, T], F32, M + 98 + 2 * i) for i in range(2)]
        sgm = [sb(f"sgm{i}", [P, T], F32, M + 102 + 2 * i) for i in range(2)]
        mt = [sb(f"mt{i}", [P, T], F32, M + 92 + 2 * i) for i in range(2)]
        mt2 = [sb(f"mt2{i}", [P, T], F32, M + (106, 116)[i]) for i in range(2)]
        xo = sb("xo", [P, NB, D], F32, M + 58)
        gfin = sb("gfin", [P, D], F32, M + 74)
        lamv = sb("lamv", [P, 4, HD], F32, M + 117.75)
        assert M + 118.75 <= (nc.sbuf_usable_end - base) / KIB

        ring = [ctx.enter_context(nc.psum_tensor(f"ring{i}", [P, T], F32)) for i in range(2)]
        bank = [ctx.enter_context(nc.psum_tensor(f"bank{i}", [P, T], F32)) for i in range(6)]

        def cc(name, r=slice(0, P)):
            at, n = CCOL[name]
            return con[r, at:at + n]

        def pc(name, i=0, n=1, r=slice(0, P)):
            return par[r, PCOL[name][0] + i:PCOL[name][0] + i + n]

        ident = cc("ident")
        sm_at = [0]

        def sm(n):
            at = sm_at[0]
            sm_at[0] += n
            assert sm_at[0] <= 300
            return small[:, at:at + n]

        ss_x, var_x, rs_x = sm(4), sm(4), sm(4)
        rs_col = sm(4)
        lbd, lbe, lbr, lbp, lb, lb1 = (sm(2) for _ in range(6))
        nbcf = sm(2)
        gq8 = sm(1)
        colB = sm(32)
        denB, recB = sm(4), sm(4)
        msB, rsB = sm(16), sm(16)
        nmx = sm(4)
        rsum = sm(16)
        recA, msA, rsA = sm(8), sm(8), sm(8)
        rsum2, rec2, rec4, wgt2 = sm(16), sm(2), sm(4), sm(2)
        ms2, rs2 = sm(4), sm(4)
        lams = sm(2)
        lame = sm(2)
        nlam = sm(1)
        gsub = sm(1)
        ssf = sm(16)
        sst, rsf = sm(4), sm(4)
        lamm = sb("lamm", [P, 2, HD], F32, M + 108)

        chunks = []
        chunk_of = {}

        def chunk(name, *areas):
            parts, at = [], 0
            for sources in areas:
                if not isinstance(sources, list):
                    sources = [sources]
                nk, n = sources[0].shape[1], sum(src.shape[2] for src in sources)
                parts.append((at, nk, n, sources))
                at += nk * n
            assert at <= SLOT
            chunk_of[name] = len(chunks)
            chunks.append((name, parts, at))

        tiles = []
        tile_at = {}
        last_use = {}

        def tile(name, of=None):
            tile_at[name] = len(tiles)
            tiles.append(name)
            if of is not None:
                last_use[chunk_of[of]] = len(tiles) - 1

        k_in = w_in_d.rearrange("(k p) n -> p k n", p=P)
        k_out = w_out_d.rearrange("(k p) n -> p k n", p=P)
        k_up = w_up_d.rearrange("(k p) n -> p k n", p=P)
        k_down = w_down_d.rearrange("(k p) n -> p k n", p=P)
        k_in2 = w_in2_d.rearrange("(k p) n -> p k n", p=P)
        k_uq = w_uq_d.rearrange("(k p) (h n) -> p k h n", p=P, h=4)
        k_ukv = w_ukv_d.rearrange("(k p) n -> p k n", p=P)
        k_pd = w_pd_d.rearrange("(k p) n -> p k n", p=P)
        k_pm = w_pm_d.rearrange("(k p) n -> p k n", p=P)
        k_out2 = w_out2_d.rearrange("(k p) n -> p k n", p=P)

        order = []

        def stage(*s):
            order.append(s)

        POOL_GAIN = (1, 2)

        for s in (("x_norm", 0), ("x_norm", 1), ("x", 0), ("x_norm", 2), ("x_norm", 3), ("x", 1), ("x", 2), ("x", 3)):
            for half in range(2):
                if s[0] == "x":
                    stage(*s, half)
            if s[0] == "x_norm":
                stage(*s)
        stage("params")

        def in_chunk(name, at):
            chunk(name, k_in[:, :, at:at + 256])

        for i in range(2):
            chunk(f"c_f{i}", k_in[:, :, OFF_CF + P * i:OFF_CF + P * i + P])
        in_chunk("c_q", OFF_CQ)
        chunk("gates", w_gate_d)
        for i in range(2):
            in_chunk(f"b_qk{i}", OFF_BQK + 256 * i)
        in_chunk("c_g", OFF_CG)
        in_chunk("c_i", OFF_CI)
        in_chunk("b_o", OFF_BO)
        in_chunk("b_v", OFF_BV)
        for kind, at in (("a_q", OFF_AQ), ("a_k", OFF_AK), ("a_v", OFF_AV)):
            for i in range(2):
                in_chunk(f"{kind}{i}", at + 256 * i)

        def in_tile(kind, i, of):
            if (kind, i) in tile_at:
                last_use[chunk_of[of]] = tile_at[kind, i]
            else:
                tile((kind, i), of)
            stage(kind, i)

        def begin(kind, i, part):
            if part == 0:
                tile((kind, i))
            stage("begin", kind, i, part)

        att = iter(range(LC - 1, -1, -1))
        in_tile("c_f", 0, "c_f0")
        in_tile("c_f", 1, "c_f1")
        in_tile("c_q", 0, "c_q")
        in_tile("c_q", 1, "c_q")
        stage("hg_begin")

        def attend(n):
            for _ in range(n):
                stage("hg_att", next(att))

        in_tile("gates", 0, "gates")
        attend(2)
        in_tile("b_qk", 0, "b_qk0")
        attend(3)
        in_tile("b_qk", 1, "b_qk0")
        attend(3)
        in_tile("b_qk", 2, "b_qk1")
        attend(3)
        in_tile("b_qk", 3, "b_qk1")
        attend(3)
        in_tile("c_g", 0, "c_g")
        attend(2)
        in_tile("c_g", 1, "c_g")
        stage("gate_math")
        stage("hg_att_out")
        stage("hg_kdT", 0)
        stage("hg_kdT", 1)
        in_tile("c_i", 0, "c_i")
        stage("gate_exp")

        def each(kind, p, parts):
            for i in parts:
                stage(kind, p, i)

        each("hg_vx", 0, (0, 1))
        in_tile("c_i", 1, "c_i")
        each("hg_u", 0, (0, 1))
        each("hg_vx", 0, (2, 3))
        in_tile("b_o", 0, "b_o")
        stage("gate_cols")
        each("hg_u", 0, (2, 3))
        each("hg_rep", 0, (0, 1))
        stage("hg_scan", 0)
        stage("conv", 0)
        in_tile("b_o", 1, "b_o")
        each("hg_vx", 1, (0, 1))
        each("hg_o", 0, (0, 1))
        begin("b_v", 0, 0)
        each("hg_o", 0, (2, 3))
        stage("hg_sq", 0)
        stage("conv", 1)
        in_tile("b_v", 0, "b_v")
        stage("hg_y", 0)
        each("hg_u", 1, (0, 1))
        each("hg_vx", 1, (2, 3))
        stage("conv", 2)
        in_tile("b_v", 1, "b_v")
        each("hg_u", 1, (2, 3))
        each("hg_rep", 1, (0, 1))
        stage("hg_scan", 1)
        stage("conv", 3)
        stage("decay")
        in_tile("a_q", 0, "a_q0")
        stage("conv_act")
        for part in range(3):
            begin("a_q", 1, part)
            each("hg_o", 1, ((0,), (1,), (2, 3))[part])
        stage("hg_sq", 1)
        in_tile("a_q", 1, "a_q0")
        stage("hg_y", 1)
        stage("qk_sq", 0)
        rest = [("a_q", 2, "a_q1"), ("a_q", 3, "a_q1")] + [("a_k", i, f"a_k{i // 2}") for i in range(4)]
        rest += [("a_v", i, f"a_v{i // 2}") for i in (0, 2)]
        for i, (kind, t, of) in enumerate(rest):
            in_tile(kind, t, of)
            stage("qk_norm", i)
            if i + 1 < 8:
                stage("qk_sq", i + 1)
            if 1 <= i <= BH:
                stage("ml_o", i - 1)
            if i < BH:
                stage("ml", i)
            if i == BH + 1:
                stage("yb_norm")
            if i >= BH + 2:
                tile(("yb", i - BH - 2))
                stage("yb", i - BH - 2)
        for half in range(2):
            chunk(f"wo_b{half}", k_out[:, 4:8, 512 * half:512 * half + 512])
        for half in range(2):
            chunk(f"wo_a{half}", k_out[:, 0:4, 512 * half:512 * half + 512])
        fox = [(qb, h) for qb in range(NB) for h in range(AH)]

        def attention(name, heads, norm, fill_at):
            n = NB * heads
            for u in range(n + 8):
                if u < n:
                    stage(name + "_s", u)
                if name == "dif" and 1 <= u < n + 1:
                    stage(name + "_c", u - 1)
                if 2 <= u < n + 2:
                    stage(name + "_t", u - 2)
                if 3 <= u < n + 3:
                    stage(name + "_v", u - 3)
                steps = {"ya": ("ya_n", "ya_v", "ya_s", "ya", "ya_l"), "yd": ("yd_n", "yd_s", "yd", "yd_l"), "ym": ("ym_n", "ym", "ym_l")}[norm]
                for late, kind in enumerate(steps, 4):
                    qb = (u - late) // heads
                    if (u - late) % heads == heads - 1 and 0 <= qb < NB:
                        if kind == norm:
                            tile((norm, qb))
                        stage(kind, qb)
                for f in fill_at.get(u, []):
                    if f[0] in no_tile:
                        stage(*f)
                    elif len(f) == 3 and isinstance(f[2], int):
                        begin(*f)
                    elif len(f) == 3:
                        in_tile(*f)
                    else:
                        tile(f)
                        stage(*f)

        no_tile = ("y_split", "gate_act", "lat_t")

        def wo_b(*js):
            return [("wo_b", j, f"wo_b{j // 4}") for j in js]

        attention("fox", AH, "ya", {
            1: [("a_v", 1, 0)], 2: [("a_v", 1, "a_v0")], 3: [("a_v", 3, 0)], 4: [("a_v", 3, "a_v1"), ("y_split", 0)],
            5: [("y_split", 1)], 6: [("wo_b", 0, 0), ("y_split", 2)], 7: [("y_split", 3)], 8: [("wo_b", 0, 1)], 9: wo_b(0),
            10: [("wo_b", 1, 0)], 11: [("wo_b", 1, 1)], 13: wo_b(1), 14: [("wo_b", 2, 0)], 15: [("wo_b", 2, 1)], 16: wo_b(2),
            17: [("wo_b", 3, 0)], 18: [("wo_b", 3, 1)], 19: wo_b(3), 22: [("wo_b", 4, 0)], 23: [("wo_b", 4, 1)], 24: wo_b(4),
            34: [("wo_b", 5, 0), ("wo_b", 5, 1)], 36: wo_b(5) + [("wo_b", 6, 0), ("wo_b", 6, 1)], 37: wo_b(6),
            38: [("wo_b", 7, 0), ("wo_b", 7, 1)] + wo_b(7)})

        for j in range(KD):
            tile(("wo_a", j), f"wo_a{j // 4}")
            stage("wo_a", j)
            stage("n_sq", 0, j)
            if j < KD // 2:
                stage("n_split", 0, j)
        stage("n_last", 0)
        for j in range(KD // 2, KD):
            stage("n_split", 0, j)

        def up_pair(c):
            for kind, at in (("gate", 0), ("up", DFF)):
                chunk(f"{kind}{c}", k_up[:, :, at + 256 * c:at + 256 * c + 256])
                for i in (2 * c, 2 * c + 1):
                    tile((kind, i), f"{kind}{c}")
                    stage(kind, i)
                    if (kind, i) == ("gate", 0):
                        stage("n_sum", 0)

        def down_half(half):
            k0, nk = half * FHALF[0], FHALF[half]
            for j in range(KD):
                chunk(f"down{half}{j}", k_down[:, k0:k0 + nk, P * j:P * j + P])
                tile(("down", half, j), f"down{half}{j}")
                stage("down", half, j)
                if (half, j) == (0, 2):
                    stage("rope_tables")
                if half == 1:
                    stage("n_sq", 1, j)
                    stage("n_split", 1, j)
                    if j == KD - 1:
                        stage("n_last", 1)

        for c in range(FT // 2):
            up_pair(c)
            if 2 * c == FHALF[0]:
                down_half(0)
        stage("hid_flush")
        down_half(1)
        def in2_chunk(name, *areas):
            chunk(name, *[[k_in2[:, :, at:at + n] for at, n in area] for area in areas])

        for kind, at in (("dq", OFF_DQ), ("dk", OFF_DK), ("dv", OFF_DV)):
            for c in range(2):
                in2_chunk(f"{kind}{c}", [(at + 256 * c, 256)])
            for i in range(4):
                in_tile(kind, i, f"{kind}{i // 2}")
                if (kind, i) == ("dq", 0):
                    stage("n_sum", 1)
                if (kind, i) == ("dk", 3):
                    stage("rs_col")
        for c in range(2):
            in2_chunk(f"dg{c}", [(OFF_DG + 256 * c, 256)])
        in2_chunk("cq0", [(OFF_CQ2, 256)])
        in2_chunk("cq1", [(OFF_CQ2 + 256, P)], [(OFF_KR, 64)] * 2)
        in2_chunk("ckv", [(OFF_CKV, 256)])
        chunk("uqn", *[k_uq[:, :, h, 0:128] for h in range(4)])
        chunk("uqr", [k_uq[:, :, h, 128:192] for h in range(4)])
        chunk("ukv", k_ukv)
        for c in range(2):
            in2_chunk(f"mg{c}", [(OFF_MG + 256 * c, 256)])
        dif = mla = [(qb, h) for qb in range(NB) for h in range(4)]

        lats = [("lat", i, ("cq0", "cq0", "cq1", "ckv", "ckv")[i]) for i in range(5)]
        attention("dif", 4, "yd", {
            0: [("dg", 0, "dg0")], 1: [("dg", 1, "dg0")], 2: [("dg", 2, "dg1")], 3: [("dg", 3, "dg1"), ("gate_act", "dg")],
            4: lats[0:1], 5: lats[1:2], 7: lats[2:3], 8: [("kr", 0, "cq1")], 9: [("lat_norm", 0)], 10: lats[3:4], 11: [("lat_t", 0)],
            12: lats[4:5], 13: [("lat_norm", 1)],
            18: [("lat_t", 1)] + [("qn", i, "uqn") for i in range(4)], 19: [("qr", 0, "uqr"), ("qr", 1, "uqr")],
            20: [("kn", i, "ukv") for i in range(4)], 21: [("mv", i, "ukv") for i in range(4)],
            22: [("mg", i, f"mg{i // 2}") for i in range(4)]})
        for c in range(4):
            chunk(f"gd{c}", k_in2[:, :, OFF_GD + 256 * c:OFF_GD + 256 * c + 256])
            chunk(f"gm{c}", k_in2[:, :, OFF_GM + 256 * c:OFF_GM + 256 * c + 256])
            chunk(f"pj{c}", k_pd[:, :, 256 * c:256 * c + 256], k_pm[:, :, 256 * c:256 * c + 256])
        attention("mla", 4, "ym", {2: [("gate_act", "mg"), ("gd", 0, "gd0")], 7: [("gd", 1, "gd0")], 12: [("gm", 0, "gm0")], 19: [("gm", 1, "gm0")]})
        for c in range(4):
            for kind, of in (("gd", f"gd{c}"), ("gm", f"gm{c}")):
                for i in (2 * c, 2 * c + 1):
                    if c >= 1:
                        in_tile(kind, i, of)
                    stage(kind + "_act", i)
            for kind in ("pd", "pm"):
                for i in (2 * c, 2 * c + 1):
                    in_tile(kind, i, f"pj{c}")
        stage("m_flush")
        for c in range(4):
            chunk(f"w_out2{c}", k_out2[:, :, 256 * c:256 * c + 256])
            for i in range(2):
                tile(("out", c, i), f"w_out2{c}")
                stage("out", c, i)
                if c == 3:
                    stage("final", i)

        def upto(name):
            return tile_at[name] + 1

        def bank_free(name):
            return ring_free[tile_at[name] % 2]

        def drains(name):
            return tile_at[name] // 2 + 1

        def at_ring(name):
            return ring[tile_at[name] % 2]

        def v3(ap, b):
            return ap.rearrange("p (a b) -> p a b", b=b)

        def nslot(i, j):
            return (j + KD // 2) % KD if i == 0 else j

        def x_bank(b, half):
            return (ring + bank)[2 * b + half]

        def nrm_bank(n):
            return bank[4 if n >= 1 else 1]

        def score(b):
            return (bank[1][:, 0:T], bank[2][:, 0:T - P], bank[5][:, 0:T - 2 * P], bank[2][:, T - P:T])[b]

        HG = {("u", p, b): p * NB + b for p in range(2) for b in range(NB)}

        block = ctx.enter_context(nc.Block())

        @block.sync
        def _(sp):
            x_b = x_d.rearrange("(b p) d -> p b d", p=P)
            for b in range(NB):
                sp.dma_start(xtok[:, b, :], x_b[:, b, :]).then_inc(x_in[b], 16)
                if b == 0:
                    sp.dma_start(con[:, 0:P + 1], con_d[:, 0:P + 1]).then_inc(con_in, 16)
                    sp.dma_start(gmix[:], g_mix_d.partition_broadcast(P)).then_inc(gmix_in, 16)
            for c, (name, parts, n) in enumerate(chunks):
                if name == "wo_b0":
                    sp.wait_ge(hg_done, 2)
                    sp.dma_start(xres[:], x_b).then_inc(xres_in, 16)
                if c >= 2:
                    sp.wait_ge(split_done, c - 1)
                for at, nk, w, sources in parts:
                    dst = raw[c % 2][:, at:at + nk * w].rearrange("p (k n) -> p k n", k=nk)
                    col = 0
                    for src in sources:
                        sp.dma_start(dst[:, :, col:col + src.shape[2]], src).then_inc(raw_in[c % 2], 16)
                        col += src.shape[2]
                if c == 1:
                    sp.dma_start(par[:], par_d).then_inc(par_in, 16)
                    sp.dma_start(con[:, P + 1:], con_d[:, P + 1:]).then_inc(con_rest_in, 16)
                    for i, (at, w) in enumerate(((OFF_AV, 512), (OFF_BV, 256), (OFF_CI, 256))):
                        to = (0, 512, 768)[i]
                        sp.dma_start(bias_t[:, to:to + w], b_in_d[at:at + w].partition_broadcast(P)).then_inc(bias_in, 16)
                    sp.dma_start(lamv[:].rearrange("p a b -> p (a b)"), lam_d.partition_broadcast(P)).then_inc(lam_in, 16)
                if name == "gate3":
                    sp.dma_start(posI[:], pos_d.partition_broadcast(P)).then_inc(pos_in, 16)
            sp.wait_ge(tile_done, upto(("pm", KD - 1)))
            sp.dma_start(gfin[:], g_fin_d.partition_broadcast(P)).then_inc(gfin_in, 16)
            for b in range(NB):
                sp.wait_ge(out_dve if b % 2 else out_act, b // 2 + 1)
                sp.dma_start(out_d.rearrange("(b p) d -> p b d", p=P)[:, b, :], xo[:, b, :]).then_inc(out_done, 16)
            sp.wait_ge(out_done, 16 * NB)

        @block.gpsimd
        def _(pool):
            pool.wait_ge(gmix_in, 16)
            for b in POOL_GAIN:
                pool.wait_ge(x_in[b], 16)
                pool.tensor_tensor(htok[:, b, :], xtok[:, b, :], gmix[:], ALU.mult).then_inc(x_gain, 1)
            landed = [0, 0]
            for c, (name, parts, n) in enumerate(chunks):
                landed[c % 2] += 16 * sum(len(sources) for _, _, _, sources in parts)
                pool.wait_ge(raw_in[c % 2], landed[c % 2])
                if c >= 3:
                    pool.wait_ge(tile_done, last_use[c - 3] + 1)
                pool.tensor_scalar(whi[c % 3][:, 0:n], raw[c % 2][:, 0:n], 1.0, 0.0, ALU.mult, ALU.add).then_inc(hi_done, 1)
                pool.wait_ge(hi_done, c + 1)
                pool.tensor_tensor(wlo[c % 3][:, 0:n], raw[c % 2][:, 0:n], whi[c % 3][:, 0:n].bitcast(F32),
                                   ALU.subtract).then_inc(split_done, 1)

        @block.tensor
        def _(pe):
            def weights(of, part=0):
                c = chunk_of[of]
                at, nk, n, _ = chunks[c][1][part]
                pe.wait_ge(split_done, c + 1)
                return [w[c % 3][:, at:at + nk * n].rearrange("p (k n) -> p k n", k=nk) for w in (whi, wlo)]

            def product(out, pairs, last=True, before=None, first=True):
                for n, ((ah, al), (bh, bl)) in enumerate(pairs):
                    if before is not None:
                        before(n)
                    pe.matmul(out, ah, bh, start=(first and n == 0), stop=False)
                    pe.matmul(out, ah, bl, start=False, stop=False)
                    mm = pe.matmul(out, al, bh, start=False, stop=(last and n == len(pairs) - 1))
                return mm

            def open_bank(name):
                n = tile_at[name]
                if n >= 2:
                    pe.wait_ge(ring_free[n % 2], n // 2)
                return ring[n % 2]

            def channels(name, of, col, acts, nk=KD, part=0, before=None, turn=0, begun=0, until=None):
                out = at_ring(name) if begun else open_bank(name)
                wh, wl = weights(of, part)
                ah, al = acts
                pairs = [((wh[:, k, col:col + P], wl[:, k, col:col + P]), (ah[:, (k + turn) % KD, :], al[:, (k + turn) % KD, :]))
                         for k in range(begun, until or nk)]
                mm = product(out[:], pairs, before=before, first=(begun == 0), last=until is None)
                if until is None:
                    mm.then_inc(tile_done, 1)

            def tokens(name, of, i, acts, begun=0, until=2):
                out = at_ring(name) if begun else open_bank(name)
                wh, wl = weights(of)
                ah, al = acts
                for s in range(begun, until):
                    b = 2 * i + s
                    pairs = [((ah[:, k, b * P:b * P + P], al[:, k, b * P:b * P + P]), (wh[:, k, :], wl[:, k, :])) for k in range(KD)]
                    mm = product(out[:, 256 * s:256 * s + 256], pairs)
                if until == 2:
                    mm.then_inc(tile_done, 1)

            def keep_warm(n, out):
                for _ in range(n):
                    pe.matmul(out[:], zeros[:, 0:P], zeros[:], start=True, stop=True)

            pe.wait_ge(zeros_ready, 1)
            keep_warm(15, x_bank(NB - 1, 1))
            act = (hH, hL)
            for s in order:
                kind = s[0]
                if kind == "x":
                    b, half = s[1:]
                    pe.wait_ge(con_in, 16)
                    pe.wait_ge(x_h, b + 1)
                    out = x_bank(b, half)
                    for j in range(4):
                        mm = pe.transpose(out[:, j * P:j * P + P], htok[:, b, (4 * half + j) * P:(4 * half + j + 1) * P], ident)
                    mm.then_inc(x_mm, 1)
                    if half == 1 and b < NB - 1:
                        keep_warm((6, 4, 2)[b], x_bank(NB - 1, 1))
                    elif half == 1:
                        pe.wait_ge(h_lo, 1)
                        keep_warm(10, x_bank(0, 0))
                elif kind in ("c_f", "c_q", "c_g", "b_o", "gates"):
                    def split(k):
                        if k % (KD // 2) == 0:
                            pe.wait_ge(h_lo, 2 * NB - 1 + k // (KD // 2))

                    if kind == "c_f":
                        channels(s, f"c_f{s[1]}", 0, act, before=split if s[1] == 0 else None)
                    else:
                        channels(s, kind, P * s[1], act)
                elif kind in ("b_qk", "a_q", "a_k"):
                    channels((kind, s[1]), f"{kind}{s[1] // 2}", P * (s[1] % 2), act, begun=6 if s == ("a_q", 1) else 0)
                elif kind in ("c_i", "b_v"):
                    tokens((kind, s[1]), kind, s[1], act, begun=1 if s == ("b_v", 0) else 0)
                elif kind == "a_v":
                    tokens((kind, s[1]), f"a_v{s[1] // 2}", s[1] % 2, act, begun=s[1] % 2)
                elif kind == "gate_cols":
                    pe.wait_ge(gate_rows, 2)
                    for n, src in enumerate((g1, g3)):
                        for b in range(NB):
                            mm = pe.transpose(bank[2][:, 16 * n + 4 * b:16 * n + 4 * b + 4], src[32:36, b * P:b * P + P],
                                              con[32:36, 32:36])
                    mm.then_inc(gate_cols, 1)
                elif kind == "hg_att":
                    j = s[1]
                    n = LC - 1 - j
                    pe.wait_ge(hg_a, n + 1)
                    first = 0 if n == 0 else j
                    row = CCOL["win"][0] + LC - 1 - j
                    for p in range(2):
                        mm = pe.matmul(v3(bank[p][0:64, :], LC)[:, :, first:], con[:, row:row + 64],
                                       v3(Ab[n % 2][:, p, :], LC)[:, :, first:], start=(n == 0), stop=(n == LC - 1))
                    mm.then_inc(hg_a_used, 1)
                elif kind == "hg_kdT":
                    p = s[1]
                    pe.wait_ge(hg_q, 1)
                    for b in range(NB):
                        mm = pe.transpose(bank[4 + p][:, b * P:b * P + P], kd[:, p, 8 * b:8 * b + 8, :], ident)
                    mm.then_inc(hg_kdT_mm, 1)
                elif kind == "hg_rep":
                    p, hh = s[1:]
                    n = 2 * p + hh
                    pe.wait_ge(hg_att_s, 2)
                    if n == 0:
                        pe.wait_ge(gate_cols_out, 1)
                    if n >= 2:
                        pe.wait_ge(hg_dm, n - 1)
                    pe.matmul(bank[2 + hh][:], cc("rep", slice(32 * hh, 32 * hh + LC)), attS[32 * hh:32 * hh + LC, p, :],
                              start=True, stop=True).then_inc(hg_rep_mm, 1)
                elif kind == "hg_u":
                    p, b = s[1:]
                    n = HG["u", p, b]
                    pe.wait_ge(hg_kdT_s, 2)
                    pe.wait_ge(hg_vx, n + 1)
                    if n >= 2:
                        pe.wait_ge(hg_u_s, n - 1)
                    for hh in range(2):
                        mm = pe.matmul(bank[4 + n % 2][64 * hh:64 * hh + 64, :], kdT[:, p, b, 64 * hh:64 * hh + 64],
                                       Vx[2 * (n % 2) + hh][:], start=True, stop=True)
                    mm.then_inc(hg_u_mm, 1)
                elif kind == "hg_o":
                    p, b = s[1:]
                    pe.wait_ge(hg_scan, p + 1)
                    pe.wait_ge(hg_dm, 2 * p + 2)
                    if p == 1:
                        pe.wait_ge(nrm_rs, 1)
                    for hh in range(2):
                        r = slice(64 * hh, 64 * hh + 64)
                        pe.matmul(bank[p][r, b * P:b * P + P], ci[:, b, (2 * p + hh) * HD:(2 * p + hh + 1) * HD],
                                  Dm[hh][:, b, :], start=True, stop=False)
                        for c in range(max(8 * b, 1), 8 * b + 8):
                            mm = pe.matmul(bank[p][r, c * LC:c * LC + LC], U[r, :, c - 1], cq[r, p, c, 0:LC],
                                           start=False, stop=(c == 8 * b + 7))
                    if b == NB - 1:
                        mm.then_inc(hg_o_mm, 1)
                elif kind in ("hg_y", "qk_norm"):
                    n = s[1] + (2 if kind == "qk_norm" else 0)
                    pe.wait_ge(nrm_sq, n + 1)
                    if n == 1:
                        pe.wait_ge(hg_u_s, 2 * NB)
                    if n >= 2:
                        pe.wait_ge(nrm_rs, n)
                    pe.matmul(nrm_bank(n)[:], cc("blk"), scr[n % 2][:], start=True, stop=True).then_inc(nrm_mm, 1)
                elif kind == "ml":
                    h = s[1]
                    r = slice(64 * (h % 2), 64 * (h % 2) + 64)
                    if h == 0:
                        pe.wait_ge(hg_done, 2)
                        pe.wait_ge(hg_dm, 4)
                        pe.wait_ge(hg_u_s, 2 * NB)
                        pe.wait_ge(qkB_ready, 1)
                        pe.wait_ge(gate_rows, 2)
                    if h >= 1:
                        pe.wait_ge(ml_w, 4 * h)
                    pe.matmul(bank[0][:], con[32:36, 32 + h:33 + h].broadcast_to([4, P]), g2[32:36, :],
                              start=True, stop=True).then_inc(ml_m_mm, 1)
                    for b in range(NB):
                        if h >= 1:
                            pe.wait_ge(ml_p, 4 * h)
                        pe.matmul(score(b), qkB[r, 2 + h // 2, b * P:b * P + P], qkB[r, h // 2, b * P:T],
                                  start=True, stop=True).then_inc(ml_s_mm, 1)
                elif kind == "ml_o":
                    h = s[1]
                    pe.wait_ge(ml_p, 4 * h + 4)
                    if h >= 1:
                        pe.wait_ge(ml_o_s, h)
                    for tb in range(NB):
                        for b in range(tb + 1):
                            at = (0, 512, 896, 1152)[b] + (tb - b) * P
                            mm = pe.matmul(bank[3][:, 65 * tb:65 * tb + 65], PM[h % 2][:, at:at + P], bv[:, b, h, :],
                                           start=(b == 0), stop=(b == tb))
                    mm.then_inc(ml_o_mm, 1)
                elif kind == "yb":
                    p = s[1]
                    out = open_bank(("yb", p))
                    pe.wait_ge(yb_n, 1)
                    for b in range(NB):
                        mm = pe.transpose(out[:, b * P:b * P + P], onB[:, b, 2 * p:2 * p + 2, :], ident)
                    mm.then_inc(tile_done, 1)
                elif kind == "fox_s":
                    u = s[1]
                    qb, h = fox[u]
                    n = (qb + 1) * P
                    r = slice(64 * (h % 2), 64 * (h % 2) + 64)
                    if qb == 0:
                        pe.wait_ge(qk_done, 4 + h // 2 + 1)
                    if u == 0:
                        pe.wait_ge(negC_ready, 3)
                        pe.wait_ge(mask_ready, 3)
                        pe.wait_ge(ml_p, 16)
                        pe.wait_ge(ml_o_s, 4)
                    if u >= 2:
                        pe.wait_ge(fox_e, u - 1)
                    out = bank[u % 2]
                    pe.matmul(out[:, 0:n], qT[r, h // 2, qb * P:qb * P + P], kT[r, h // 2, 0:n], start=True, stop=False)
                    pe.matmul(out[:, 0:n], selb[:, h:h + 1].broadcast_to([P, P]), negB[:, 0:n], start=False, stop=False)
                    pe.matmul(out[:, qb * P:n], identb[:], maskb[:], start=False, stop=True).then_inc(fox_s_mm, 1)
                elif kind == "fox_t":
                    u = s[1]
                    qb, h = fox[u]
                    pe.wait_ge(fox_e, u + 1)
                    if u >= 2:
                        pe.wait_ge(fox_pt, u - 1)
                    for b in range(qb + 1):
                        mm = pe.transpose(bank[2 + u % 2][:, b * P:b * P + P], Pf[u % 2][:, b * P:b * P + P], ident)
                    mm.then_inc(fox_t_mm, 1)
                elif kind == "fox_v":
                    u = s[1]
                    qb, h = fox[u]
                    pe.wait_ge(fox_pt, u + 1)
                    if u == 0:
                        pe.wait_ge(nrm_rs, 10)
                    if qb % 2 == 0 and h % 4 == 0:
                        of = ("a_v", 2 * (h // 4) + qb // 2)
                        pe.wait_ge(bank_free(of), drains(of))
                    if h == 0:
                        if qb >= 2:
                            pe.wait_ge(fox_o_free, qb - 1)
                    for b in range(qb + 1):
                        mm = pe.matmul(bank[4 + qb % 2][:, HD * h:HD * h + HD], PTs[u % 2][:, b * P:b * P + P],
                                       av[:, b, HD * h:HD * h + HD], start=(b == 0), stop=(b == qb))
                    mm.then_inc(fox_v_mm, 1)
                elif kind == "ya":
                    qb = s[1]
                    out = open_bank(("ya", qb))
                    pe.wait_ge(ya_n, qb + 1)
                    for j in range(4):
                        mm = pe.transpose(out[:, j * P:j * P + P], on[:, 2 * j:2 * j + 2, :], ident)
                    mm.then_inc(tile_done, 1)
                elif kind == "begin" and s[1] == "a_v":
                    tokens(s[1:3], f"a_v{s[2] // 2}", s[2] % 2, act, until=1)
                elif kind == "begin" and s[1] == "b_v":
                    tokens(s[1:3], "b_v", s[2], act, until=1)
                elif kind == "begin" and s[1] == "a_q":
                    channels(s[1:3], f"a_q{s[2] // 2}", P * (s[2] % 2), act, begun=2 * s[3], until=2 * s[3] + 2)
                elif kind == "begin":
                    _, name, j, part = s
                    out = at_ring((name, j)) if part else open_bank((name, j))
                    if j == 0:
                        pe.wait_ge(y_lo, 2 * part + 2)
                    wh, wl = weights(f"wo_b{j // 4}")
                    col = P * (j % 4)
                    for k in (2 * part, 2 * part + 1):
                        pe.matmul(out[:], wh[:, k, col:col + P], hH[:, 4 + k, :], start=(k == 0), stop=False)
                        pe.matmul(out[:], wh[:, k, col:col + P], hL[:, 4 + k, :], start=False, stop=False)
                        pe.matmul(out[:], wl[:, k, col:col + P], hH[:, 4 + k, :], start=False, stop=False)
                elif kind == "wo_b":
                    j = s[1]
                    if j == 0:
                        pe.wait_ge(xres_in, 16)
                    for b in range(NB):
                        mm = pe.matmul(at_ring(s)[:, b * P:b * P + P], xres[:, b, j * P:j * P + P], ident, start=False, stop=(b == NB - 1))
                    mm.then_inc(tile_done, 1)
                elif kind == "wo_a":
                    j = s[1]
                    if j == 0:
                        pe.wait_ge(y_lo, 4 + NB)
                    channels(s, f"wo_a{j // 4}", P * (j % 4), act, nk=4)
                elif kind == "n_sum":
                    i = s[1]
                    pe.wait_ge(n_acc, (KD - 1) * (i + 1))
                    if i == 0:
                        pe.wait_ge(fox_e, len(fox))
                    pe.matmul(bank[0][:], cc("ones"), sacc[:], start=True, stop=True).then_inc(n_mm, 1)
                elif kind == "rs_col":
                    pe.wait_ge(n_rs, 2)
                    for b in range(NB):
                        mm = pe.matmul(bank[5][:, b:b + 1], rsn[:, b * P:b * P + P], con[:, 0:1], start=True, stop=True)
                    mm.then_inc(col_mm, 1)
                elif kind in ("gate", "up"):
                    def first(k):
                        pe.wait_ge(n_lo, k + 1)
                    channels(s, f"{kind}{s[1] // 2}", P * (s[1] % 2), act, before=first if s == ("gate", 0) else None, turn=KD // 2)
                elif kind == "down":
                    half, j = s[1:]
                    k0, nk = half * FHALF[0], FHALF[half]
                    def first(k):
                        pe.wait_ge(hid_lo, k0 + k + 1)

                    out = open_bank(s)
                    wh, wl = weights(f"down{half}{j}")
                    product(out[:], [((wh[:, k, :], wl[:, k, :]), (hidH[:, (k0 + k) % HSLOT, :], hidL[:, (k0 + k) % HSLOT, :]))
                                     for k in range(nk)], before=first if j == 0 else None).then_inc(tile_done, 1)
                elif kind in ("dq", "dk", "dg", "mg", "gd", "gm"):
                    def first(k):
                        pe.wait_ge(n_lo, KD + k + 1)
                    channels(s, f"{kind}{s[1] // 2}", P * (s[1] % 2), act, before=first if s == ("dq", 0) else None)
                elif kind == "dv":
                    tokens(s, f"dv{s[1] // 2}", s[1] % 2, act)
                elif kind == "lat":
                    i = s[1]
                    channels(s, ("cq0", "cq0", "cq1", "ckv", "ckv")[i], (0, P, 0, 0, P)[i], act)
                elif kind == "kr":
                    channels(s, "cq1", 0, act, part=1)
                elif kind == "lat_norm":
                    which = ((0, 1, 2), (3, 4))[s[1]]
                    out = open_bank(s)
                    pe.wait_ge(lat_sq, which[-1] + 1)
                    for n in which:
                        mm = pe.matmul(out[:], cc("ones"), latS[n][:], start=(n == which[0]), stop=(n == which[-1]))
                    mm.then_inc(tile_done, 1)
                elif kind in ("qn", "qr", "kn"):
                    i = s[1]
                    if i == 0:
                        pe.wait_ge(lat_lo, 5 if kind == "kn" else 3)
                    out = open_bank(s)
                    if kind == "qn":
                        wh, wl = weights("uqn", i)
                        st = [(wh[:, k, :], wl[:, k, :]) for k in range(3)]
                    elif kind == "qr":
                        wh, wl = weights("uqr")
                        st = [(wh[:, k, P * i:P * i + P], wl[:, k, P * i:P * i + P]) for k in range(3)]
                    else:
                        wh, wl = weights("ukv")
                        st = [(wh[:, k, 256 * i:256 * i + P], wl[:, k, 256 * i:256 * i + P]) for k in range(2)]
                    first = 3 if kind == "kn" else 0
                    product(out[:], [(w, (latH[first + k][:], latL[first + k][:])) for k, w in enumerate(st)]).then_inc(tile_done, 1)
                elif kind == "mv":
                    b = s[1]
                    out = open_bank(s)
                    wh, wl = weights("ukv")
                    of = [w.rearrange("p k (h n) -> p k h n", h=4) for w in (wh, wl)]
                    t = slice(b * P, b * P + P)
                    product(v3(out[:], P), [((latH[3 + k][:, t], latL[3 + k][:, t]), (of[0][:, k, :, P:256], of[1][:, k, :, P:256]))
                                     for k in range(2)]).then_inc(tile_done, 1)
                elif kind == "dif_s":
                    u = s[1]
                    qb, h = dif[u]
                    n = (qb + 1) * P
                    if u == 0:
                        pe.wait_ge(rope_done, 8)
                        pe.wait_ge(n_rs, 2)
                    for m in range(2):
                        r = slice(64 * m, 64 * m + 64)
                        if 2 * u + m - 1 > 0:
                            pe.wait_ge(dif_e, 2 * u + m - 1)
                        pe.matmul(bank[m][:, 0:n], dq[r, h, qb * P:qb * P + P], dk[r, h, 0:n], start=True, stop=False)
                        pe.matmul(bank[m][:, qb * P:n], identb[:], maskb[:], start=False, stop=True).then_inc(dif_s_mm, 1)
                elif kind == "dif_t":
                    u = s[1]
                    qb, h = dif[u]
                    pe.wait_ge(dif_c, u + 1)
                    if u >= 2:
                        pe.wait_ge(dif_pt, u - 1)
                    for b in range(qb + 1):
                        mm = pe.transpose(bank[2 + u % 2][:, b * P:b * P + P], P2[2 * (u % 2)][:, b * P:b * P + P], ident)
                    mm.then_inc(dif_t_mm, 1)
                elif kind in ("dif_v", "mla_v"):
                    u = s[1]
                    qb, h = dif[u]
                    name = kind[:3]
                    vals = dv if name == "dif" else mv
                    pt, o_free, v_mm = (dif_pt, dif_o_free, dif_v_mm) if name == "dif" else (mla_pt, mla_o_free, mla_v_mm)
                    pe.wait_ge(pt, u + 1)
                    if h == 0:
                        if qb >= 2:
                            pe.wait_ge(o_free, qb - 1)
                    if u == 0 and name == "dif":
                        pe.wait_ge(bank_free(("dv", 3)), drains(("dv", 3)))
                    for b in range(qb + 1):
                        mm = pe.matmul(bank[4 + qb % 2][:, P * h:P * h + P], PT2[u % 2][:, b * P:b * P + P],
                                       vals[:, b, P * h:P * h + P], start=(b == 0), stop=(b == qb))
                    mm.then_inc(v_mm, 1)
                elif kind in ("yd", "ym"):
                    qb = s[1]
                    out = open_bank(s)
                    pe.wait_ge(yd_n if kind == "yd" else mla_o_free, qb + 1)
                    for h in range(4):
                        mm = pe.transpose(out[:, h * P:h * P + P], on2[:, h, :], ident)
                    mm.then_inc(tile_done, 1)
                elif kind == "mla_s":
                    u = s[1]
                    qb, h = mla[u]
                    n = (qb + 1) * P
                    r = slice(64 * (h % 2), 64 * (h % 2) + 64)
                    if u == 0:
                        for b in range(2, 4):
                            pe.wait_ge(bank_free(("mv", b)), drains(("mv", b)))
                        pe.wait_ge(rope_done, 11)
                    if u >= 2:
                        pe.wait_ge(mla_e, u - 1)
                    out = bank[u % 2]
                    pe.matmul(out[:, 0:n], qn[:, h, qb * P:qb * P + P], kn[:, h, 0:n], start=True, stop=False)
                    pe.matmul(out[:, 0:n], qr[r, h // 2, qb * P:qb * P + P], kr[r, 0:n], start=False, stop=False)
                    pe.matmul(out[:, qb * P:n], identb[:], maskb[:], start=False, stop=True).then_inc(mla_s_mm, 1)
                elif kind == "mla_t":
                    u = s[1]
                    qb, h = mla[u]
                    pe.wait_ge(mla_e, u + 1)
                    if u >= 2:
                        pe.wait_ge(mla_pt, u - 1)
                    for b in range(qb + 1):
                        mm = pe.transpose(bank[2 + u % 2][:, b * P:b * P + P], Pm[u % 2][:, b * P:b * P + P], ident)
                    mm.then_inc(mla_t_mm, 1)
                elif kind in ("pd", "pm"):
                    i = s[1]
                    if i == 0:
                        pe.wait_ge(o_lo, NB if kind == "pd" else 2 * NB)
                    at = 0 if kind == "pd" else 4
                    channels(s, f"pj{i // 2}", P * (i % 2), (oH[:, at:at + 4, :], oL[:, at:at + 4, :]), nk=4, part=0 if kind == "pd" else 1)
                elif kind == "out":
                    c, i = s[1:]
                    out = open_bank(s)
                    wh, wl = weights(f"w_out2{c}")
                    def first(k):
                        pe.wait_ge(m_lo, k + 1)

                    for e in range(2):
                        b = 2 * i + e
                        t = slice(b * P, b * P + P)
                        to = out[:, 256 * e:256 * e + 256]
                        product(to, [((mH[:, k, t], mL[:, k, t]), (wh[:, k, :], wl[:, k, :])) for k in range(KD)], last=False,
                                before=first if (c, i, e) == (0, 0, 0) else None)
                        for j in range(2):
                            mm = pe.matmul(out[:, 256 * e + P * j:256 * e + P * j + P], xT[:, 2 * c + j, t], ident, start=False, stop=(j == 1))
                    mm.then_inc(tile_done, 1)

        @block.scalar
        def _(act):
            steps = [0]

            def step():
                steps[0] += 1
                return steps[0]

            loaded = ["natural_log_exp_and_others"]
            act.preload_act_table_set(loaded[0])

            def A(out, src, func, **more):
                home = {ACT.Exp: "natural_log_exp_and_others", ACT.Ln: "natural_log_exp_and_others", ACT.Silu: "silu_and_others",
                        ACT.Sin: "silu_and_others", ACT.Sigmoid: "sigmoid_and_others"}.get(func)
                if home is not None and home != loaded[0]:
                    loaded[0] = home
                    act.preload_act_table_set(home)
                return act.activation(out, src, func, **more)

            for s in order:
                kind = s[0]
                if kind == "x_norm":
                    b = s[1]
                    act.wait_ge(x_in[b], 16)
                    A(sqx[:, b, :], xtok[:, b, :], ACT.Square, accum_out=ss_x[:, b:b + 1]).then_inc(act_step, 1)
                    act.wait_ge(act_step, step())
                    act.wait_ge(con_in, 16)
                    A(var_x[:, b:b + 1], ss_x[:, b:b + 1], ACT.Ln, bias=cc("eps"), scale=1.0 / D).then_inc(act_step, 1)
                    act.wait_ge(act_step, step())
                    A(rs_x[:, b:b + 1], var_x[:, b:b + 1], ACT.Exp, scale=-0.5).then_inc(x_rs, 1)
                elif kind == "x":
                    b, half = s[1:]
                    act.wait_ge(x_mm, 2 * b + half + 1)
                    A(hH[:, 4 * half:4 * half + 4, b * P:b * P + P], v3(x_bank(b, half)[:], P), ACT.Identity).then_inc(h_hi, 1)
                elif kind == "params":
                    act.wait_ge(par_in, 16)
                    act.wait_ge(lb_d, 1)
                    A(lbe, lbd, ACT.Exp).then_inc(lb_e, 1)
                elif kind == "c_f":
                    p = s[1]
                    act.wait_ge(nbcf_ready, 1)
                    act.wait_ge(tile_done, upto(s))
                    A(cf[:, p].rearrange("p c t -> p (c t)"), at_ring(s)[:], ACT.Sigmoid, bias=pc("b_cf", p))
                    A(ck[:, p].rearrange("p c t -> p (c t)"), at_ring(s)[:], ACT.Sigmoid, bias=nbcf[:, p:p + 1], scale=-1.0).then_inc(bank_free(s), 1)
                elif kind == "c_q":
                    p = s[1]
                    act.wait_ge(tile_done, upto(s))
                    A(cq[:, p, :, 0:LC], v3(at_ring(s)[:], LC), ACT.Silu, bias=pc("b_cq", p)).then_inc(bank_free(s), 1)
                elif kind == "c_g":
                    act.wait_ge(tile_done, upto(s))
                    A(cg[:, s[1], :], at_ring(s)[:], ACT.Silu, bias=pc("b_cg", s[1])).then_inc(bank_free(s), 1)
                elif kind == "b_o":
                    act.wait_ge(tile_done, upto(s))
                    A(bo[:, s[1], :], at_ring(s)[:], ACT.Sigmoid, bias=pc("b_bo", s[1])).then_inc(bank_free(s), 1)
                elif kind == "gates":
                    act.wait_ge(tile_done, upto(s))
                    A(gz[:], at_ring(s)[0:96, :], ACT.Identity, bias=pc("b_gate", r=slice(0, 96))).then_inc(bank_free(s), 1)
                elif kind == "gate_math":
                    act.wait_ge(bank_free(("gates", 0)), drains(("gates", 0)))
                    A(g1[:], gz[:], ACT.Abs).then_inc(act_step, 1)
                    act.wait_ge(act_step, step())
                    A(g1[:], g1[:], ACT.Exp, scale=-1.0).then_inc(act_step, 1)
                    act.wait_ge(act_step, step())
                    A(g1[:], g1[:], ACT.Ln, bias=1.0).then_inc(gate_ln, 1)
                elif kind == "gate_exp":
                    act.wait_ge(gate_m, 1)
                    A(g3[32:36, :], g3[32:36, :], ACT.Exp, scale=-1.0).then_inc(gate_rows, 1)
                elif kind in ("b_qk", "a_q", "a_k"):
                    i = s[1]
                    dst, b = {"b_qk": (bqk[:, i, 3:T + 3], "b_bqk"), "a_q": (qT[:, i, :], "b_aq"), "a_k": (kT[:, i, :], "b_ak")}[kind]
                    act.wait_ge(tile_done, upto(s))
                    A(dst, at_ring(s)[:], ACT.Identity, bias=pc(b, i)).then_inc(bank_free(s), 1)
                elif kind == "hg_att_out":
                    act.wait_ge(hg_a_used, LC)
                    act.wait_ge(hg_q, 1)
                    for p in range(2):
                        A(attS[:, p, :], bank[p][0:64, :], ACT.Identity).then_inc(hg_att_s, 1)
                elif kind == "hg_kdT":
                    p = s[1]
                    act.wait_ge(hg_kdT_mm, p + 1)
                    A(kdT[:, p].rearrange("p b d -> p (b d)"), bank[4 + p][:], ACT.Identity).then_inc(hg_kdT_s, 1)
                elif kind == "hg_u":
                    p, b = s[1:]
                    n = HG["u", p, b]
                    act.wait_ge(hg_u_mm, n + 1)
                    if p == 1:
                        act.wait_ge(hg_o_mm, 1)
                    A(U[:, :, 8 * b:8 * b + 8], bank[4 + n % 2][:].rearrange("p (c e) -> p e c", e=HD), ACT.Identity).then_inc(hg_u_s, 1)
                elif kind in ("hg_sq", "qk_sq"):
                    i = s[1]
                    n = i + (2 if kind == "qk_sq" else 0)
                    if n >= 2:
                        act.wait_ge(nrm_done, n - 1)
                    if kind == "hg_sq":
                        act.wait_ge(hg_o_mm, i + 1)
                        src = bank[i][:]
                    else:
                        src = (qT if i < 4 else kT)[:, i % 4, :]
                        of = ("a_q" if i < 4 else "a_k", i % 4)
                        act.wait_ge(bank_free(of), drains(of))
                    A(scr[n % 2][:], src, ACT.Square).then_inc(nrm_sq, 1)
                elif kind in ("hg_y", "qk_norm"):
                    n = s[1] + (2 if kind == "qk_norm" else 0)
                    act.wait_ge(nrm_mm, n + 1)
                    A(scr[n % 2][:], nrm_bank(n)[:], ACT.Ln, bias=cc("eps"), scale=1.0 / HD).then_inc(act_step, 1)
                    act.wait_ge(act_step, step())
                    A(scr[n % 2][:], scr[n % 2][:], ACT.Exp, scale=-0.5).then_inc(nrm_rs, 1)
                elif kind == "conv_act":
                    act.wait_ge(conv_b, 4)
                    A(qkB[:], qkB[:], ACT.Silu).then_inc(qkB_ready, 1)
                elif kind == "ml":
                    h = s[1]
                    act.wait_ge(ml_w, 4 * h + 4)
                    A(PM[h % 2][:], PM[h % 2][:], ACT.Exp).then_inc(ml_e, 1)
                elif kind == "yb_norm":
                    act.wait_ge(yb_var, 1)
                    A(msB, msB, ACT.Ln).then_inc(act_step, 1)
                    act.wait_ge(act_step, step())
                    A(rsB, msB, ACT.Exp, scale=-0.5).then_inc(yb_rs, 1)
                elif kind == "fox_s":
                    u = s[1]
                    qb, h = fox[u]
                    n = (qb + 1) * P
                    act.wait_ge(fox_m, u + 1)
                    if u >= 2:
                        act.wait_ge(fox_t_mm, u - 1)
                    A(Pf[u % 2][:, 0:n], bank[u % 2][:, 0:n], ACT.Exp, bias=nmx[:, u % 4:u % 4 + 1],
                      accum_out=rsum[:, 8 * (qb % 2) + h:8 * (qb % 2) + h + 1]).then_inc(fox_e, 1)
                elif kind == "ya_n":
                    qb = s[1]
                    act.wait_ge(fox_o_free, qb + 1)
                    A(sqA[:], on[:], ACT.Square).then_inc(ya_sq, 1)
                elif kind == "ya_v":
                    qb = s[1]
                    act.wait_ge(ya_var, qb + 1)
                    A(msA, msA, ACT.Ln).then_inc(act_step, 1)
                    act.wait_ge(act_step, step())
                    A(rsA, msA, ACT.Exp, scale=-0.5).then_inc(ya_rs, 1)
                elif kind == "ya":
                    qb = s[1]
                    act.wait_ge(bank_free(s), drains(s))
                    A(hH[:, 0:4, qb * P:qb * P + P], yt[:], ACT.Identity).then_inc(ya_hi, 1)
                elif kind == "y_split":
                    i = s[1]
                    src = (bo if i < 2 else cg)[:, i % 2, :]
                    if i == 0:
                        act.wait_ge(bank_free(("yb", 0)), drains(("yb", 0)))
                        act.wait_ge(bank_free(("yb", 1)), drains(("yb", 1)))
                        act.wait_ge(hg_done, 2)
                        act.wait_ge(tile_done, upto(("a_v", 3)))
                    A(hH[:, 4 + i, :], src, ACT.Identity).then_inc(ys_hi, 1)
                elif kind == "wo_b":
                    j = s[1]
                    act.wait_ge(tile_done, upto(s))
                    A(xT[:, j, :], at_ring(s)[:], ACT.Identity).then_inc(bank_free(s), 1)
                elif kind == "n_sq":
                    i, j = s[1:]
                    src = ("wo_a", j) if i == 0 else ("down", 1, j)
                    act.wait_ge(bank_free(src), drains(src))
                    before = (KD - 1) * i + max(j - 2, 0)
                    if before >= 1:
                        act.wait_ge(n_acc, before)
                    A(sacc[:] if j == 0 else sqn[j % 2][:], xT[:, j, :], ACT.Square).then_inc(n_sq, 1)
                elif kind == "n_split":
                    i, j = s[1:]
                    if i == 0 and j == KD // 2:
                        act.wait_ge(tile_done, upto(("wo_a", KD - 1)))
                    A(hH[:, nslot(i, j), :], xT[:, j, :], ACT.Identity, scale=pc(("g_ffn", "g_in2")[i], j)).then_inc(n_hi, 1)
                elif kind == "n_sum":
                    i = s[1]
                    act.wait_ge(n_mm, i + 1)
                    A(rsn[:], bank[0][:], ACT.Ln, bias=cc("eps"), scale=1.0 / D).then_inc(act_step, 1)
                    act.wait_ge(act_step, step())
                    A(rsn[:], rsn[:], ACT.Exp, scale=-0.5).then_inc(n_rs, 1)
                elif kind == "up":
                    i = s[1]
                    act.wait_ge(conv_g, i + 1)
                    A(cvg[i % 2][:], cvg[i % 2][:], ACT.Silu).then_inc(silu_ready, 1)
                    if i >= 1:
                        act.wait_ge(hidden, i)
                        A(hidH[:, (i - 1) % HSLOT, :], hid[(i - 1) % 2][:], ACT.Identity).then_inc(hid_hi, 1)
                elif kind == "hid_flush":
                    act.wait_ge(hidden, FT)
                    A(hidH[:, (FT - 1) % HSLOT, :], hid[(FT - 1) % 2][:], ACT.Identity).then_inc(hid_hi, 1)
                elif kind == "rope_tables":
                    act.wait_ge(rot_ready, 1)
                    A(sinT[:], rotT[:], ACT.Sin).then_inc(sin_ready, 1)
                    act.wait_ge(rot_ready, 2)
                    A(cosT[:], angT[:], ACT.Sin).then_inc(cos_ready, 1)
                    act.wait_ge(lam_s, 2)
                    A(lame, lams, ACT.Exp).then_inc(lam_e, 1)
                elif kind in ("dq", "dk", "qr", "kr"):
                    n = {"dq": 0, "dk": 4, "kr": 8, "qr": 9}[kind] + s[1]
                    act.wait_ge(tile_done, upto(s))
                    if n >= 2:
                        act.wait_ge(rope_done, n - 1)
                    z, o = zs[n % 2], at_ring(s)
                    for g in range(4):
                        f = g ^ 1
                        ins = A(z[32 * g:32 * g + 32, :], o[32 * f:32 * f + 32, :], ACT.Identity)
                    ins.then_inc(rope_z, 1)
                elif kind == "gate_act":
                    for i in range(4):
                        act.wait_ge(bank_free((s[1], i)), drains((s[1], i)))
                    gate = (sdg if s[1] == "dg" else smg)[:]
                    A(gate, gate, ACT.Silu).then_inc(gate_on, 1)
                elif kind == "dif_s":
                    u = s[1]
                    qb, h = dif[u]
                    n = (qb + 1) * P
                    if u == 0:
                        act.wait_ge(lam_done, 1)
                        act.wait_ge(cos_ready, 1)
                    for m in range(2):
                        act.wait_ge(dif_m, 2 * u + m + 1)
                        if m == 0:
                            if u >= 2:
                                act.wait_ge(dif_t_mm, u - 1)
                            if u >= 2:
                                act.wait_ge(dif_c, u - 1)
                        A(P2[2 * (u % 2) + m][:, 0:n], bank[m][:, 0:n], ACT.Exp, bias=nmx[:, 2 * (u % 2) + m:2 * (u % 2) + m + 1],
                          accum_out=rsum2[:, 8 * (qb % 2) + 4 * m + h:8 * (qb % 2) + 4 * m + h + 1]).then_inc(dif_e, 1)
                elif kind == "dif_t":
                    u = s[1]
                    n = (dif[u][0] + 1) * P
                    act.wait_ge(dif_t_mm, u + 1)
                    if u >= 2:
                        act.wait_ge(dif_v_mm, u - 1)
                    A(PT2[u % 2][:, 0:n], bank[2 + u % 2][:, 0:n], ACT.Identity).then_inc(dif_pt, 1)
                elif kind == "yd_n":
                    qb = s[1]
                    act.wait_ge(dif_o_free, qb + 1)
                    for h in range(4):
                        A(sq2[:, h, :], on2[:, h, :], ACT.Square, accum_out=ms2[:, h:h + 1]).then_inc(yd_sq, 1)
                    act.wait_ge(yd_sq, 4 * qb + 4)
                    A(ms2, ms2, ACT.Ln, bias=cc("eps"), scale=1.0 / P).then_inc(act_step, 1)
                    act.wait_ge(act_step, step())
                    A(rs2, ms2, ACT.Exp, scale=-0.5).then_inc(yd_rs, 1)
                elif kind == "yd":
                    qb = s[1]
                    act.wait_ge(bank_free(s), drains(s))
                    A(oH[:, 0:4, qb * P:qb * P + P], yt2[:], ACT.Identity).then_inc(o_hi, 1)
                elif kind == "ym":
                    qb = s[1]
                    act.wait_ge(bank_free(s), drains(s))
                    if qb == 0:
                        act.wait_ge(tile_done, upto(("mv", 3)))
                    A(oH[:, 4:8, qb * P:qb * P + P], yt2[:], ACT.Identity).then_inc(o_hi, 1)
                elif kind == "lat":
                    i = s[1]
                    act.wait_ge(bank_free(s), drains(s))
                    A(latS[i][:], lat[i][:], ACT.Square).then_inc(lat_sq, 1)
                elif kind == "lat_norm":
                    i = s[1]
                    act.wait_ge(tile_done, upto(s))
                    if i == 0:
                        act.wait_ge(rope_done, 9)
                    else:
                        act.wait_ge(lat_t, 3)
                    A(rsl[:], at_ring(s)[:], ACT.Ln, bias=cc("eps"), scale=1.0 / (384, 256)[i]).then_inc(bank_free(s), 1)
                    act.wait_ge(bank_free(s), drains(s))
                    A(rsl[:], rsl[:], ACT.Exp, scale=-0.5).then_inc(lat_rs, 1)
                elif kind == "lat_t":
                    i = s[1]
                    for n in ((0, 1, 2), (3, 4))[i]:
                        act.wait_ge(lat_t, n + 1)
                        A(latH[n][:], lat[n][:], ACT.Identity).then_inc(lat_hi, 1)
                elif kind in ("qn", "kn"):
                    act.wait_ge(tile_done, upto(s))
                    A((qn if kind == "qn" else kn)[:, s[1], :], at_ring(s)[:], ACT.Identity,
                      scale=MLA_SCALE if kind == "qn" else 1.0).then_inc(bank_free(s), 1)
                elif kind == "mv":
                    act.wait_ge(tile_done, upto(s))
                    A(mv[:, s[1], :], at_ring(s)[:], ACT.Identity).then_inc(bank_free(s), 1)
                elif kind == "mla_s":
                    u = s[1]
                    qb, h = mla[u]
                    n = (qb + 1) * P
                    act.wait_ge(mla_m, u + 1)
                    if u >= 2:
                        act.wait_ge(mla_t_mm, u - 1)
                    A(Pm[u % 2][:, 0:n], bank[u % 2][:, 0:n], ACT.Exp, bias=nmx[:, u % 4:u % 4 + 1],
                      accum_out=rsum2[:, 4 * (qb % 2) + h:4 * (qb % 2) + h + 1]).then_inc(mla_e, 1)
                elif kind in ("gd_act", "gm_act"):
                    i = s[1]
                    of = (kind[:2], i)
                    act.wait_ge(bank_free(of), drains(of))
                    gate = (sgd if kind == "gd_act" else sgm)[i % 2][:]
                    A(gate, gate, ACT.Sigmoid).then_inc(gd_on if kind == "gd_act" else gm_on, 1)
                elif kind == "pm":
                    i = s[1]
                    if i >= 1:
                        if i >= 1:
                            act.wait_ge(merged, i)
                        A(mH[:, i - 1, :], mt2[(i - 1) % 2][:], ACT.Identity).then_inc(m_hi, 1)
                elif kind == "m_flush":
                    act.wait_ge(merged, KD)
                    A(mH[:, KD - 1, :], mt2[(KD - 1) % 2][:], ACT.Identity).then_inc(m_hi, 1)
                    loaded[0] = "natural_log_exp_and_others"
                    act.preload_act_table_set(loaded[0])
                elif kind == "out":
                    c, i = s[1:]
                    act.wait_ge(tile_done, upto(s))
                    A(xo[:, 2 * i:2 * i + 2, 256 * c:256 * c + 256], v3(at_ring(s)[:], 256), ACT.Identity).then_inc(bank_free(s), 1)
                    act.wait_ge(bank_free(s), drains(s))
                    for e in range(2):
                        b = 2 * i + e
                        A(sqn[e][:, 0:256], xo[:, b, 256 * c:256 * c + 256], ACT.Square,
                          accum_out=ssf[:, 4 * b + c:4 * b + c + 1]).then_inc(ssf_ready, 1)
                    act.wait_ge(ssf_ready, 4 * c + 2 * i + 2)
                elif kind == "final":
                    i = s[1]
                    act.wait_ge(f_var, i + 1)
                    mine = slice(2 * i, 2 * i + 2)
                    A(sst[:, mine], sst[:, mine], ACT.Ln).then_inc(act_step, 1)
                    act.wait_ge(act_step, step())
                    A(rsf[:, mine], sst[:, mine], ACT.Exp, scale=-0.5).then_inc(f_rs, 1)
                    act.wait_ge(f_rs, i + 1)
                    act.wait_ge(xo_g, 7 + i)
                    b = 2 * i
                    A(xo[:, b, :], xo[:, b, :], ACT.Identity, scale=rsf[:, b:b + 1]).then_inc(out_act, 1)

        @block.vector
        def _(dve):
            steps = [0]

            def step():
                steps[0] += 1
                return steps[0]

            TT, TS, STT, CP = dve.tensor_tensor, dve.tensor_scalar, dve.scalar_tensor_tensor, dve.tensor_copy

            def wide(ap, n):
                return ap.unsqueeze(2).broadcast_to([ap.shape[0], ap.shape[1], n])

            def low(hi, full, dst):
                return TT(dst, full, hi.bitcast(F32), ALU.subtract)

            dve.memset(zeros[:], 0.0).then_inc(zeros_ready, 1)
            for s in order:
                kind = s[0]
                if kind == "x_norm":
                    b = s[1]
                    dve.wait_ge(x_rs, b + 1)
                    if b in POOL_GAIN:
                        dve.wait_ge(x_gain, POOL_GAIN.index(b) + 1)
                        TS(htok[:, b, :], htok[:, b, :], rs_x[:, b:b + 1], None, ALU.mult).then_inc(x_h, 1)
                    else:
                        dve.wait_ge(gmix_in, 16)
                        STT(htok[:, b, :], xtok[:, b, :], rs_x[:, b:b + 1], gmix[:], ALU.mult, ALU.mult).then_inc(x_h, 1)
                elif kind == "x":
                    b, half = s[1:]
                    k = slice(4 * half, 4 * half + 4)
                    dve.wait_ge(h_hi, 2 * b + half + 1)
                    low(hH[:, k, b * P:b * P + P], v3(x_bank(b, half)[:], P), hL[:, k, b * P:b * P + P]).then_inc(h_lo, 1)
                elif kind == "params":
                    dve.wait_ge(par_in, 16)
                    dve.wait_ge(con_rest_in, 16)
                    TT(lbd, pc("lb", 0, 2), pc("lb", 0, 2), ALU.subtract).then_inc(lb_d, 1)
                    TS(nbcf, pc("b_cf", 0, 2), -1.0, None, ALU.mult).then_inc(nbcf_ready, 1)
                    TS(gq8, pc("g_aq"), HD ** -0.5, None, ALU.mult).then_inc(dve_step, 1)
                    dve.wait_ge(dve_step, step())
                    TS(gsub, pc("g_sub"), 1.0 - LAMBDA_INIT, None, ALU.mult).then_inc(dve_step, 1)
                    dve.wait_ge(dve_step, step())
                    CP(identb[:], cc("ident")).then_inc(mask_ready, 1)
                    CP(maskb[:], cc("neg")).then_inc(mask_ready, 1)
                    CP(selb[:], cc("sel")).then_inc(mask_ready, 1)
                    dve.wait_ge(lb_e, 1)
                    dve.reciprocal(lbr, lbe).then_inc(dve_step, 1)
                    dve.wait_ge(dve_step, step())
                    TT(lbp, lbe, lbr, ALU.mult).then_inc(dve_step, 1)
                    dve.wait_ge(dve_step, step())
                    TT(lb, lbp, lbp, ALU.subtract).then_inc(dve_step, 1)
                    dve.wait_ge(dve_step, step())
                    TS(lb, lb, 0.0, None, ALU.max).then_inc(dve_step, 1)
                    dve.wait_ge(dve_step, step())
                    TS(lb1, lb, -1.0, 1.0, ALU.mult, ALU.add).then_inc(dve_step, 1)
                    dve.wait_ge(dve_step, step())
                elif kind == "hg_begin":
                    for p in range(2):
                        dve.wait_ge(bank_free(("c_f", p)), drains(("c_f", p)))
                        dve.wait_ge(bank_free(("c_q", p)), drains(("c_q", p)))
                        TS(cf[:, p], cf[:, p], lb1[:, p:p + 1], lb[:, p:p + 1], ALU.mult, ALU.add).then_inc(dve_step, 1)
                        dve.wait_ge(dve_step, step())
                        TS(ck[:, p], ck[:, p], lb1[:, p:p + 1], None, ALU.mult).then_inc(dve_step, 1)
                        dve.wait_ge(dve_step, step())
                    dve.memset(cq[:, :, :, LC:LC + 1], 1.0).then_inc(dve_step, 1)
                    dve.wait_ge(dve_step, step())
                elif kind == "c_i":
                    i = s[1]
                    if i == 0:
                        dve.wait_ge(bias_in, 48)
                    dve.wait_ge(tile_done, upto(s))
                    TT(ci[:, 2 * i:2 * i + 2, :], v3(at_ring(s)[:], 256),
                            bias_t[:, 768:1024].unsqueeze(1).broadcast_to([P, 2, 256]), ALU.add).then_inc(bank_free(s), 1)
                elif kind == "b_v":
                    i = s[1]
                    if i == 0:
                        dve.wait_ge(x_mm, 2 * NB)
                        dve.memset(bv[:, :, :, HD:HD + 1], 1.0).then_inc(dve_step, 1)
                        dve.wait_ge(dve_step, step())
                    dve.wait_ge(tile_done, upto(s))
                    for e in range(2):
                        ins = TT(bv[:, 2 * i + e, :, 0:HD], v3(at_ring(s)[:, 256 * e:256 * e + 256], HD), v3(bias_t[:, 512:768], HD), ALU.add)
                    ins.then_inc(bank_free(s), 1)
                elif kind == "a_v":
                    i = s[1]
                    half, e = i // 2, i % 2
                    dve.wait_ge(tile_done, upto(s))
                    TT(av[:, 2 * e:2 * e + 2, 256 * half:256 * half + 256], v3(at_ring(s)[:], 256),
                            bias_t[:, 256 * half:256 * half + 256].unsqueeze(1).broadcast_to([P, 2, 256]), ALU.add).then_inc(bank_free(s), 1)
                elif kind == "gate_math":
                    dve.wait_ge(gate_ln, 1)
                    STT(g2[:], gz[:], 0.0, g1[:], ALU.min, ALU.subtract).then_inc(dve_step, 1)
                    dve.wait_ge(dve_step, step())
                    dve.memset(g1[:], 1.0).then_inc(dve_step, 1)
                    dve.wait_ge(dve_step, step())
                    dve.tensor_tensor_scan(g3[:], g1[:], g2[:], 0.0, ALU.mult, ALU.add).then_inc(dve_step, 1)
                    dve.wait_ge(dve_step, step())
                    CP(g3[32:36, :], g3[64:68, :]).then_inc(dve_step, 1)
                    dve.wait_ge(dve_step, step())
                    TT(gz[32:36, :], gz[32:36, :], g3[32:36, :], ALU.subtract).then_inc(dve_step, 1)
                    dve.wait_ge(dve_step, step())
                    dve.tensor_tensor_scan(g2[32:36, :], g1[32:36, :], gz[32:36, :], -3e38, ALU.mult, ALU.max).then_inc(dve_step, 1)
                    dve.wait_ge(dve_step, step())
                    CP(g1[32:36, :], gz[32:36, :]).then_inc(dve_step, 1)
                    dve.wait_ge(dve_step, step())
                    TT(g3[32:36, :], g3[32:36, :], g2[32:36, :], ALU.add).then_inc(gate_m, 1)
                    dve.wait_ge(gate_m, 1)
                    TS(g2[32:36, :], g2[32:36, :], -1.0, None, ALU.mult).then_inc(gate_rows, 1)
                elif kind == "decay":
                    dve.memset(negB[:], 0.0).then_inc(dve_step, 1)
                    dve.wait_ge(dve_step, step())
                    TS(negC[:], g3[0:8, :], -1.0, None, ALU.mult).then_inc(dve_step, 1)
                    dve.wait_ge(dve_step, step())
                    for part in range(3):
                        CP(negT[:], negC[:]).then_inc(dve_step, 1)
                        dve.wait_ge(dve_step, step())
                        CP(negB[32 * part:32 * part + 8, :], negT[:]).then_inc(negC_ready, 1)
                        dve.wait_ge(negC_ready, part + 1)
                        if part < 2:
                            TT(negC[:], negC[:], negT[:], ALU.subtract).then_inc(dve_step, 1)
                            dve.wait_ge(dve_step, step())
                elif kind == "gate_cols":
                    dve.wait_ge(gate_cols, 1)
                    CP(colB, bank[2][:, 0:32]).then_inc(gate_cols_out, 1)
                elif kind == "hg_att":
                    j = s[1]
                    n = LC - 1 - j
                    if n >= 2:
                        dve.wait_ge(hg_a_used, n - 1)
                    q64 = cq[:].rearrange("p h c t -> p (h c) t")
                    f64 = cf[:].rearrange("p h c t -> p (h c) t")
                    k64 = ck[:].rearrange("p h c t -> p (h c) t")
                    d64 = kd[:].rearrange("p h c t -> p (h c) t")
                    t0 = 0 if n == 0 else j
                    TT(Ab[n % 2][:].rearrange("p h (c t) -> p (h c) t", t=LC)[:, :, t0:], q64[:, :, t0:LC],
                       k64[:, :, j:j + 1].broadcast_to([P, 64, LC - t0]), ALU.mult).then_inc(hg_a, 1)
                    TT(d64[:, :, j:j + 1], q64[:, :, LC:LC + 1], k64[:, :, j:j + 1], ALU.mult).then_inc(dve_step, 1)
                    dve.wait_ge(dve_step, step())
                    dve.wait_ge(hg_a, n + 1)
                    m = LC + 1 - j
                    ins = TT(q64[:, :, j:LC + 1], q64[:, :, j:LC + 1], f64[:, :, j:j + 1].broadcast_to([P, 64, m]), ALU.mult)
                    if j == 0:
                        ins.then_inc(hg_q, 1)
                        dve.wait_ge(hg_q, 1)
                        for p in range(2):
                            dve.memset(cq[:, p, 0, LC:LC + 1], 0.0).then_inc(dve_step, 1)
                            dve.wait_ge(dve_step, step())
                    else:
                        ins.then_inc(dve_step, 1)
                        dve.wait_ge(dve_step, step())
                elif kind == "hg_rep":
                    p, hh = s[1:]
                    n = 2 * p + hh
                    dve.wait_ge(hg_rep_mm, n + 1)
                    if p >= 1:
                        dve.wait_ge(hg_o_mm, p)
                    TT(Dm[hh][:], v3(bank[2 + hh][:], P), cc("chunk").unsqueeze(1).broadcast_to([P, NB, P]), ALU.mult).then_inc(hg_dm, 1)
                elif kind == "hg_vx":
                    p, b = s[1:]
                    n = HG["u", p, b]
                    if n >= 2:
                        dve.wait_ge(hg_u_mm, n - 1)
                    of = ("c_i", b // 2)
                    dve.wait_ge(bank_free(of), drains(of))
                    if n == 0:
                        dve.wait_ge(hg_a_used, LC)
                    for hh in range(2):
                        c = (2 * p + hh) * HD
                        ins = TT(Vx[2 * (n % 2) + hh][:], ci[:, b, c:c + HD].unsqueeze(1).broadcast_to([P, 8, HD]),
                                 wide(cc("inchunk"), HD), ALU.mult)
                    ins.then_inc(hg_vx, 1)
                elif kind == "hg_scan":
                    p = s[1]
                    CP(Gx[:], cq[:, p, :, LC:LC + 1].rearrange("p c o -> p o c").broadcast_to([P, HD // 2, NC])).then_inc(dve_step, 1)
                    dve.wait_ge(dve_step, step())
                    dve.wait_ge(hg_u_s, NB * (p + 1))
                    g = Gx[:].rearrange("p e c -> p (e c)")
                    for e in range(2):
                        u = U[:, 32 * e:32 * e + 32, :].rearrange("p e c -> p (e c)")
                        ins = dve.tensor_tensor_scan(u, g, u, 0.0, ALU.mult, ALU.add)
                        if e == 0:
                            ins.then_inc(dve_step, 1)
                            dve.wait_ge(dve_step, step())
                    ins.then_inc(hg_scan, 1)
                    dve.wait_ge(hg_scan, p + 1)
                elif kind == "hg_y":
                    p = s[1]
                    dve.wait_ge(nrm_rs, p + 1)
                    TT(scr[p][:], bank[p][:], scr[p][:], ALU.mult).then_inc(hg_n, 1)
                    dve.wait_ge(hg_n, p + 1)
                    STT(cg[:, p, :], scr[p][:], pc("g_out", 6 + p), cg[:, p, :], ALU.mult, ALU.mult).then_inc(nrm_done, 1)
                    dve.wait_ge(nrm_done, p + 1)
                    dve.engine_nop().then_inc(hg_done, 1)
                elif kind == "conv":
                    t = s[1]
                    if t == 0:
                        dve.memset(bqk[:, :, 0:3], 0.0).then_inc(dve_step, 1)
                        dve.wait_ge(dve_step, step())
                    dve.wait_ge(bank_free(("b_qk", t)), drains(("b_qk", t)))
                    TS(qkB[:, t, :], bqk[:, t, 0:T], pc("w_bconv", t), None, ALU.mult).then_inc(dve_step, 1)
                    dve.wait_ge(dve_step, step())
                    for k in range(1, 4):
                        ins = STT(qkB[:, t, :], bqk[:, t, k:k + T], pc("w_bconv", 4 * k + t), qkB[:, t, :], ALU.mult, ALU.add)
                        if k < 3:
                            ins.then_inc(dve_step, 1)
                            dve.wait_ge(dve_step, step())
                    ins.then_inc(conv_b, 1)
                elif kind == "ml":
                    h = s[1]
                    segs = (0, 512, 896, 1152)
                    dve.wait_ge(ml_m_mm, h + 1)
                    if h >= 2:
                        dve.wait_ge(ml_o_mm, h - 1)
                    for b in range(NB):
                        w = T - P * b
                        TS(PM[h % 2][:, segs[b]:segs[b] + w], bank[0][:, b * P:T], colB[:, 4 * b + h:4 * b + h + 1], 0.0,
                           ALU.add, ALU.min).then_inc(ml_w, 1)
                    dve.wait_ge(ml_e, h + 1)
                    for b in range(NB):
                        TT(PM[h % 2][:, segs[b]:segs[b] + P], PM[h % 2][:, segs[b]:segs[b] + P], cc("tri"), ALU.mult).then_inc(dve_step, 1)
                        dve.wait_ge(dve_step, step())
                    for b in range(NB):
                        w = T - P * b
                        dve.wait_ge(ml_s_mm, 4 * h + 4)
                        seg = PM[h % 2][:, segs[b]:segs[b] + w]
                        STT(seg, score(b), HD ** -0.5, seg, ALU.mult, ALU.mult).then_inc(ml_p, 1)
                elif kind == "ml_o":
                    h = s[1]
                    dve.wait_ge(ml_o_mm, h + 1)
                    CP(Oh[:].rearrange("p b e -> p (b e)"), bank[3][:, 0:260]).then_inc(ml_o_s, 1)
                    dve.wait_ge(ml_o_s, h + 1)
                    den = Oh[:, :, HD:HD + 1].rearrange("p b o -> p (b o)")
                    STT(denB, den, -1.0, den, ALU.mult, ALU.max).then_inc(dve_step, 1)
                    dve.wait_ge(dve_step, step())
                    em = colB[:, 16:32].rearrange("p (b h) -> p b h", h=4)[:, :, h:h + 1].rearrange("p b o -> p (b o)")
                    TT(denB, denB, em, ALU.max).then_inc(dve_step, 1)
                    dve.wait_ge(dve_step, step())
                    dve.reciprocal(recB, denB).then_inc(dve_step, 1)
                    dve.wait_ge(dve_step, step())
                    TT(onB[:, :, h, :], Oh[:, :, 0:HD], wide(recB, HD), ALU.mult).then_inc(dve_step, 1)
                    dve.wait_ge(dve_step, step())
                elif kind == "qk_norm":
                    i = s[1]
                    dve.wait_ge(nrm_rs, i + 3)
                    dst = (qT if i < 4 else kT)[:, i % 4, :]
                    STT(dst, dst, gq8 if i < 4 else pc("g_ak"), scr[i % 2][:], ALU.mult, ALU.mult).then_inc(nrm_done, 1)
                    dve.wait_ge(nrm_done, i + 3)
                    dve.engine_nop().then_inc(qk_done, 1)
                elif kind == "yb_norm":
                    o16 = onB[:].rearrange("p b h e -> p (b h) e")
                    q16 = sqB[:].rearrange("p b h e -> p (b h) e")
                    TT(q16, o16, o16, ALU.mult).then_inc(dve_step, 1)
                    dve.wait_ge(dve_step, step())
                    dve.tensor_reduce(msB, q16, AX.X, ALU.add).then_inc(dve_step, 1)
                    dve.wait_ge(dve_step, step())
                    TS(msB, msB, 1.0 / HD, EPS, ALU.mult, ALU.add).then_inc(yb_var, 1)
                    dve.wait_ge(yb_rs, 1)
                    TT(o16, o16, wide(rsB, HD), ALU.mult).then_inc(yb_n, 1)
                elif kind == "yb":
                    p = s[1]
                    dve.wait_ge(tile_done, upto(s))
                    STT(bo[:, p, :], at_ring(s)[:], pc("g_out", 4 + p), bo[:, p, :], ALU.mult, ALU.mult).then_inc(bank_free(s), 1)
                elif kind == "fox_s":
                    u = s[1]
                    qb, h = fox[u]
                    n = (qb + 1) * P
                    dve.wait_ge(fox_s_mm, u + 1)
                    dve.tensor_reduce(nmx[:, u % 4:u % 4 + 1], bank[u % 2][:, 0:n], AX.X, ALU.max, negate=True).then_inc(fox_m, 1)
                elif kind == "fox_t":
                    u = s[1]
                    qb, h = fox[u]
                    n = (qb + 1) * P
                    dve.wait_ge(fox_t_mm, u + 1)
                    if u >= 2:
                        dve.wait_ge(fox_v_mm, u - 1)
                    CP(PTs[u % 2][:, 0:n], bank[2 + u % 2][:, 0:n]).then_inc(fox_pt, 1)
                elif kind == "ya_n":
                    qb = s[1]
                    dve.wait_ge(fox_v_mm, AH * (qb + 1))
                    dve.reciprocal(recA, rsum[:, 8 * (qb % 2):8 * (qb % 2) + 8]).then_inc(dve_step, 1)
                    dve.wait_ge(dve_step, step())
                    if qb >= 1:
                        dve.wait_ge(tile_done, upto(("ya", qb - 1)))
                    TT(on[:], v3(bank[4 + qb % 2][:], HD), wide(recA, HD), ALU.mult).then_inc(fox_o_free, 1)
                elif kind == "ya_v":
                    dve.wait_ge(ya_sq, s[1] + 1)
                    dve.tensor_reduce(msA, sqA[:], AX.X, ALU.add).then_inc(dve_step, 1)
                    dve.wait_ge(dve_step, step())
                    TS(msA, msA, 1.0 / HD, EPS, ALU.mult, ALU.add).then_inc(ya_var, 1)
                elif kind == "ya_s":
                    dve.wait_ge(ya_rs, s[1] + 1)
                    TT(on[:], on[:], wide(rsA, HD), ALU.mult).then_inc(ya_n, 1)
                elif kind == "ya":
                    qb = s[1]
                    dve.wait_ge(tile_done, upto(s))
                    if qb >= 1:
                        dve.wait_ge(ya_hi, qb)
                    TT(yt[:], v3(at_ring(s)[:], P), wide(pc("g_out", 0, 4), P), ALU.mult).then_inc(bank_free(s), 1)
                elif kind == "ya_l":
                    qb = s[1]
                    dve.wait_ge(ya_hi, qb + 1)
                    t = slice(qb * P, qb * P + P)
                    low(hH[:, 0:4, t], yt[:], hL[:, 0:4, t]).then_inc(y_lo, 1)
                    dve.wait_ge(y_lo, 4 + qb + 1)
                elif kind == "y_split":
                    i = s[1]
                    dve.wait_ge(ys_hi, i + 1)
                    low(hH[:, 4 + i, :], (bo if i < 2 else cg)[:, i % 2, :], hL[:, 4 + i, :]).then_inc(y_lo, 1)
                elif kind == "wo_a":
                    j = s[1]
                    dve.wait_ge(tile_done, upto(s))
                    dve.wait_ge(bank_free(("wo_b", j)), drains(("wo_b", j)))
                    TT(xT[:, j, :], xT[:, j, :], at_ring(s)[:], ALU.add).then_inc(bank_free(s), 1)
                elif kind in ("n_sq", "n_last"):
                    i = s[1]
                    for j in range(KD - 1, KD) if kind == "n_last" else range(max(s[2] - 1, 1), s[2]):
                        dve.wait_ge(n_sq, KD * i + j + 1)
                        if j >= 2:
                            dve.wait_ge(n_acc, (KD - 1) * i + j - 1)
                        TT(sacc[:], sacc[:], sqn[j % 2][:], ALU.add).then_inc(n_acc, 1)
                elif kind == "n_split":
                    i, j = s[1:]
                    src = ("wo_a", j) if i == 0 else ("down", 1, j)
                    dve.wait_ge(bank_free(src), drains(src))
                    dve.wait_ge(n_hi, KD * i + j + 1)
                    at = nslot(i, j)
                    STT(hL[:, at, :], xT[:, j, :], pc(("g_ffn", "g_in2")[i], j), hH[:, at, :].bitcast(F32),
                        ALU.mult, ALU.subtract).then_inc(n_lo, 1)
                elif kind in ("gate", "up"):
                    i = s[1]
                    g = 0 if kind == "gate" else FT
                    z = zp[(0 if kind == "gate" else 2) + i % 2]
                    dst = (cvg if kind == "gate" else cvu)[i % 2]
                    if s == ("gate", 0):
                        for pad in zp:
                            pad_zero = dve.memset(pad[:, 0:2], 0.0)
                        pad_zero.then_inc(zp_zero, 1)
                        dve.wait_ge(zp_zero, 1)
                        dve.wait_ge(n_rs, 1)
                    dve.wait_ge(tile_done, upto(s))
                    if i >= 2:
                        dve.wait_ge(conv_g if kind == "gate" else conv_u, i - 1)
                        dve.wait_ge(hidden, i - 1)
                    TT(z[:, 2:T + 2], at_ring(s)[:], rsn[:], ALU.mult).then_inc(bank_free(s), 1)
                    dve.wait_ge(bank_free(s), drains(s))
                    TS(dst[:], z[:, 0:T], pc("w_fconv", g + i), pc("b_fconv", g + i), ALU.mult, ALU.add).then_inc(dve_step, 1)
                    dve.wait_ge(dve_step, step())
                    STT(dst[:], z[:, 1:T + 1], pc("w_fconv", 44 + g + i), dst[:], ALU.mult, ALU.add).then_inc(dve_step, 1)
                    dve.wait_ge(dve_step, step())
                    STT(dst[:], z[:, 2:T + 2], pc("w_fconv", 88 + g + i), dst[:], ALU.mult, ALU.add).then_inc(
                        conv_g if kind == "gate" else conv_u, 1)
                    if kind == "up":
                        dve.wait_ge(conv_u, i + 1)
                        dve.wait_ge(silu_ready, i + 1)
                        if i >= 2:
                            dve.wait_ge(hid_lo, i - 1)
                        TT(hid[i % 2][:], cvg[i % 2][:], cvu[i % 2][:], ALU.mult).then_inc(hidden, 1)
                        if i >= 1:
                            dve.wait_ge(hid_hi, i)
                            low(hidH[:, (i - 1) % HSLOT, :], hid[(i - 1) % 2][:], hidL[:, (i - 1) % HSLOT, :]).then_inc(hid_lo, 1)
                elif kind == "hid_flush":
                    dve.wait_ge(hid_hi, FT)
                    low(hidH[:, (FT - 1) % HSLOT, :], hid[(FT - 1) % 2][:], hidL[:, (FT - 1) % HSLOT, :]).then_inc(hid_lo, 1)
                elif kind == "down":
                    half, j = s[1:]
                    dve.wait_ge(tile_done, upto(s))
                    if half == 1:
                        dve.wait_ge(bank_free(("down", 0, j)), drains(("down", 0, j)))
                    TT(xT[:, j, :], xT[:, j, :], at_ring(s)[:], ALU.add).then_inc(bank_free(s), 1)
                elif kind == "rope_tables":
                    dve.wait_ge(pos_in, 16)
                    CP(angT[:], posI[:]).then_inc(dve_step, 1)
                    dve.wait_ge(dve_step, step())
                    TS(angT[:], angT[:], cc("freq"), None, ALU.mult).then_inc(dve_step, 1)
                    dve.wait_ge(dve_step, step())
                    two_pi = 2 * np.pi
                    parts = [6.28125, float(np.float32(two_pi - 6.28125)), 0.0]
                    parts[2] = float(two_pi - parts[0] - parts[1])
                    magic = 1.5 * 2.0 ** 23
                    for which in range(2):
                        turn = cosT if which == 0 else sqn[0]
                        if which == 0:
                            TS(cosT[:], angT[:], 1.0 / two_pi, magic, ALU.mult, ALU.add).then_inc(dve_step, 1)
                            dve.wait_ge(dve_step, step())
                        else:
                            TS(sqn[0][:], angT[:], 1.0 / two_pi, 0.25, ALU.mult, ALU.add).then_inc(dve_step, 1)
                            dve.wait_ge(dve_step, step())
                            TS(sqn[0][:], sqn[0][:], magic, None, ALU.add).then_inc(dve_step, 1)
                            dve.wait_ge(dve_step, step())
                        TS(turn[:], turn[:], -magic, None, ALU.add).then_inc(dve_step, 1)
                        dve.wait_ge(dve_step, step())
                        dst = rotT if which == 0 else angT
                        src = angT
                        for part in parts:
                            STT(dst[:], turn[:], -part, src[:], ALU.mult, ALU.add).then_inc(dve_step, 1)
                            dve.wait_ge(dve_step, step())
                            src = dst
                        if which == 1:
                            TS(dst[:], dst[:], cc("halfpi"), None, ALU.add).then_inc(dve_step, 1)
                            dve.wait_ge(dve_step, step())
                        TS(dst[:], dst[:], 3.1415925, -3.1415925, ALU.min, ALU.max).then_inc(rot_ready, 1)
                        dve.wait_ge(rot_ready, which + 1)
                    dve.wait_ge(sin_ready, 1)
                    TS(sinT[:], sinT[:], cc("sign"), None, ALU.mult).then_inc(dve_step, 1)
                    dve.wait_ge(dve_step, step())
                    dve.wait_ge(lam_in, 16)
                    lv = lamv[:].rearrange("p (a b) d -> p a b d", b=2)
                    for m in range(2):
                        TT(lamm[:, m, :], lv[:, m, 0, :], lv[:, m, 1, :], ALU.mult).then_inc(dve_step, 1)
                        dve.wait_ge(dve_step, step())
                        dve.tensor_reduce(lams[:, m:m + 1], lamm[:, m, :], AX.X, ALU.add).then_inc(lam_s, 1)
                    dve.wait_ge(lam_e, 1)
                    TT(nlam, lame[:, 1:2], lame[:, 0:1], ALU.subtract).then_inc(dve_step, 1)
                    dve.wait_ge(dve_step, step())
                    TS(nlam, nlam, -LAMBDA_INIT, None, ALU.add).then_inc(lam_done, 1)
                    dve.wait_ge(lam_done, 1)
                    dve.wait_ge(cos_ready, 1)
                elif kind in ("dq", "dk", "qr", "kr"):
                    n = {"dq": 0, "dk": 4, "kr": 8, "qr": 9}[kind] + s[1]
                    sc = {"dq": HD ** -0.5, "dk": 1.0, "qr": MLA_SCALE, "kr": 1.0}[kind]
                    dst = kr[:] if kind == "kr" else {"dq": dq, "dk": dk, "qr": qr}[kind][:, s[1], :]
                    if n == 0:
                        dve.wait_ge(n_rs, 2)
                        TT(cosR[:], cosT[:], rsn[:], ALU.mult).then_inc(dve_step, 1)
                        dve.wait_ge(dve_step, step())
                        TT(sinR[:], sinT[:], rsn[:], ALU.mult).then_inc(dve_step, 1)
                        dve.wait_ge(dve_step, step())
                    c, sn = (cosT, sinT) if kind == "qr" else (cosR, sinR)
                    dve.wait_ge(rope_z, n + 1)
                    STT(dst, at_ring(s)[:], sc, c[:], ALU.mult, ALU.mult).then_inc(bank_free(s), 1)
                    STT(zs[n % 2][:], zs[n % 2][:], sc, sn[:], ALU.mult, ALU.mult).then_inc(dve_step, 1)
                    dve.wait_ge(dve_step, step())
                    dve.wait_ge(bank_free(s), drains(s))
                    TT(dst, dst, zs[n % 2][:], ALU.add).then_inc(rope_done, 1)
                elif kind == "rs_col":
                    dve.wait_ge(col_mm, 1)
                    CP(rs_col, bank[5][:, 0:NB]).then_inc(dve_step, 1)
                    dve.wait_ge(dve_step, step())
                elif kind == "dv":
                    i = s[1]
                    half, e = i // 2, i % 2
                    dve.wait_ge(tile_done, upto(s))
                    for b in (2 * e, 2 * e + 1):
                        at = 256 * (b % 2)
                        ins = TS(dv[:, b, 256 * half:256 * half + 256], at_ring(s)[:, at:at + 256], rs_col[:, b:b + 1], None, ALU.mult)
                    ins.then_inc(bank_free(s), 1)
                elif kind in ("dg", "mg", "lat"):
                    i = s[1]
                    dst = lat[i][:] if kind == "lat" else (sdg if kind == "dg" else smg)[:, i, :]
                    dve.wait_ge(tile_done, upto(s))
                    TT(dst, at_ring(s)[:], rsn[:], ALU.mult).then_inc(bank_free(s), 1)
                elif kind in ("gd", "gm"):
                    i = s[1]
                    dve.wait_ge(tile_done, upto(s))
                    if i >= 2:
                        dve.wait_ge(gated_d if kind == "gd" else gated_m, i - 1)
                    TT((sgd if kind == "gd" else sgm)[i % 2][:], at_ring(s)[:], rsn[:], ALU.mult).then_inc(bank_free(s), 1)
                elif kind == "dif_s":
                    u = s[1]
                    qb, h = dif[u]
                    n = (qb + 1) * P
                    for m in range(2):
                        dve.wait_ge(dif_s_mm, 2 * u + m + 1)
                        dve.tensor_reduce(nmx[:, 2 * (u % 2) + m:2 * (u % 2) + m + 1], bank[m][:, 0:n], AX.X, ALU.max,
                                          negate=True).then_inc(dif_m, 1)
                elif kind == "dif_c":
                    u = s[1]
                    qb, h = dif[u]
                    n = (qb + 1) * P
                    dve.wait_ge(dif_e, 2 * u + 2)
                    r0, r1 = (rsum2[:, 8 * (qb % 2) + 4 * m + h:8 * (qb % 2) + 4 * m + h + 1] for m in range(2))
                    w, rc = wgt2[:, u % 2:u % 2 + 1], rec2[:, u % 2:u % 2 + 1]
                    dve.reciprocal(rc, r1).then_inc(dve_step, 1)
                    dve.wait_ge(dve_step, step())
                    TS(w, r0, rc, nlam, ALU.mult, ALU.mult).then_inc(dve_step, 1)
                    dve.wait_ge(dve_step, step())
                    a, b = P2[2 * (u % 2)], P2[2 * (u % 2) + 1]
                    STT(a[:, 0:n], b[:, 0:n], w, a[:, 0:n], ALU.mult, ALU.add).then_inc(dif_c, 1)
                elif kind == "mla_s":
                    u = s[1]
                    qb, h = mla[u]
                    n = (qb + 1) * P
                    dve.wait_ge(mla_s_mm, u + 1)
                    dve.tensor_reduce(nmx[:, u % 4:u % 4 + 1], bank[u % 2][:, 0:n], AX.X, ALU.max, negate=True).then_inc(mla_m, 1)
                elif kind == "mla_t":
                    u = s[1]
                    qb, h = mla[u]
                    n = (qb + 1) * P
                    dve.wait_ge(mla_t_mm, u + 1)
                    if u >= 2:
                        dve.wait_ge(mla_v_mm, u - 1)
                    CP(PT2[u % 2][:, 0:n], bank[2 + u % 2][:, 0:n]).then_inc(mla_pt, 1)
                elif kind in ("yd_n", "ym_n"):
                    qb = s[1]
                    own = kind == "yd_n"
                    o_free, v_mm = (dif_o_free, dif_v_mm) if own else (mla_o_free, mla_v_mm)
                    dve.wait_ge(v_mm, 4 * (qb + 1))
                    at = (8 if own else 4) * (qb % 2)
                    dve.reciprocal(rec4, rsum2[:, at:at + 4]).then_inc(dve_step, 1)
                    dve.wait_ge(dve_step, step())
                    if qb >= 1 or not own:
                        dve.wait_ge(tile_done, upto(("yd" if own else "ym", qb - 1) if qb >= 1 else ("yd", NB - 1)))
                    TT(on2[:], v3(bank[4 + qb % 2][:], P), wide(rec4, P), ALU.mult).then_inc(o_free, 1)
                elif kind == "yd_s":
                    dve.wait_ge(yd_rs, s[1] + 1)
                    TT(on2[:], on2[:], wide(rs2, P), ALU.mult).then_inc(yd_n, 1)
                elif kind in ("yd", "ym"):
                    qb = s[1]
                    dve.wait_ge(tile_done, upto(s))
                    t = slice(qb * P, qb * P + P)
                    gate = sdg if kind == "yd" else smg
                    dve.wait_ge(gate_on, 1 if kind == "yd" else 2)
                    if kind == "yd":
                        STT(yt2[:], v3(at_ring(s)[:], P), gsub, gate[:, :, t], ALU.mult, ALU.mult).then_inc(bank_free(s), 1)
                    else:
                        TT(yt2[:], v3(at_ring(s)[:], P), gate[:, :, t], ALU.mult).then_inc(bank_free(s), 1)
                elif kind in ("yd_l", "ym_l"):
                    qb = s[1]
                    n = qb + (0 if kind == "yd_l" else NB)
                    t = slice(qb * P, qb * P + P)
                    first = 0 if kind == "yd_l" else 4
                    dve.wait_ge(o_hi, n + 1)
                    low(oH[:, first:first + 4, t], yt2[:], oL[:, first:first + 4, t]).then_inc(o_lo, 1)
                    dve.wait_ge(o_lo, n + 1)
                elif kind == "lat_t":
                    i = s[1]
                    dve.wait_ge(lat_rs, i + 1)
                    for n in ((0, 1, 2), (3, 4))[i]:
                        g = pc("g_cq2", n) if i == 0 else pc("g_ckv", n - 3)
                        STT(lat[n][:], lat[n][:], g, rsl[:], ALU.mult, ALU.mult).then_inc(lat_t, 1)
                    for n in ((0, 1, 2), (3, 4))[i]:
                        dve.wait_ge(lat_hi, n + 1)
                        low(latH[n][:], lat[n][:], latL[n][:]).then_inc(lat_lo, 1)
                elif kind in ("pd", "pm"):
                    i = s[1]
                    dve.wait_ge(tile_done, upto(s))
                    dve.wait_ge(gd_on if kind == "pd" else gm_on, i + 1)
                    dst = (mt if kind == "pd" else mt2)[i % 2]
                    src = (sgd if kind == "pd" else sgm)[i % 2]
                    if kind == "pm":
                        if i >= 2:
                            dve.wait_ge(m_lo, i - 1)
                    elif i >= 2:
                        if i >= 2:
                            dve.wait_ge(merged, i - 1)
                    TT(dst[:], at_ring(s)[:], src[:], ALU.mult).then_inc((gated_d if kind == "pd" else gated_m), 1)
                    dve.wait_ge((gated_d if kind == "pd" else gated_m), i + 1)
                    if kind == "pd":
                        dve.engine_nop().then_inc(bank_free(s), 1)
                    else:
                        TT(mt2[i % 2][:], mt[i % 2][:], mt2[i % 2][:], ALU.add).then_inc(bank_free(s), 1)
                        dve.wait_ge(bank_free(s), drains(s))
                        dve.engine_nop().then_inc(merged, 1)
                        if i >= 1:
                            if i >= 1:
                                dve.wait_ge(m_hi, i)
                            low(mH[:, i - 1, :], mt2[(i - 1) % 2][:], mL[:, i - 1, :]).then_inc(m_lo, 1)
                elif kind == "m_flush":
                    dve.wait_ge(m_hi, KD)
                    low(mH[:, KD - 1, :], mt2[(KD - 1) % 2][:], mL[:, KD - 1, :]).then_inc(m_lo, 1)
                elif kind == "out":
                    c, i = s[1:]
                    dve.wait_ge(gfin_in, 16)
                    dve.wait_ge(ssf_ready, 4 * c + 2 * i + 2)
                    at = slice(256 * c, 256 * c + 256)
                    TT(xo[:, 2 * i:2 * i + 2, at], xo[:, 2 * i:2 * i + 2, at], gfin[:, at].unsqueeze(1).broadcast_to([P, 2, 256]),
                       ALU.mult).then_inc(xo_g, 1)
                elif kind == "final":
                    i = s[1]
                    mine = slice(2 * i, 2 * i + 2)
                    dve.tensor_reduce(sst[:, mine], v3(ssf, 4)[:, mine, :], AX.X, ALU.add).then_inc(dve_step, 1)
                    dve.wait_ge(dve_step, step())
                    TS(sst[:, mine], sst[:, mine], 1.0 / D, EPS, ALU.mult, ALU.add).then_inc(f_var, 1)
                    dve.wait_ge(f_rs, i + 1)
                    dve.wait_ge(xo_g, 7 + i)
                    b = 2 * i + 1
                    TS(xo[:, b, :], xo[:, b, :], rsf[:, b:b + 1], None, ALU.mult).then_inc(out_dve, 1)


def kernel(**inputs):
    import numpy as _np
    import concourse.bacc as _bacc
    from concourse import mybir as _mybir
    from concourse.bass_utils import run_bass_kernel_spmd as _run

    a = {k: _np.asarray(v) for k, v in inputs.items()}
    w_in, b_in = a["w_in"][0], a["b_in"][0]

    par = _np.zeros((P, NPC), _np.float32)

    def cols(name, v):
        at, n = PCOL[name]
        par[:, at:at + n] = v.reshape(n, P).T

    cols("g_ffn", a["norm_ffn_g"][0])
    cols("g_in2", a["norm_in_2"][0])
    cols("g_out", a["out_g"][0])
    for name, at, n in (("b_aq", OFF_AQ, 512), ("b_ak", OFF_AK, 512), ("b_bqk", OFF_BQK, 512), ("b_bo", OFF_BO, 256),
                        ("b_cq", OFF_CQ, 256), ("b_cf", OFF_CF, 256), ("b_cg", OFF_CG, 256)):
        cols(name, b_in[at:at + n])
    cols("g_cq2", a["mla_q_norm_2"][0])
    cols("g_ckv", a["mla_kv_norm_2"][0])
    cols("lb", a["lb_logits"][0])
    cols("w_bconv", a["b_conv_w"][0].reshape(-1))
    cols("g_sub", a["diff_subln_2"][0])
    cols("g_aq", _np.concatenate([a["a_q_g"][0]] * 2))
    cols("g_ak", _np.concatenate([a["a_k_g"][0]] * 2))
    cols("w_fconv", a["ffn_conv_w"][0].reshape(-1))
    cols("b_fconv", a["ffn_conv_b"][0])
    w_gate = _np.zeros((P, KD, P), _np.float32)
    for row, at, n in ((0, OFF_AF, AH), (32, OFF_BI, BH), (64, OFF_BF, BH)):
        w_gate[:, :, row:row + n] = w_in[:, at:at + n].reshape(KD, P, n).transpose(1, 0, 2)
        par[row:row + n, PCOL["b_gate"][0]] = b_in[at:at + n]
    lam = _np.concatenate([a[f"diff_lambda_{v}_2"][0] for v in ("q1", "k1", "q2", "k2")])

    send = [("x", a["x"][0]), ("w_in", w_in), ("b_in", b_in), ("w_gate", w_gate), ("w_out", a["w_out"][0]),
            ("w_up", a["w_up"][0]), ("w_down", a["w_down"][0]), ("pos", a["positions_2"][0]), ("w_in2", a["w_in_2"][0]),
            ("lam", lam), ("w_uq", a["w_uq_2"][0]), ("w_ukv", a["w_ukv_2"][0]), ("w_pd", a["w_proj_diff_2"][0]),
            ("w_pm", a["w_proj_mla_2"][0]), ("w_out2", a["w_out_2"][0]), ("g_mix", a["norm_mix_g"][0]), ("g_fin", a["norm_final_2"]), ("par", par),
            ("con", constant_table())]
    nc = _bacc.Bacc("TRN2", target_bir_lowering=False, num_devices=1, dynamic_dma_scratch_size=1024)
    arrays, args = {}, []
    for name, v in send:
        v = _np.ascontiguousarray(v)
        arrays[f"in_{name}"] = v
        args.append(nc.dram_tensor(f"in_{name}", v.shape, _mybir.dt.from_np(v.dtype), kind="ExternalInput").ap())
    args.append(nc.dram_tensor("out_0", (T, D), F32, kind="ExternalOutput").ap())
    two_blocks(nc, *args)
    r = _run(nc, [arrays], core_ids=[0])
    return r.results[0]["out_0"].reshape(1, T, D)
```
